# Optimizing a Trainium2 kernel written in Bass

```python
import math
import jax, jax.numpy as jnp
from jax import lax
import numpy as np

"""Hybrid decoder block (Hymba-style parallel head groups).

Per layer:
  h = RMSNorm(x); [u | q | k | v] = h @ W_in   (one combined input projection)
  head group A (S5): u -> 32 channel groups of 16, each driving a 64-dim complex diagonal
      state (ZOH, per-group step), associative scan over positions, y = Re(C s) + D u, GELU + GLU
  head group B (stick-breaking attention, 8 heads x 64, QK-norm, no positional encoding)
  x = x + concat(RMSNorm(y_A), RMSNorm(y_B)) @ W_out
  x = x + CrossAttn(RMSNorm(x), RMSNorm(mem))   (4 heads, QK-norm, softmax over 256 memory tokens)
  x = x + W_down relu(W_up RMSNorm(x))^2
Inputs: x (BATCH, SEQ, D_MODEL), mem (BATCH, 256, D_MODEL), per-layer parameters with a leading DEPTH axis.
Output: (BATCH, SEQ, D_MODEL).
"""

D_MODEL = 1024
BATCH = 1
SEQ = 2048
DEPTH = 1

SSM_WIDTH = D_MODEL // 2
SSM_GROUP = 16
SSM_GROUPS = SSM_WIDTH // SSM_GROUP
SSM_STATE = 64
SB_HEAD_DIM = 64
SB_WIDTH = D_MODEL // 2
SB_HEADS = SB_WIDTH // SB_HEAD_DIM
MIX_WIDTH = SSM_WIDTH + SB_WIDTH
IN_WIDTH = SSM_WIDTH + 3 * SB_WIDTH
Q_BLOCK = 128
MEM_LEN = 256
XA_HEADS = 4
XA_HEAD_DIM = 128
XA_WIDTH = XA_HEADS * XA_HEAD_DIM
D_FF = 4 * D_MODEL
NORM_EPS = 1e-6
DT_MIN = 1e-3
DT_MAX = 1e-1

kernel_name = "hymba_s5_stickbreaking_block"

def rmsnorm(x, g):
    xf = x.astype(jnp.float32)
    xf = xf * lax.rsqrt(jnp.mean(xf * xf, axis=-1, keepdims=True) + NORM_EPS)
    return (xf * g.astype(jnp.float32)).astype(x.dtype)

def _linear_recurrence_combine(left, right):
    a_l, b_l = left
    a_r, b_r = right
    return a_r * a_l, a_r * b_l + b_r

def s5_mixer(u, a_re, a_im, log_dt, b_re, b_im, c_re, c_im, d_skip, w_glu):
    bsz, seq, _ = u.shape
    f32 = jnp.float32
    uf = u.astype(f32).reshape(bsz, seq, SSM_GROUPS, SSM_GROUP)
    lam = lax.complex(a_re.astype(f32), a_im.astype(f32))
    dt = jnp.exp(log_dt.astype(f32))[:, None]
    a_bar = jnp.exp(lam * dt)
    b = lax.complex(b_re.astype(f32), b_im.astype(f32))
    b_bar = ((a_bar - 1.0) / lam)[..., None] * b
    c = lax.complex(c_re.astype(f32), c_im.astype(f32))
    bu = jnp.einsum('bsgc,gpc->bsgp', uf.astype(jnp.complex64), b_bar)
    a_seq = jnp.broadcast_to(a_bar[None, None], (1, seq, SSM_GROUPS, SSM_STATE))
    _, states = lax.associative_scan(_linear_recurrence_combine, (a_seq, bu), axis=1)
    y = jnp.einsum('bsgp,gcp->bsgc', states, c).real + d_skip.astype(f32).reshape(SSM_GROUPS, SSM_GROUP) * uf
    y = jax.nn.gelu(y.reshape(bsz, seq, SSM_WIDTH))
    y = y * jax.nn.sigmoid(y @ w_glu.astype(f32))
    return y.astype(u.dtype)

def stick_breaking_attention(q, k, v):
    bsz, seq, h, dh = q.shape
    nblk = seq // Q_BLOCK
    scale = dh ** -0.5
    qb = q.reshape(bsz, nblk, Q_BLOCK, h, dh).transpose(1, 0, 2, 3, 4)
    key_pos = jnp.arange(seq)

    def block(args):
        qi, i = args
        logits = jnp.einsum('bqhd,bkhd->bhqk', qi, k, preferred_element_type=jnp.float32) * scale
        q_pos = i * Q_BLOCK + jnp.arange(Q_BLOCK)
        mask = key_pos[None, :] < q_pos[:, None]
        log_beta = jax.nn.log_sigmoid(logits)
        log_1m_beta = jnp.where(mask, jax.nn.log_sigmoid(-logits), 0.0)
        after = lax.cumsum(log_1m_beta, axis=3, reverse=True) - log_1m_beta
        w = jnp.where(mask, jnp.exp(log_beta + after), 0.0)
        return jnp.einsum('bhqk,bkhd->bqhd', w.astype(v.dtype), v)

    out = lax.map(block, (qb, jnp.arange(nblk)))
    return out.transpose(1, 0, 2, 3, 4).reshape(bsz, seq, h, dh)

def memory_cross_attention(h, mem_n, w_q, w_kv, g_q, g_k, w_o):
    bsz, seq, _ = h.shape
    mlen = mem_n.shape[1]
    q = (h @ w_q).reshape(bsz, seq, XA_HEADS, XA_HEAD_DIM)
    kv = mem_n @ w_kv
    k = kv[..., :XA_WIDTH].reshape(bsz, mlen, XA_HEADS, XA_HEAD_DIM)
    v = kv[..., XA_WIDTH:].reshape(bsz, mlen, XA_HEADS, XA_HEAD_DIM)
    q = rmsnorm(q, g_q)
    k = rmsnorm(k, g_k)
    scores = jnp.einsum('bqhd,bkhd->bhqk', q, k, preferred_element_type=jnp.float32) * (XA_HEAD_DIM ** -0.5)
    p = jax.nn.softmax(scores, axis=-1).astype(v.dtype)
    o = jnp.einsum('bhqk,bkhd->bqhd', p, v).reshape(bsz, seq, XA_WIDTH)
    return o @ w_o

def setup_inputs(seed: int = 0) -> dict:
    key = jax.random.key(seed)
    ks = jax.random.split(key, 32)

    def nrm(k, shape, scale):
        return jax.random.normal(k, shape, jnp.float32) * scale

    def gain(k, shape):
        return 1.0 + 0.01 * jax.random.normal(k, shape, jnp.float32)

    L = DEPTH
    n = jnp.arange(SSM_STATE, dtype=jnp.float32)
    return {
        "x": nrm(ks[0], (BATCH, SEQ, D_MODEL), 1.0),
        "mem": nrm(ks[1], (BATCH, MEM_LEN, D_MODEL), 1.0),
        "g_mix": gain(ks[2], (L, D_MODEL)),
        "w_in": nrm(ks[3], (L, D_MODEL, IN_WIDTH), D_MODEL ** -0.5),
        "ssm_a_re": -0.5 + 0.01 * jax.random.normal(ks[4], (L, SSM_GROUPS, SSM_STATE), jnp.float32),
        "ssm_a_im": jnp.pi * n + 0.01 * jax.random.normal(ks[5], (L, SSM_GROUPS, SSM_STATE), jnp.float32),
        "ssm_log_dt": jax.random.uniform(ks[6], (L, SSM_GROUPS), jnp.float32, math.log(DT_MIN), math.log(DT_MAX)),
        "ssm_b_re": nrm(ks[7], (L, SSM_GROUPS, SSM_STATE, SSM_GROUP), (2 * SSM_GROUP) ** -0.5),
        "ssm_b_im": nrm(ks[8], (L, SSM_GROUPS, SSM_STATE, SSM_GROUP), (2 * SSM_GROUP) ** -0.5),
        "ssm_c_re": nrm(ks[9], (L, SSM_GROUPS, SSM_GROUP, SSM_STATE), 0.5),
        "ssm_c_im": nrm(ks[10], (L, SSM_GROUPS, SSM_GROUP, SSM_STATE), 0.5),
        "ssm_d": nrm(ks[11], (L, SSM_WIDTH), 1.0),
        "ssm_w_glu": nrm(ks[12], (L, SSM_WIDTH, SSM_WIDTH), SSM_WIDTH ** -0.5),
        "sb_g_q": gain(ks[13], (L, SB_HEAD_DIM)),
        "sb_g_k": gain(ks[14], (L, SB_HEAD_DIM)),
        "g_out_ssm": gain(ks[15], (L, SSM_WIDTH)),
        "g_out_sb": gain(ks[16], (L, SB_WIDTH)),
        "w_out": nrm(ks[17], (L, MIX_WIDTH, D_MODEL), MIX_WIDTH ** -0.5),
        "g_xa": gain(ks[18], (L, D_MODEL)),
        "g_mem": gain(ks[19], (L, D_MODEL)),
        "xa_w_q": nrm(ks[20], (L, D_MODEL, XA_WIDTH), D_MODEL ** -0.5),
        "xa_w_kv": nrm(ks[21], (L, D_MODEL, 2 * XA_WIDTH), D_MODEL ** -0.5),
        "xa_g_q": gain(ks[22], (L, XA_HEAD_DIM)),
        "xa_g_k": gain(ks[23], (L, XA_HEAD_DIM)),
        "xa_w_o": nrm(ks[24], (L, XA_WIDTH, D_MODEL), XA_WIDTH ** -0.5),
        "g_mlp": gain(ks[25], (L, D_MODEL)),
        "w_up": nrm(ks[26], (L, D_MODEL, D_FF), D_MODEL ** -0.5),
        "w_down": nrm(ks[27], (L, D_FF, D_MODEL), D_FF ** -0.5),
    }

def reference(x, mem, g_mix, w_in, ssm_a_re, ssm_a_im, ssm_log_dt, ssm_b_re, ssm_b_im,
              ssm_c_re, ssm_c_im, ssm_d, ssm_w_glu, sb_g_q, sb_g_k, g_out_ssm, g_out_sb,
              w_out, g_xa, g_mem, xa_w_q, xa_w_kv, xa_g_q, xa_g_k, xa_w_o, g_mlp, w_up, w_down):
    bsz, seq, _ = x.shape
    for l in range(DEPTH):
        h = rmsnorm(x, g_mix[l])
        proj = h @ w_in[l]
        u = proj[..., :SSM_WIDTH]
        q = proj[..., SSM_WIDTH:SSM_WIDTH + SB_WIDTH].reshape(bsz, seq, SB_HEADS, SB_HEAD_DIM)
        k = proj[..., SSM_WIDTH + SB_WIDTH:SSM_WIDTH + 2 * SB_WIDTH].reshape(bsz, seq, SB_HEADS, SB_HEAD_DIM)
        v = proj[..., SSM_WIDTH + 2 * SB_WIDTH:].reshape(bsz, seq, SB_HEADS, SB_HEAD_DIM)
        y_ssm = s5_mixer(u, ssm_a_re[l], ssm_a_im[l], ssm_log_dt[l], ssm_b_re[l], ssm_b_im[l],
                         ssm_c_re[l], ssm_c_im[l], ssm_d[l], ssm_w_glu[l])
        q = rmsnorm(q, sb_g_q[l])
        k = rmsnorm(k, sb_g_k[l])
        y_sb = stick_breaking_attention(q, k, v).reshape(bsz, seq, SB_WIDTH)
        y = jnp.concatenate([rmsnorm(y_ssm, g_out_ssm[l]), rmsnorm(y_sb, g_out_sb[l])], axis=-1)
        x = x + y @ w_out[l]
        h = rmsnorm(x, g_xa[l])
        mem_n = rmsnorm(mem, g_mem[l])
        x = x + memory_cross_attention(h, mem_n, xa_w_q[l], xa_w_kv[l], xa_g_q[l], xa_g_k[l], xa_w_o[l])
        h = rmsnorm(x, g_mlp[l])
        x = x + jnp.square(jax.nn.relu(h @ w_up[l])) @ w_down[l]
    return x


_drawn_inputs = setup_inputs


def setup_inputs(seed=0):
    import zlib

    import numpy as np

    out = dict(_drawn_inputs(seed))
    spreads = {}
    factors = {'g_mix': 6.438,
     'ssm_a_re': 8.0,
     'sb_g_q': 8.0,
     'sb_g_k': 8.0,
     'g_out_ssm': 8.0,
     'g_out_sb': 8.0,
     'g_xa': 8.0,
     'g_mem': 8.0,
     'xa_g_q': 8.0,
     'xa_g_k': 8.0,
     'g_mlp': 7.411}
    for name, (base, spread) in spreads.items():
        noise = np.random.default_rng([zlib.crc32(name.encode()), seed]).standard_normal(out[name].shape)
        drawn = base * np.exp(spread * noise) if base else spread * noise
        out[name] = __import__('jax').numpy.asarray(drawn.astype(out[name].dtype))
    for name, factor in factors.items():
        out[name] = (out[name] * factor).astype(out[name].dtype)
    return out
```

```python
import math
from contextlib import ExitStack, contextmanager

from concourse import mybir
F32 = mybir.dt.float32
F32R = mybir.dt.float32r
BF16 = mybir.dt.bfloat16
I32 = mybir.dt.int32
ALU = mybir.AluOpType
ACT = mybir.ActivationFunctionType
AX_X = mybir.AxisListType.X

P = 128
BANK = 512
D_MODEL = 1024
SEQ = 2048
SSM_WIDTH = 512
SSM_GROUP = 16
SSM_GROUPS = 32
SSM_STATE = 64
HEADS = 8
HEAD = 64
SB_WIDTH = HEADS * HEAD
MEM = 256
XA_HEADS = 4
XA_HEAD = 128
XA_WIDTH = XA_HEADS * XA_HEAD
D_FF = 4096
EPS = 1e-6
KC = D_MODEL // P
SUB = P // SSM_GROUP
CHUNKS = SEQ // SUB
DMA = 16


class Tally:

    def __init__(self, sem, per, lead=2):
        self.sem, self.per, self.lead = sem, per, lead

    def start(self, eng):
        eng.sem_inc(self.sem, self.per * self.lead)

    def at(self, step, k):
        return step * self.per + (self.lead * self.per + k)


@contextmanager
def semaphores(nc, prefix):
    used = []

    def sem(name):
        used.append(nc.alloc_semaphore(name=prefix + name))
        return used[-1]

    yield sem
    nc.clear_and_free_semaphores(used)
    nc.all_engine_barrier()


class Chain:

    def __init__(self, eng, sem):
        self.eng, self.sem, self.base, self.n = eng, sem, 0, 0

    def begin(self, base):
        self.base, self.n = base, 0

    def __call__(self, ins):
        self.n += 1
        ins.then_inc(self.sem, 1)
        self.eng.wait_ge(self.sem, self.base + self.n)


def rsqrt_mean(dve, link, total, count, mean, y, t):
    link(dve.tensor_scalar(mean, total, 1.0 / count, EPS, ALU.mult, ALU.add))
    link(dve.tensor_scalar(t.bitcast(I32), mean.bitcast(I32), 1, None, ALU.arith_shift_right))
    link(dve.tensor_scalar(y.bitcast(I32), t.bitcast(I32), -1.0, float(0x5F3759DF), ALU.mult, ALU.add))
    for _ in range(3):
        link(dve.tensor_tensor(t, y, y, ALU.mult))
        link(dve.scalar_tensor_tensor(t, t, -0.5, mean, ALU.mult, ALU.mult))
        link(dve.scalar_tensor_tensor(y, t, 1.5, y, ALU.add, ALU.mult))


RSQRT_LINKS = 12


def fill_identity(pool, ident, sem):
    pool.memset(ident, 0.0).then_inc(sem, 1)
    pool.wait_ge(sem, 1)
    pool.affine_select(out=ident, in_=ident, compare_op=ALU.not_equal, fill=1.0, base=0,
                       pattern=[[-1, P]], channel_multiplier=1).then_inc(sem, 1)


def input_projection(nc, x, g_mix, w_in, g_q, g_k, u_dram, q_dram, k_dram, v_dram):
    ROWS = 256
    STEPS = SEQ // ROWS
    with ExitStack() as ctx:
        def sb(name, shape, dt=F32):
            return ctx.enter_context(nc.sbuf_tensor("p_" + name, shape, dt))

        def ps(name, shape):
            return ctx.enter_context(nc.psum_tensor("p_" + name, shape, F32))

        sem = ctx.enter_context(semaphores(nc, "p_"))

        w_hi = sb("w_hi", [P, KC, 2048], F32R)
        w_lo = sb("w_lo", [P, KC, 2048], F32R)
        ident = sb("ident", [P, P])
        g_row = sb("g_row", [P, D_MODEL])
        gq_row = sb("gq_row", [P, 2, HEAD])
        xt = sb("xt", [P, 2, D_MODEL])
        xstat = sb("xstat", [P, 4, 2])
        ht_hi = [sb(f"ht_hi{b}", [P, KC, ROWS], F32R) for b in range(2)]
        ht_lo = [sb(f"ht_lo{b}", [P, KC, ROWS], F32R) for b in range(2)]
        sq = sb("sq", [P, 2, SB_WIDTH])
        qstat = sb("qstat", [P, 4, 2 * HEADS])
        qn = sb("qn", [P, 2, SB_WIDTH])
        qs = sb("qs", [P, 2, HEADS, 2, HEAD])
        w_raw = qs[:, :, :, :, :].rearrange("p a h s d -> p a (h s d)")
        qt = sb("qt", [P, 2, HEADS, P])
        v_out = sb("v_out", [P, 2, SB_WIDTH])
        u_out = sb("u_out", [P, 2, ROWS])

        acc = [ps(f"acc{i}", [P, BANK]) for i in range(4)]
        th_ps = ps("th_ps", [P, KC, P])
        tq_ps = ps("tq_ps", [P, HEADS, P])

        ident_ready = sem("ident_ready")
        rows_in = sem("rows_in")
        w_loaded = [sem(f"w_loaded{i}") for i in range(2)]
        w_split = sem("w_split")
        x_loaded = [sem(f"x_loaded{j}") for j in range(2)]
        dve_chain = sem("dve_chain")
        w_hi_ready = sem("w_hi_ready")
        squared = Tally(sem("squared"), 2)
        normed = Tally(sem("normed"), 2)
        h_turned = Tally(sem("h_turned"), 2)
        h_hi = Tally(sem("h_hi"), 2)
        h_lo = Tally(sem("h_lo"), 2)
        product = Tally(sem("product"), 10)
        qk_squared = Tally(sem("qk_squared"), 4)
        qk_normed = Tally(sem("qk_normed"), 4)
        qk_gained = Tally(sem("qk_gained"), 4)
        qk_hi = Tally(sem("qk_hi"), 4)
        qk_lo = Tally(sem("qk_lo"), 4)
        qk_turned = Tally(sem("qk_turned"), 4)
        qk_out = Tally(sem("qk_out"), 4)
        copied = Tally(sem("copied"), 6)
        qk_stored = [Tally(sem(f"qk_stored{i}"), 2 * DMA) for i in range(2)]
        v_stored = [Tally(sem(f"v_stored{i}"), DMA) for i in range(2)]
        u_stored = [Tally(sem(f"u_stored{i}"), 2 * DMA) for i in range(2)]
        ACT_TALLIES = [squared, h_hi, qk_squared, qk_hi, copied, qk_out]
        DVE_TALLIES = [normed, h_lo, qk_normed]
        POOL_TALLIES = [qk_gained, qk_lo]
        PE_TALLIES = [h_turned, product, qk_turned]
        SYNC_TALLIES = qk_stored + v_stored + u_stored

        block = ctx.enter_context(nc.Block())

        W_PIECES = 16

        def steps(eng, body):
            with eng.Fori(0, STEPS - 2, 2) as c:
                body(c, 0, True)
                body(c + 1, 1, True)
            body(STEPS - 2, 0, True)
            body(STEPS - 1, 1, False)

        @block.sync
        def _(sp):
            for tally in SYNC_TALLIES:
                tally.start(sp)

            def load_x(c):
                for j in range(2):
                    sp.wait_ge(h_turned.sem, h_turned.at(c - 1, j + 1))
                    sp.dma_start(xt[:, j, :], x[c * ROWS + j * P:c * ROWS + (j + 1) * P, :]).then_inc(x_loaded[j], DMA)

            load_x(0)
            sp.dma_start(g_row[:, :], g_mix.partition_broadcast(P)).then_inc(rows_in, DMA)
            sp.dma_start(gq_row[:, 0, :], g_q.partition_broadcast(P)).then_inc(rows_in, DMA)
            sp.dma_start(gq_row[:, 1, :], g_k.partition_broadcast(P)).then_inc(rows_in, DMA)
            for n in range(W_PIECES):
                k, cols = W_PIECE(n)
                if n >= 2:
                    sp.wait_ge(w_split, n - 1)
                sp.dma_start(w_raw[:, n % 2, :].rearrange("p (k f) -> p k f", k=2),
                             w_in[k * P:(k + 2) * P, cols].rearrange("(k p) f -> p k f", p=P)
                             ).then_inc(w_loaded[n % 2], DMA)

            def body(c, b, more):
                if more:
                    load_x(c + 1)
                for j in range(2):
                    row = c * ROWS + j * P
                    for n, dst in ((2 * j, q_dram), (2 * j + 1, k_dram)):
                        sp.wait_ge(qk_out.sem, qk_out.at(c, n + 1))
                        sp.dma_start(dst[:, :, row:row + P].rearrange("h d t -> d h t"),
                                     qt[:, n % 2, :, :]).then_inc(qk_stored[n % 2].sem, DMA)
                    sp.wait_ge(copied.sem, copied.at(c, j + 1))
                    sp.dma_start(v_dram[row:row + P, :], v_out[:, j, :]).then_inc(v_stored[j].sem, DMA)
                for f in range(4):
                    sp.wait_ge(copied.sem, copied.at(c, 3 + f))
                    n_here = ROWS // SUB
                    sp.dma_start(u_dram[f * P:(f + 1) * P, :, c * n_here:(c + 1) * n_here],
                                 u_out[:, f % 2, :].rearrange("p (l n) -> p l n", l=SUB)
                                 ).then_inc(u_stored[f % 2].sem, DMA)

            for c in range(STEPS):
                body(c, c % 2, c < STEPS - 1)
            for tally in SYNC_TALLIES:
                sp.wait_ge(tally.sem, tally.at(STEPS - 1, tally.per))

        @block.gpsimd
        def _(pool):
            for tally in POOL_TALLIES:
                tally.start(pool)
            fill_identity(pool, ident[:, :], ident_ready)
            pool.wait_ge(rows_in, 3 * DMA)

            def body(c, b, more):
                for j in range(2):
                    for n in (2 * j, 2 * j + 1):
                        pool.wait_ge(qk_normed.sem, qk_normed.at(c, n + 1))
                        view = qn[:, n % 2, :].rearrange("p (h d) -> p h d", h=HEADS)
                        gain = gq_row[:, n % 2, None, :].to_broadcast([P, HEADS, HEAD])
                        pool.tensor_tensor(view, view, gain, ALU.mult).then_inc(qk_gained.sem, 1)
                    for n in (2 * j, 2 * j + 1):
                        pool.wait_ge(qk_hi.sem, qk_hi.at(c, n + 1))
                        pool.tensor_tensor(qs[:, n % 2, :, 1, :], qn[:, n % 2, :].rearrange("p (h d) -> p h d", h=HEADS),
                                           qs[:, n % 2, :, 0, :], ALU.subtract).then_inc(qk_lo.sem, 1)

            steps(pool, body)

        @block.scalar
        def _(act):
            for tally in ACT_TALLIES:
                tally.start(act)

            def square_x(c, j, count):
                act.wait_ge(x_loaded[j], count)
                act.wait_ge(normed.sem, normed.at(c - 1, 2))
                act.wait_ge(squared.sem, squared.at(c, j))
                act.wait_ge(qk_normed.sem, qk_normed.at(c - 2, 4))
                act.activation(sq[:, :, :].rearrange("p a n -> p (a n)"), xt[:, j, :], ACT.Square,
                               accum_out=xstat[:, 0, j:j + 1]).then_inc(squared.sem, 1)

            def high_of_h(c, j, b):
                act.wait_ge(h_turned.sem, h_turned.at(c, j + 1))
                act.wait_ge(product.sem, product.at(c - 2, 10))
                act.activation(ht_hi[b][:, :, j * P:(j + 1) * P], th_ps[:, :, :], ACT.Copy).then_inc(h_hi.sem, 1)

            square_x(0, 0, DMA)
            square_x(0, 1, DMA)
            for n in range(W_PIECES):
                act.wait_ge(w_loaded[n % 2], DMA * (n // 2 + 1))
                k, cols = W_PIECE(n)
                act.activation(w_hi[:, k:k + 2, cols], w_raw[:, n % 2, :].rearrange("p (k f) -> p k f", k=2),
                               ACT.Copy).then_inc(w_hi_ready, 1)
                if n == 3:
                    high_of_h(0, 0, 0)
                if n == 5:
                    high_of_h(0, 1, 0)

            def square_qk(c, n):
                act.wait_ge(product.sem, product.at(c, (1, 2, 4, 5)[n]))
                if more_steps:
                    act.wait_ge(squared.sem, squared.at(c + 1, 2))
                act.wait_ge(qk_normed.sem, qk_normed.at(c - 1, 4) if n < 2 else qk_normed.at(c, 2))
                act.activation(sq[:, n % 2, :], acc[ACC(c_par, (0, 1, 3, 4)[n])][:, :], ACT.Square
                               ).then_inc(qk_squared.sem, 1)

            def high_qk(c, n):
                act.wait_ge(qk_gained.sem, qk_gained.at(c, n + 1))
                act.wait_ge(qk_turned.sem, qk_turned.at(c - 1, n + 3) if n < 2 else qk_turned.at(c, n - 1))
                act.activation(qs[:, n % 2, :, 0, :].bitcast(F32R), qn[:, n % 2, :].rearrange("p (h d) -> p h d", h=HEADS),
                               ACT.Copy).then_inc(qk_hi.sem, 1)

            def copy_v(c, j):
                act.wait_ge(product.sem, product.at(c, 3 * j + 3))
                act.wait_ge(v_stored[j].sem, v_stored[j].at(c - 1, DMA))
                act.activation(v_out[:, j, :], acc[ACC(c_par, 3 * j + 2)][:, :], ACT.Copy).then_inc(copied.sem, 1)

            def copy_u(c, f):
                act.wait_ge(product.sem, product.at(c, 7 + f))
                act.wait_ge(u_stored[f % 2].sem, u_stored[f % 2].at(c - 1 + f // 2, DMA * (2 - f // 2)))
                act.activation(u_out[:, f % 2, :].rearrange("p (l n) -> p n l", l=SUB),
                               acc[ACC(c_par, 6 + f)][:, 0:ROWS].rearrange("p (n l) -> p n l", l=SUB),
                               ACT.Copy).then_inc(copied.sem, 1)

            def out_qk(c, n):
                act.wait_ge(qk_turned.sem, qk_turned.at(c, n + 1))
                act.wait_ge(qk_stored[n % 2].sem, qk_stored[n % 2].at(c - 1 + n // 2, DMA * (2 - n // 2)))
                act.activation(qt[:, n % 2, :, :], tq_ps[:, :, :], ACT.Copy).then_inc(qk_out.sem, 1)

            def body(c, b, more):
                nonlocal c_par, more_steps
                c_par, more_steps = b, more
                if more:
                    square_x(c + 1, 0, c * DMA + 2 * DMA)
                    square_x(c + 1, 1, c * DMA + 2 * DMA)
                square_qk(c, 0)
                square_qk(c, 1)
                copy_v(c, 0)
                if more:
                    high_of_h(c + 1, 0, 1 - b)
                high_qk(c, 0)
                high_qk(c, 1)
                square_qk(c, 2)
                out_qk(c, 0)
                out_qk(c, 1)
                square_qk(c, 3)
                copy_v(c, 1)
                if more:
                    high_of_h(c + 1, 1, 1 - b)
                copy_u(c, 0)
                high_qk(c, 2)
                high_qk(c, 3)
                copy_u(c, 1)
                out_qk(c, 2)
                out_qk(c, 3)
                copy_u(c, 2)
                copy_u(c, 3)

            c_par, more_steps = 0, True
            steps(act, body)

        @block.vector
        def _(dve):
            for tally in DVE_TALLIES:
                tally.start(dve)
            link = Chain(dve, dve_chain)

            def stats_x(c):
                dve.wait_ge(squared.sem, squared.at(c, 2))
                rsqrt_mean(dve, link, xstat[:, 0, :], D_MODEL, xstat[:, 1, :], xstat[:, 2, :], xstat[:, 3, :])

            def norm_x(c, j):
                dve.scalar_tensor_tensor(xt[:, j, :], xt[:, j, :], xstat[:, 2, j:j + 1], g_row[:, :],
                                         ALU.mult, ALU.mult).then_inc(normed.sem, 1)

            def low_of_h(c, j, b):
                dve.wait_ge(h_hi.sem, h_hi.at(c, j + 1))
                dve.tensor_tensor(ht_lo[b][:, :, j * P:(j + 1) * P], th_ps[:, :, :],
                                  ht_hi[b][:, :, j * P:(j + 1) * P].bitcast(F32), ALU.subtract).then_inc(h_lo.sem, 1)

            dve.wait_ge(rows_in, 3 * DMA)
            stats_x(0)
            norm_x(0, 0)
            for n in range(W_PIECES):
                dve.wait_ge(w_hi_ready, n + 1)
                k, cols = W_PIECE(n)
                dve.tensor_tensor(w_lo[:, k:k + 2, cols], w_raw[:, n % 2, :].rearrange("p (k f) -> p k f", k=2),
                                  w_hi[:, k:k + 2, cols].bitcast(F32),
                                  ALU.subtract).then_inc(w_split, 1)
                if n == 3:
                    low_of_h(0, 0, 0)
                    norm_x(0, 1)
                if n == 5:
                    low_of_h(0, 1, 0)

            def norm_qk(c, j):
                for n in (2 * j, 2 * j + 1):
                    dve.wait_ge(qk_squared.sem, qk_squared.at(c, n + 1))
                    link(dve.tensor_reduce(qstat[:, 0, (n % 2) * HEADS:(n % 2 + 1) * HEADS],
                                           sq[:, n % 2, :].rearrange("p (h d) -> p h d", h=HEADS), AX_X, ALU.add))
                rsqrt_mean(dve, link, qstat[:, 0, :], HEAD, qstat[:, 1, :], qstat[:, 2, :], qstat[:, 3, :])
                for n in (2 * j, 2 * j + 1):
                    dve.wait_ge(qk_lo.sem, qk_lo.at(c - 1, n + 3) if n < 2 else qk_lo.at(c, n - 1))
                    scale = qstat[:, 2, (n % 2) * HEADS:(n % 2 + 1) * HEADS]
                    dve.tensor_tensor(qn[:, n % 2, :].rearrange("p (h d) -> p h d", h=HEADS),
                                      acc[ACC(c_par, (0, 1, 3, 4)[n])][:, :].rearrange("p (h d) -> p h d", h=HEADS),
                                      scale[:, :, None].to_broadcast([P, HEADS, HEAD]), ALU.mult
                                      ).then_inc(qk_normed.sem, 1)

            LINKS = RSQRT_LINKS + 2 * (2 + RSQRT_LINKS)

            def body(c, b, more):
                nonlocal c_par
                c_par = b
                link.begin(c * LINKS + RSQRT_LINKS)
                if more:
                    stats_x(c + 1)
                    norm_x(c + 1, 0)
                norm_qk(c, 0)
                if more:
                    low_of_h(c + 1, 0, 1 - b)
                    norm_x(c + 1, 1)
                norm_qk(c, 1)
                if more:
                    low_of_h(c + 1, 1, 1 - b)
                assert link.n == LINKS or not more

            c_par = 0
            steps(dve, body)

        @block.tensor
        def _(pe):
            for tally in PE_TALLIES:
                tally.start(pe)
            pe.wait_ge(ident_ready, 2)

            def turn_h(c, j):
                pe.wait_ge(normed.sem, normed.at(c, j + 1))
                pe.wait_ge(h_lo.sem, h_lo.at(c - 1, 2) if j == 0 else h_lo.at(c, 1))
                for k in range(KC):
                    mm = pe.transpose(th_ps[:, k, :], xt[:, j, k * P:(k + 1) * P], ident[:, :])
                mm.then_inc(h_turned.sem, 1)

            def turn_qk(c, n):
                pe.wait_ge(qk_lo.sem, qk_lo.at(c, n + 1))
                pe.wait_ge(qk_out.sem, qk_out.at(c - 1, 4) if n == 0 else qk_out.at(c, n))
                for h in range(HEADS):
                    mm = pe.transpose(tq_ps[:, h, :], qs[:, n % 2, h, :, :].rearrange("p s d -> p (s d)"), ident[:, :])
                mm.then_inc(qk_turned.sem, 1)

            def await_bank(c, n):
                prev, cc = n - 4, c
                if prev < 0:
                    prev, cc = prev + 10, c - 1
                if prev in (0, 1, 3, 4):
                    pe.wait_ge(qk_normed.sem, qk_normed.at(cc, (0, 1, 3, 4).index(prev) + 1))
                else:
                    pe.wait_ge(copied.sem, copied.at(cc, (2, 5, 6, 7, 8, 9).index(prev) + 1))

            def rows_product(c, b, n):
                j, kind = n // 3, n % 3
                await_bank(c, n)
                pe.wait_ge(w_split, 4 * (kind + 1))
                cols = slice(SSM_WIDTH * (kind + 1), SSM_WIDTH * (kind + 2))
                rows = slice(j * P, (j + 1) * P)
                out = acc[ACC(b, n)][:, :]
                for k in range(KC):
                    pe.matmul(out, ht_hi[b][:, k, rows], w_hi[:, k, cols], start=(k == 0), stop=False)
                    pe.matmul(out, ht_hi[b][:, k, rows], w_lo[:, k, cols], start=False, stop=False)
                    mm = pe.matmul(out, ht_lo[b][:, k, rows], w_hi[:, k, cols], start=False, stop=(k == KC - 1))
                mm.then_inc(product.sem, 1)

            def feature_product(c, b, f):
                await_bank(c, 6 + f)
                pe.wait_ge(w_split, W_PIECES)
                cols = slice(f * P, (f + 1) * P)
                out = acc[ACC(b, 6 + f)][:, 0:ROWS]
                for k in range(KC):
                    pe.matmul(out, w_hi[:, k, cols], ht_hi[b][:, k, :], start=(k == 0), stop=False)
                    pe.matmul(out, w_hi[:, k, cols], ht_lo[b][:, k, :], start=False, stop=False)
                    mm = pe.matmul(out, w_lo[:, k, cols], ht_hi[b][:, k, :], start=False, stop=(k == KC - 1))
                mm.then_inc(product.sem, 1)

            turn_h(0, 0)
            turn_h(0, 1)

            def body(c, b, more):
                pe.wait_ge(h_hi.sem, h_hi.at(c, 2))
                pe.wait_ge(h_lo.sem, h_lo.at(c, 2))
                rows_product(c, b, 0)
                rows_product(c, b, 1)
                rows_product(c, b, 2)
                if more:
                    turn_h(c + 1, 0)
                rows_product(c, b, 3)
                turn_qk(c, 0)
                turn_qk(c, 1)
                rows_product(c, b, 4)
                rows_product(c, b, 5)
                if more:
                    turn_h(c + 1, 1)
                feature_product(c, b, 0)
                feature_product(c, b, 1)
                turn_qk(c, 2)
                turn_qk(c, 3)
                feature_product(c, b, 2)
                feature_product(c, b, 3)

            steps(pe, body)


def W_PIECE(n):
    part = (n // 4 + 1) % 4
    return 2 * (n % 4), slice(part * 512, (part + 1) * 512)


def ACC(parity, n):
    return (10 * parity + n) % 4


def attention_units():
    units = []
    for i in range(SEQ // P):
        tiles = i + 1
        if tiles <= 8:
            units.append((i, 0, tiles * P, True, True))
        else:
            cut = tiles // 2
            units.append((i, cut * P, tiles * P, True, False))
            units.append((i, 0, cut * P, False, True))
    return units


def stick_breaking(nc, q_dram, k_dram, v_dram, y_dram):
    UNITS = attention_units()
    NU = len(UNITS)
    SLOTS = [(a, *u) for a in range(2) for u in UNITS]
    N = len(SLOTS)
    STEPS = HEADS // 2
    BLOCKS = SEQ // P
    SCALE = HEAD ** -0.5
    WIDE = 1024
    with ExitStack() as ctx:
        def sb(name, shape, dt=F32):
            return ctx.enter_context(nc.sbuf_tensor("a_" + name, shape, dt))

        sem = ctx.enter_context(semaphores(nc, "a_"))

        q2 = [sb(f"q2_{a}", [P, SEQ], F32R) for a in range(2)]
        k2_hi = [sb(f"k2_hi{a}", [P, SEQ], F32R) for a in range(2)]
        k2_lo = [sb(f"k2_lo{a}", [P, SEQ], F32R) for a in range(2)]
        v = [sb(f"v{a}", [P, BLOCKS, HEAD]) for a in range(2)]
        y = [sb(f"y{a}", [P, BLOCKS, HEAD]) for a in range(2)]
        off = [sb(f"off{b}", [P, WIDE]) for b in range(3)]
        on = [sb(f"on{b}", [P, WIDE]) for b in range(3)]
        left = [sb(f"left{b}", [P, SEQ + 1]) for b in range(2)]
        w = [sb(f"w{b}", [P, WIDE]) for b in range(3)]
        wt = [sb(f"wt{b}", [P, WIDE // P, P]) for b in range(3)]
        ident = sb("ident", [P, P])
        ident16 = sb("ident16", [P, P], BF16)
        never16 = sb("never16", [P, P], BF16)
        z_ps = [ctx.enter_context(nc.psum_tensor(f"a_ps_z{b}", [P, WIDE], F32)) for b in range(2)]
        wt_ps = [ctx.enter_context(nc.psum_tensor(f"a_ps_wt{b}", [P, BANK], F32)) for b in range(2)]
        y_ps = [ctx.enter_context(nc.psum_tensor(f"a_ps_y{b}", [P, BANK], F32)) for b in range(2)]

        constants = sem("constants")
        ones_ready = sem("ones_ready")
        head_loaded = [Tally(sem(f"head_loaded{a}"), 6 * DMA, 0) for a in range(2)]
        head_stored = [Tally(sem(f"head_stored{a}"), DMA, 1) for a in range(2)]
        scored = Tally(sem("scored"), N, 1)
        sig_off = Tally(sem("sig_off"), N, 1)
        sig_on = Tally(sem("sig_on"), N, 1)
        scanned = Tally(sem("scanned"), N, 1)
        by_pool = [m % 4 == 3 for m in range(N)]
        n_pool = sum(by_pool)
        weighed = Tally(sem("weighed"), N - n_pool, 1)
        weighed_p = Tally(sem("weighed_p"), n_pool, 1)
        groups = [(m, t0, min(4, (s[3] - s[2]) // P - t0)) for m, s in enumerate(SLOTS)
                  for t0 in range(0, (s[3] - s[2]) // P, 4)]
        first_group = [next(i for i, g in enumerate(groups) if g[0] == m) for m in range(N)] + [len(groups)]
        by_act = [g[1] > 0 for g in groups]
        turned = Tally(sem("turned"), len(groups), 1)
        copied_a = Tally(sem("copied_a"), sum(by_act), 1)
        copied_d = Tally(sem("copied_d"), len(groups) - sum(by_act), 1)
        gathered = Tally(sem("gathered"), N, 1)
        y_copied = Tally(sem("y_copied"), 2 * BLOCKS, 1)
        blocks_before = [sum(1 for s in SLOTS[:m] if s[5]) for m in range(N + 1)]

        blocks_of = [a * BLOCKS + i for a, i, *_ in SLOTS]

        block = ctx.enter_context(nc.Block())

        def wait_weighed(eng, s, m):
            p = sum(by_pool[:m + 1]) if m >= -1 else -sum(by_pool[m + 1:])
            eng.wait_ge(weighed_p.sem, weighed_p.at(s, p))
            eng.wait_ge(weighed.sem, weighed.at(s, m + 1 - p))

        def wait_copied(eng, s, g):
            p = sum(by_act[:g + 1]) if g >= -1 else -sum(by_act[g + 1:])
            eng.wait_ge(copied_a.sem, copied_a.at(s, p))
            eng.wait_ge(copied_d.sem, copied_d.at(s, g + 1 - p))

        def weigh(eng, s, m, tally):
            a, i, k0, k1, first, last = SLOTS[m]
            at = SEQ - (i + 1) * P
            eng.wait_ge(scanned.sem, scanned.at(s, m + 1))
            eng.wait_ge(sig_on.sem, sig_on.at(s, m + 1))
            eng.wait_ge(turned.sem, turned.at(s, first_group[m - 2] if m >= 2 else first_group[N + m - 2] - len(groups)))
            eng.tensor_tensor(w[m % 3][:, 0:k1 - k0], on[m % 3][:, 0:k1 - k0],
                              left[i % 2][:, at + k0 + 1:at + k1 + 1], ALU.mult).then_inc(tally.sem, 1)

        @block.sync
        def _(sp):
            for tally in head_stored:
                tally.start(sp)

            def load(s, a):
                h = 2 * s + a
                if s > 0:
                    sp.wait_ge(gathered.sem, gathered.at(s - 1, NU * (a + 1)))
                for dst, src in ((q2[a][:, :], q_dram[h]),
                                 (v[a][:, :, :], v_dram[:, h * HEAD:(h + 1) * HEAD].rearrange("(i p) d -> p i d", p=P))):
                    sp.dma_start(dst.bitcast(F32), src).then_inc(head_loaded[a].sem, DMA)
                for dst, part in ((k2_hi[a], 0), (k2_lo[a], 1)):
                    for copy in range(2):
                        sp.dma_start(dst[copy * HEAD:(copy + 1) * HEAD, :].bitcast(F32),
                                     k_dram[h, part * HEAD:(part + 1) * HEAD, :]).then_inc(head_loaded[a].sem, DMA)

            load(0, 0)
            load(0, 1)
            for s in range(STEPS):
                for a in range(2):
                    if s + 1 < STEPS:
                        load(s + 1, a)
                    sp.wait_ge(y_copied.sem, y_copied.at(s, BLOCKS * (a + 1)))
                    h = 2 * s + a
                    sp.dma_start(y_dram[:, h * HEAD:(h + 1) * HEAD].rearrange("(i p) d -> p i d", p=P),
                                 y[a][:, :, :]).then_inc(head_stored[a].sem, DMA)
            for tally in head_stored:
                sp.wait_ge(tally.sem, tally.at(STEPS - 1, DMA))

        @block.gpsimd
        def _(pool):
            weighed_p.start(pool)
            fill_identity(pool, ident[:, :], constants)
            pool.wait_ge(constants, 2)
            pool.tensor_copy(ident16[:, :], ident[:, :]).then_inc(constants, 1)
            pool.memset(never16[:, :], 0.0).then_inc(constants, 1)
            pool.wait_ge(constants, 4)
            pool.affine_select(out=never16[:, :], in_=never16[:, :], compare_op=ALU.is_gt, fill=-1e30, base=0,
                               pattern=[[-1, P]], channel_multiplier=1).then_inc(constants, 1)

            with pool.Fori(0, STEPS) as s:
                for m, (a, i, k0, k1, first, last) in enumerate(SLOTS):
                    if by_pool[m]:
                        weigh(pool, s, m, weighed_p)

        @block.scalar
        def _(act):
            sig_off.start(act)
            sig_on.start(act)
            copied_a.start(act)

            def sigmoids(s, m):
                a, i, k0, k1, first, last = SLOTS[m]
                act.wait_ge(scored.sem, scored.at(s, m + 1))
                act.wait_ge(scanned.sem, scanned.at(s, m - 2))
                act.activation(off[m % 3][:, 0:k1 - k0], z_ps[m % 2][:, 0:k1 - k0], ACT.Sigmoid,
                               scale=-SCALE).then_inc(sig_off.sem, 1)
                wait_weighed(act, s, m - 3)
                act.activation(on[m % 3][:, 0:k1 - k0], z_ps[m % 2][:, 0:k1 - k0], ACT.Sigmoid,
                               scale=SCALE).then_inc(sig_on.sem, 1)

            def copies(s, m):
                for g in range(first_group[m], first_group[m + 1]):
                    if by_act[g]:
                        _, t0, n = groups[g]
                        act.wait_ge(turned.sem, turned.at(s, g + 1))
                        act.wait_ge(gathered.sem, gathered.at(s, m - 2))
                        act.activation(wt[m % 3][:, t0:t0 + n, :], wt_ps[g % 2][:, 0:n * P].rearrange("p (t q) -> p t q", q=P),
                                       ACT.Copy).then_inc(copied_a.sem, 1)

            with act.Fori(0, STEPS) as s:
                for m in range(N + 2):
                    if m < N:
                        sigmoids(s, m)
                    if m >= 2:
                        copies(s, m - 2)

        @block.vector
        def _(dve):
            scanned.start(dve)
            weighed.start(dve)
            copied_d.start(dve)
            y_copied.start(dve)
            for b in range(2):
                dve.memset(left[b][:, SEQ:SEQ + 1], 1.0).then_inc(ones_ready, 1)
            dve.wait_ge(ones_ready, 2)

            def scan(s, m):
                a, i, k0, k1, first, last = SLOTS[m]
                at = SEQ - (i + 1) * P
                dve.wait_ge(sig_off.sem, sig_off.at(s, m + 1))
                readers = [n for n in range(m) if blocks_of[n] == blocks_of[m] - 2]
                wait_weighed(dve, s, readers[-1] if readers else -1)
                dve.wait_ge(scanned.sem, scanned.at(s, m))
                old = off[m % 3][:, 0:k1 - k0]
                dve.tensor_tensor_scan(left[i % 2][:, at + k0:at + k1][:, ::-1], old[:, ::-1], old[:, ::-1],
                                       1.0 if first else left[i % 2][:, at + k1:at + k1 + 1],
                                       ALU.mult, ALU.bypass).then_inc(scanned.sem, 1)

            def copies(s, m):
                for g in range(first_group[m], first_group[m + 1]):
                    if not by_act[g]:
                        _, t0, n = groups[g]
                        dve.wait_ge(turned.sem, turned.at(s, g + 1))
                        dve.wait_ge(gathered.sem, gathered.at(s, m - 2))
                        dve.tensor_copy(wt[m % 3][:, t0:t0 + n, :],
                                        wt_ps[g % 2][:, 0:n * P].rearrange("p (t q) -> p t q", q=P)
                                        ).then_inc(copied_d.sem, 1)

            def copy_y(s, m):
                a, i, k0, k1, first, last = SLOTS[m]
                if last:
                    dve.wait_ge(gathered.sem, gathered.at(s, m + 1))
                    if i == 0:
                        dve.wait_ge(head_stored[a].sem, head_stored[a].at(s - 1, DMA))
                    dve.tensor_copy(y[a][:, i, :], y_ps[i % 2][:, 0:HEAD]).then_inc(y_copied.sem, 1)

            with dve.Fori(0, STEPS) as s:
                for m in range(N + 4):
                    if m < N:
                        scan(s, m)
                    if 1 <= m <= N and not by_pool[m - 1]:
                        weigh(dve, s, m - 1, weighed)
                    if 2 <= m < N + 2:
                        copies(s, m - 2)
                    if m >= 4:
                        copy_y(s, m - 4)

        @block.tensor
        def _(pe):
            for tally in (scored, turned, gathered):
                tally.start(pe)
            pe.wait_ge(constants, 5)

            def score(s, m):
                a, i, k0, k1, first, last = SLOTS[m]
                if i == 0:
                    pe.wait_ge(head_loaded[a].sem, head_loaded[a].at(s, 6 * DMA))
                pe.wait_ge(sig_on.sem, sig_on.at(s, m - 1))
                for c0 in range(k0, k1, BANK):
                    c1 = min(c0 + BANK, k1)
                    out = z_ps[m % 2][:, c0 - k0:c1 - k0]
                    diagonal = first and c1 == k1
                    pe.matmul(out, q2[a][:, i * P:(i + 1) * P], k2_hi[a][:, c0:c1], start=True, stop=False)
                    mm = pe.matmul(out, q2[a][:, i * P:(i + 1) * P], k2_lo[a][:, c0:c1], start=False, stop=not diagonal)
                    if diagonal:
                        mm = pe.matmul(z_ps[m % 2][:, k1 - P - k0:k1 - k0], ident16[:, :], never16[:, :],
                                       start=False, stop=True)
                mm.then_inc(scored.sem, 1)

            def turn(s, m):
                wait_weighed(pe, s, m)
                for g in range(first_group[m], first_group[m + 1]):
                    _, t0, n = groups[g]
                    wait_copied(pe, s, g - 2)
                    for t in range(n):
                        mm = pe.transpose(wt_ps[g % 2][:, t * P:(t + 1) * P], w[m % 3][:, (t0 + t) * P:(t0 + t + 1) * P],
                                          ident[:, :])
                    mm.then_inc(turned.sem, 1)

            def gather(s, m):
                a, i, k0, k1, first, last = SLOTS[m]
                wait_copied(pe, s, first_group[m + 1] - 1)
                pe.wait_ge(y_copied.sem, y_copied.at(s, blocks_before[m] - 1))
                for t in range((k1 - k0) // P):
                    mm = pe.matmul(y_ps[i % 2][:, 0:HEAD], wt[m % 3][:, t, :], v[a][:, k0 // P + t, :],
                                   start=(first and t == 0), stop=(last and t == (k1 - k0) // P - 1))
                mm.then_inc(gathered.sem, 1)

            with pe.Fori(0, STEPS) as s:
                score(s, 0)
                score(s, 1)
                for m in range(N + 3):
                    if m + 2 < N:
                        score(s, m + 2)
                    if 1 <= m <= N:
                        turn(s, m - 1)
                    if m >= 3:
                        gather(s, m - 3)


def ssm_scan(nc, a_re, a_im, log_dt, b_re, b_im, c_re, c_im, u_dram, y_dram):
    PC = SSM_STATE
    G = SSM_GROUPS
    C = SSM_GROUP
    LEVELS = int(math.log2(CHUNKS))
    with ExitStack() as ctx:
        def sb(name, shape, dt=F32):
            return ctx.enter_context(nc.sbuf_tensor("s_" + name, shape, dt))

        def ps(name, shape):
            return ctx.enter_context(nc.psum_tensor("s_ps_" + name, shape, F32))

        sem = ctx.enter_context(semaphores(nc, "s_"))

        ident = sb("ident", [P, P])
        swap = sb("swap", [P, P])
        a_rows = sb("a_rows", [G, 2, 2, PC])
        lam = sb("lam", [P, 2, G])
        dt = sb("dt", [P, G])
        num = sb("num", [P, 16, G])
        sgn = sb("sgn", [P, 1])
        abar = sb("abar", [P, 2, G])
        coef = sb("coef", [P, 2, G])
        pw = sb("pw", [P, SUB + 1, 2, G])
        dbl = sb("dbl", [P, LEVELS, 2, G])
        b_in = sb("b_in", [P, 2, G, C])
        bb = sb("bb", [P, 2, G, C])
        c_rows = sb("c_rows", [P, 4, 3, PC])
        cc = sb("cc", [P, 2, G * C])
        t_in = sb("t_in", [P, G, SUB, C])
        mat_out = sb("mat_out", [P, G, SUB + 1, C])
        mat_in = sb("mat_in", [P, G, P])
        kern = sb("kern", [C, G, P])
        mat_within = sb("mat_within", [P, G, P])
        scratch = sb("scratch", [P, G, C])
        scratch2 = sb("scratch2", [P, G, C])

        u = sb("u", [P, G, CHUNKS])
        a_mat = [sb(f"a_mat{b}", [P, 2, LEVELS, P]) for b in range(4)]
        turned_part = sb("turned_part", [P, LEVELS, P])
        plain_part = [sb(f"plain_part{b}", [P, LEVELS, P]) for b in range(2)]
        s = [sb(f"s{b}", [P, 2, CHUNKS]) for b in range(4)]
        y = [sb(f"y{b}", [P, 2, CHUNKS]) for b in range(2)]
        bank = [ps(f"bank{i}", [P, BANK]) for i in range(8)]

        consts = sem("consts")
        params_in = sem("params_in")
        u_in = sem("u_in")
        dve_link = sem("dve_link")
        params_turned = sem("params_turned")
        params_read = sem("params_read")
        angles = sem("angles")
        sines = sem("sines")
        powers = sem("powers")
        in_rows = sem("in_rows")
        out_rows = sem("out_rows")
        in_turned = sem("in_turned")
        in_copied = sem("in_copied")
        kern_made = sem("kern_made")
        kern_copied = sem("kern_copied")
        cleared = sem("cleared")
        within_in = sem("within_in")
        PAIRS = G // 2
        plain_ready = sem("plain_ready")
        turned_ready = sem("turned_ready")
        a_ready = sem("a_ready")
        v_made = sem("v_made")
        term_made = [sem(f"term_made{i}") for i in range(2)]
        s_ready = [sem(f"s_ready{i}") for i in range(2)]
        y_made = sem("y_made")
        y_copied = sem("y_copied")
        y_stored = [sem(f"y_stored{i}") for i in range(2)]
        STEP = LEVELS + 1

        block = ctx.enter_context(nc.Block())

        @block.sync
        def _(sp):
            for part, src in ((0, a_re), (1, a_im)):
                for copy in range(2):
                    sp.dma_start(a_rows[:, part, copy, :], src).then_inc(params_in, DMA)
            sp.dma_start(dt[:, :], log_dt.partition_broadcast(P)).then_inc(params_in, DMA)
            for h, parts in ((0, (b_re, b_im)), (1, (b_im, b_re))):
                for x in range(2):
                    sp.dma_start(b_in[h * PC:(h + 1) * PC, x, :, :], parts[x].rearrange("g p c -> p g c")
                                 ).then_inc(params_in, DMA)
            for part, src in enumerate((c_re, c_im, c_re)):
                sp.dma_start(c_rows[:, :, part, :], src.rearrange("(s g) c p -> (g c) s p", s=4)).then_inc(params_in, DMA)
            for slab in range(4):
                for l in range(SUB):
                    sp.dma_start(u[l * C:(l + 1) * C, slab * 8:(slab + 1) * 8, :],
                                 u_dram[slab * P:(slab + 1) * P, l, :].rearrange("(g c) n -> c g n", c=C)
                                 ).then_inc(u_in, DMA)
            sp.wait_ge(kern_copied, G // 4)
            sp.wait_ge(cleared, 1)
            for l in range(SUB):
                sp.dma_start(mat_within[l * C:(l + 1) * C, :, l * C:], kern[:, :, 0:P - l * C]).then_inc(within_in, DMA)
            for p in range(PAIRS):
                sp.wait_ge(y_copied, p + 1)
                for i in range(2):
                    g = 2 * p + i
                    sp.dma_start(y_dram[g * C:(g + 1) * C, :, :].rearrange("c l n -> l c n"), y[p % 2][:, i, :]
                                 ).then_inc(y_stored[p % 2], DMA)
            for b in range(2):
                sp.wait_ge(y_stored[b], PAIRS * DMA)

        @block.gpsimd
        def _(pool):
            fill_identity(pool, ident[:, :], consts)
            pool.wait_ge(consts, 2)
            pool.tensor_copy(swap[:, 0:PC], ident[:, PC:P]).then_inc(consts, 1)
            pool.tensor_copy(swap[:, PC:P], ident[:, 0:PC]).then_inc(consts, 1)
            pool.memset(sgn[:, :], 1.0).then_inc(consts, 1)
            pool.wait_ge(consts, 5)
            pool.memset(sgn[0:PC, :], -1.0).then_inc(consts, 1)
            pool.memset(mat_within[:, :, :], 0.0).then_inc(cleared, 1)
            pool.wait_ge(powers, 1)
            pool.wait_ge(consts, 6)
            for g in range(G):
                if g >= 1:
                    pool.wait_ge(a_ready, g)
                pool.tensor_tensor(turned_part[:, :, :], swap[:, None, :].to_broadcast([P, LEVELS, P]),
                                   dbl[:, :, 1, g:g + 1].to_broadcast([P, LEVELS, P]), ALU.mult
                                   ).then_inc(turned_ready, 1)
                pool.wait_ge(turned_ready, g + 1)
                pool.wait_ge(plain_ready, g + 1)
                if g >= 8:
                    pool.wait_ge(y_made, g // 2 - 3)
                pool.tensor_tensor(a_mat[g // 2 % 4][:, g % 2, :, :], plain_part[g % 2][:, :, :], turned_part[:, :, :],
                                   ALU.add).then_inc(a_ready, 1)

        @block.scalar
        def _(act):
            act.wait_ge(angles, 1)
            act.activation(num[:, 6, :], num[:, 5, :], ACT.Sin).then_inc(sines, 1)
            act.activation(num[:, 7, :], num[:, 5, :], ACT.Sin, scale=0.5).then_inc(sines, 1)
            act.wait_ge(powers, 1)
            act.wait_ge(consts, 2)

            def plain(g):
                if g >= 2:
                    act.wait_ge(a_ready, g - 1)
                for k in range(LEVELS):
                    ins = act.activation(plain_part[g % 2][:, k, :], ident[:, :], ACT.Copy, scale=dbl[:, k, 0, g:g + 1])
                ins.then_inc(plain_ready, 1)

            plain(0)
            plain(1)
            for n in range(G // 4):
                act.wait_ge(in_turned, n + 1)
                act.activation(mat_in[:, 4 * n:4 * n + 4, :], bank[4 + n % 2][:, :].rearrange("p (g s) -> p g s", g=4),
                               ACT.Copy).then_inc(in_copied, 1)
            plain(2)
            plain(3)
            plain(4)
            plain(5)
            for p in range(PAIRS):
                if 2 * p + 7 < G:
                    plain(2 * p + 6)
                    plain(2 * p + 7)
                act.wait_ge(y_made, p + 1)
                if p >= 2:
                    act.wait_ge(y_stored[p % 2], p // 2 * 2 * DMA)
                act.activation(y[p % 2][:, :, :], bank[2 + p % 2][:, :].rearrange("p (g n) -> p g n", g=2),
                               ACT.Copy).then_inc(y_copied, 1)

        @block.vector
        def _(dve):
            link = Chain(dve, dve_link)

            def tt(out, a, b, op):
                link(dve.tensor_tensor(out, a, b, op))

            def ts(out, a, x, op0, y_=None, op1=ALU.bypass):
                link(dve.tensor_scalar(out, a, x, y_, op0, op1))

            def stt(out, a, x, op0, b, op1):
                link(dve.scalar_tensor_tensor(out, a, x, b, op0, op1))

            ROUND = 12582912.0

            def exp_of(out, x, k, r):
                ts(x, x, -87.0, ALU.max, 88.0, ALU.min)
                ts(k, x, 1.4426950408889634, ALU.mult, ROUND, ALU.add)
                ts(k, k, ROUND, ALU.subtract)
                stt(r, k, -0.693359375, ALU.mult, x, ALU.add)
                stt(r, k, 2.12194440e-4, ALU.mult, r, ALU.add)
                ts(out, r, 1.0 / 5040, ALU.mult)
                for term in (1 / 720, 1 / 120, 1 / 24, 1 / 6, 1 / 2, 1.0):
                    stt(out, out, term, ALU.add, r, ALU.mult)
                ts(out, out, 1.0, ALU.add)
                ts(k.bitcast(I32), k, 127.0, ALU.add, 8388608.0, ALU.mult)
                tt(out, out, k, ALU.mult)

            dve.wait_ge(params_in, 12 * DMA)
            dve.wait_ge(consts, 6)
            dve.wait_ge(params_turned, 2)
            link(dve.tensor_copy(lam[:, :, :], bank[0][:, 0:2 * G].rearrange("p (a g) -> p a g", a=2)))
            dve.wait_ge(params_turned, 10)
            for x in range(2):
                ts(cc[:, x, :], bank[1 + x][:, :], sgn[:, 0:1], ALU.mult, -1.0, ALU.mult)
            step, x_, k_, r_, e_ = dt[:, :], num[:, 0, :], num[:, 1, :], num[:, 2, :], num[:, 3, :]
            exp_of(num[:, 8, :], step, k_, r_)
            step = num[:, 8, :]
            tt(num[:, 4, :], lam[:, 1, :], step, ALU.mult)
            ts(k_, num[:, 4, :], 1.0 / (2 * math.pi), ALU.mult, ROUND, ALU.add)
            ts(k_, k_, ROUND, ALU.subtract)
            stt(r_, k_, -6.28125, ALU.mult, num[:, 4, :], ALU.add)
            stt(r_, k_, -TWO_PI_MID, ALU.mult, r_, ALU.add)
            stt(r_, k_, -TWO_PI_LOW, ALU.mult, r_, ALU.add)
            dve.tensor_scalar(num[:, 5, :], r_, -3.1415925, 3.1415925, ALU.max, ALU.min).then_inc(angles, 1)
            tt(x_, lam[:, 0, :], step, ALU.mult)
            exp_of(e_, x_, k_, r_)
            dve.wait_ge(sines, 2)
            tt(num[:, 9, :], num[:, 7, :], num[:, 7, :], ALU.mult)
            ts(num[:, 9, :], num[:, 9, :], -2.0, ALU.mult, 1.0, ALU.add)
            tt(abar[:, 0, :], e_, num[:, 9, :], ALU.mult)
            stt(abar[:, 1, :], num[:, 6, :], sgn[:, 0:1], ALU.mult, e_, ALU.mult)
            ts(num[:, 10, :], abar[:, 0, :], -1.0, ALU.add)
            ts(num[:, 11, :], lam[:, 1, :], sgn[:, 0:1], ALU.mult)
            tt(num[:, 12, :], lam[:, 0, :], lam[:, 0, :], ALU.mult)
            tt(num[:, 13, :], lam[:, 1, :], lam[:, 1, :], ALU.mult)
            tt(num[:, 12, :], num[:, 12, :], num[:, 13, :], ALU.add)
            link(dve.reciprocal(num[:, 12, :], num[:, 12, :]))
            tt(num[:, 13, :], num[:, 10, :], lam[:, 0, :], ALU.mult)
            tt(num[:, 14, :], abar[:, 1, :], num[:, 11, :], ALU.mult)
            tt(num[:, 13, :], num[:, 13, :], num[:, 14, :], ALU.add)
            tt(coef[:, 0, :], num[:, 13, :], num[:, 12, :], ALU.mult)
            tt(num[:, 13, :], abar[:, 1, :], lam[:, 0, :], ALU.mult)
            tt(num[:, 14, :], num[:, 10, :], num[:, 11, :], ALU.mult)
            tt(num[:, 13, :], num[:, 13, :], num[:, 14, :], ALU.subtract)
            tt(coef[:, 1, :], num[:, 13, :], num[:, 12, :], ALU.mult)
            link(dve.memset(pw[:, 0, 0, :], 1.0))
            link(dve.memset(pw[:, 0, 1, :], 0.0))
            link(dve.tensor_copy(pw[:, 1, :, :], abar[:, :, :]))

            def complex_product(out, a, b):
                tt(num[:, 14, :], a[:, 0, :], b[:, 0, :], ALU.mult)
                tt(num[:, 15, :], a[:, 1, :], b[:, 1, :], ALU.mult)
                tt(out[:, 0, :], num[:, 14, :], num[:, 15, :], ALU.subtract)
                tt(num[:, 14, :], a[:, 0, :], b[:, 1, :], ALU.mult)
                tt(num[:, 15, :], a[:, 1, :], b[:, 0, :], ALU.mult)
                tt(out[:, 1, :], num[:, 14, :], num[:, 15, :], ALU.add)

            for m in range(2, SUB + 1):
                complex_product(pw[:, m, :, :], pw[:, m - 1, :, :], abar)
            link(dve.tensor_copy(dbl[:, 0, 0, :], pw[:, SUB, 0, :]))
            ts(dbl[:, 0, 1, :], pw[:, SUB, 1, :], -1.0, ALU.mult)
            for k in range(1, LEVELS):
                complex_product(dbl[:, k, :, :], dbl[:, k - 1, :, :], dbl[:, k - 1, :, :])
            dve.engine_nop().then_inc(powers, 1)

            def by_group(x):
                return x[:, :, None].to_broadcast([P, G, C])

            tt(scratch[:, :, :], b_in[:, 0, :, :], by_group(coef[:, 0, :]), ALU.mult)
            tt(scratch2[:, :, :], b_in[:, 1, :, :], by_group(coef[:, 1, :]), ALU.mult)
            tt(bb[:, 0, :, :], scratch[:, :, :], scratch2[:, :, :], ALU.add)
            tt(scratch[:, :, :], b_in[:, 1, :, :], by_group(coef[:, 0, :]), ALU.mult)
            tt(scratch2[:, :, :], b_in[:, 0, :, :], by_group(coef[:, 1, :]), ALU.mult)
            tt(bb[:, 1, :, :], scratch[:, :, :], scratch2[:, :, :], ALU.subtract)
            for l in range(SUB):
                tt(scratch[:, :, :], bb[:, 0, :, :], by_group(pw[:, SUB - 1 - l, 0, :]), ALU.mult)
                tt(scratch2[:, :, :], bb[:, 1, :, :], by_group(pw[:, SUB - 1 - l, 1, :]), ALU.mult)
                tt(t_in[:, :, l, :], scratch[:, :, :], scratch2[:, :, :], ALU.add)
            dve.engine_nop().then_inc(in_rows, 1)
            c_of = [cc[:, x, :].rearrange("p (g c) -> p g c", c=C) for x in range(2)]
            for m in range(SUB + 1):
                tt(scratch[:, :, :], c_of[0], by_group(pw[:, m, 0, :]), ALU.mult)
                tt(scratch2[:, :, :], c_of[1], by_group(pw[:, m, 1, :]), ALU.mult)
                tt(mat_out[:, :, m, :], scratch[:, :, :], scratch2[:, :, :], ALU.add)
            dve.engine_nop().then_inc(out_rows, 1)
            for n in range(G // 4):
                dve.wait_ge(kern_made, n + 1)
                dve.tensor_copy(kern[:, 4 * n:4 * n + 4, :], bank[6 + n % 2][0:C, :].rearrange("p (g s) -> p g s", g=4)
                                ).then_inc(kern_copied, 1)
            for b in range(4):
                link(dve.memset(s[b][:, :, 0:1], 0.0))

            def take_v(p):
                dve.wait_ge(v_made, p + 1)
                if p >= 4:
                    dve.wait_ge(y_made, p - 3)
                dve.tensor_copy(s[p % 4][:, :, 1:CHUNKS],
                                bank[p % 2][:, :].rearrange("p (g n) -> p g n", g=2)[:, :, 0:CHUNKS - 1]
                                ).then_inc(s_ready[p % 2], 1)

            def add_term(p, k):
                d = 1 << k
                dve.wait_ge(term_made[p % 2], p // 2 * LEVELS + k + 1)
                dve.wait_ge(s_ready[p % 2], p // 2 * STEP + k + 1)
                dve.tensor_tensor(s[p % 4][:, :, d:], s[p % 4][:, :, d:],
                                  bank[p % 2][:, :].rearrange("p (g n) -> p g n", g=2)[:, :, 0:CHUNKS - d],
                                  ALU.add).then_inc(s_ready[p % 2], 1)

            for q in range(PAIRS // 2):
                take_v(2 * q)
                take_v(2 * q + 1)
                for k in range(LEVELS):
                    add_term(2 * q, k)
                    add_term(2 * q + 1, k)

        @block.tensor
        def _(pe):
            pe.wait_ge(consts, 2)
            pe.wait_ge(params_in, 12 * DMA)
            for part in range(2):
                pe.transpose(bank[0][:, part * G:(part + 1) * G], a_rows[:, part, :, :].rearrange("g a p -> g (a p)"),
                             ident[0:G, 0:G]).then_inc(params_turned, 1)
            for x in range(2):
                for slab in range(4):
                    pe.transpose(bank[1 + x][:, slab * P:(slab + 1) * P],
                                 c_rows[:, slab, x:x + 2, :].rearrange("q a p -> q (a p)"), ident[:, :]
                                 ).then_inc(params_turned, 1)
            pe.wait_ge(in_rows, 1)
            for n in range(G // 4):
                if n >= 2:
                    pe.wait_ge(in_copied, n - 1)
                for i in range(4):
                    mm = pe.transpose(bank[4 + n % 2][:, i * P:(i + 1) * P],
                                      t_in[:, 4 * n + i, :, :].rearrange("p l c -> p (l c)"), ident[:, :])
                mm.then_inc(in_turned, 1)
            pe.wait_ge(out_rows, 1)
            for n in range(G // 4):
                if n >= 2:
                    pe.wait_ge(kern_copied, n - 1)
                for i in range(4):
                    mm = pe.matmul(bank[6 + n % 2][0:C, i * P:(i + 1) * P], bb[:, 0, 4 * n + i, :],
                                   mat_out[:, 4 * n + i, 0:SUB, :].rearrange("p l c -> p (l c)"), start=True, stop=True)
                mm.then_inc(kern_made, 1)
            pe.wait_ge(in_copied, G // 4)
            pe.wait_ge(u_in, 4 * SUB * DMA)

            def make_v(p):
                if p >= 2:
                    pe.wait_ge(s_ready[p % 2], p // 2 * STEP)
                for i in range(2):
                    g = 2 * p + i
                    mm = pe.matmul(bank[p % 2][:, i * CHUNKS:(i + 1) * CHUNKS], mat_in[:, g, :], u[:, g, :],
                                   start=True, stop=True)
                mm.then_inc(v_made, 1)

            def make_term(p, k):
                d = 1 << k
                pe.wait_ge(s_ready[p % 2], p // 2 * STEP + k + 1)
                pe.wait_ge(a_ready, 2 * p + 2)
                for i in range(2):
                    mm = pe.matmul(bank[p % 2][:, i * CHUNKS:(i + 1) * CHUNKS - d], a_mat[p % 4][:, i, k, :],
                                   s[p % 4][:, i, 0:CHUNKS - d], start=True, stop=True)
                mm.then_inc(term_made[p % 2], 1)

            def make_y(p):
                pe.wait_ge(s_ready[p % 2], (p // 2 + 1) * STEP)
                if p >= 2:
                    pe.wait_ge(y_copied, p - 1)
                pe.wait_ge(within_in, SUB * DMA)
                for i in range(2):
                    g = 2 * p + i
                    out = bank[2 + p % 2][:, i * CHUNKS:(i + 1) * CHUNKS]
                    pe.matmul(out, mat_within[:, g, :], u[:, g, :], start=True, stop=False)
                    mm = pe.matmul(out, mat_out[:, g, 1:SUB + 1, :].rearrange("p l c -> p (l c)"), s[p % 4][:, i, :],
                                   start=False, stop=True)
                mm.then_inc(y_made, 1)

            for q in range(PAIRS // 2):
                make_v(2 * q)
                make_v(2 * q + 1)
                if q >= 1:
                    make_y(2 * q - 2)
                    make_y(2 * q - 1)
                for k in range(LEVELS):
                    make_term(2 * q, k)
                    make_term(2 * q + 1, k)
            make_y(PAIRS - 2)
            make_y(PAIRS - 1)


TWO_PI_MID = 0.0019350051879882812
TWO_PI_LOW = 2 * math.pi - 6.28125 - TWO_PI_MID


def mix_heads(nc, x, u_dram, y_ssm_dram, y_sb_dram, d_skip, w_glu, g_ssm, g_sb, w_out, x1_dram):
    ROWS = 512
    STEPS = SEQ // ROWS
    TILES = ROWS // P
    NF = SSM_WIDTH // P
    NCH = ROWS // SUB
    with ExitStack() as ctx:
        def sb(name, shape, dt=F32):
            return ctx.enter_context(nc.sbuf_tensor("m_" + name, shape, dt))

        def ps(name, shape):
            return ctx.enter_context(nc.psum_tensor("m_ps_" + name, shape, F32))

        sem = ctx.enter_context(semaphores(nc, "m_"))

        w_raw = sb("w_raw", [P, 2, 1024])
        glu_hi = sb("glu_hi", [P, NF, SSM_WIDTH], F32R)
        glu_lo = sb("glu_lo", [P, NF, SSM_WIDTH], F32R)
        out_hi = sb("out_hi", [P, KC, D_MODEL], F32R)
        out_lo = sb("out_lo", [P, KC, D_MODEL], F32R)
        gain = sb("gain", [P, KC])
        skip = sb("skip", [P, NF])
        ident = sb("ident", [P, P])
        ones = sb("ones", [P, 1])
        u = sb("u", [P, NF, ROWS])
        y = sb("y", [P, NF, ROWS])
        g = sb("g", [P, NF, ROWS])
        g_hi = sb("g_hi", [P, NF, ROWS], F32R)
        g_lo = sb("g_lo", [P, NF, ROWS], F32R)
        gate = sb("gate", [P, 2, ROWS])
        y2 = sb("y2", [P, NF, ROWS])
        y2_sq = sb("y2_sq", [P, NF, ROWS])
        y2_hi = sb("y2_hi", [P, NF, ROWS], F32R)
        y2_lo = sb("y2_lo", [P, NF, ROWS], F32R)
        xt = sb("xt", [P, TILES, D_MODEL])
        ys = sb("ys", [P, TILES, SB_WIDTH])
        junk = sb("junk", [P, SB_WIDTH])
        ys_hi = sb("ys_hi", [P, 4, P], F32R)
        ys_lo = sb("ys_lo", [P, 4, P], F32R)
        norm = sb("norm", [P, 2, TILES])
        stat = sb("stat", [P, 4, 2, TILES])

        a_ps = ps("a", [P, D_MODEL])
        b_ps = ps("b", [P, D_MODEL])
        glu_ps = [ps(f"glu{i}", [P, BANK]) for i in range(2)]
        turn_ps = ps("turn", [P, 4, P])
        sum_ps = ps("sum", [P, BANK])

        consts = sem("consts")
        params_in = sem("params_in")
        w_loaded = [sem(f"w_loaded{i}") for i in range(2)]
        w_hi_ready = sem("w_hi_ready")
        w_split = sem("w_split")
        dve_link = sem("dve_link")
        uy_loaded = sem("uy_loaded")
        x_loaded = [sem(f"x_loaded{j}") for j in range(TILES)]
        ys_loaded = [sem(f"ys_loaded{j}") for j in range(TILES)]
        skipped = Tally(sem("skipped"), NF)
        gelued = Tally(sem("gelued"), NF)
        g_high = Tally(sem("g_high"), NF)
        g_low = Tally(sem("g_low"), NF)
        glued = Tally(sem("glued"), NF)
        gated = Tally(sem("gated"), NF)
        y2_ready = Tally(sem("y2_ready"), NF)
        y2_squared = Tally(sem("y2_squared"), NF)
        y2_high = Tally(sem("y2_high"), NF)
        y2_low = Tally(sem("y2_low"), NF)
        summed = Tally(sem("summed"), 1)
        ys_squared = Tally(sem("ys_squared"), TILES)
        normed = Tally(sem("normed"), 1)
        turned = Tally(sem("turned"), TILES)
        ys_high = Tally(sem("ys_high"), TILES)
        ys_low = Tally(sem("ys_low"), TILES)
        a_made = Tally(sem("a_made"), TILES)
        b_made = Tally(sem("b_made"), TILES)
        a_added = Tally(sem("a_added"), TILES)
        b_added = Tally(sem("b_added"), TILES)
        stored = [Tally(sem(f"stored{j}"), DMA) for j in range(TILES)]
        ACT_TALLIES = [gelued, g_high, gated, y2_squared, y2_high, ys_squared, ys_high]
        DVE_TALLIES = [skipped, y2_ready, y2_low, normed, ys_low, a_added, b_added]
        PE_TALLIES = [glued, summed, turned, a_made, b_made]

        block = ctx.enter_context(nc.Block())
        W_GLU = 2
        W_PIECES = W_GLU + KC

        def w_piece(n):
            if n < W_GLU:
                rows = slice(2 * n, 2 * n + 2)
                src = w_glu.rearrange("(k p) f -> p k f", p=P)[:, rows, :]
                return src, glu_hi[:, rows, :], glu_lo[:, rows, :], None
            k = n - W_GLU
            src = w_out[k * P:(k + 1) * P, :].rearrange("p (o f) -> p o f", o=2)
            return (src, out_hi[:, k, :].rearrange("p (o f) -> p o f", o=2),
                    out_lo[:, k, :].rearrange("p (o f) -> p o f", o=2), k)

        def raw(n):
            return w_raw[:, n % 2, :].rearrange("p (o f) -> p o f", o=2)

        @block.sync
        def _(sp):
            for tally in stored:
                tally.start(sp)

            def load_uy(c):
                for src, dst in ((u_dram, u), (y_ssm_dram, y)):
                    if c > 0:
                        sp.wait_ge(gelued.sem, gelued.at(c - 1, NF))
                    for f in range(NF):
                        sp.dma_start(dst[:, f, :].rearrange("p (l n) -> p l n", l=SUB),
                                     src[f * P:(f + 1) * P, :, c * NCH:(c + 1) * NCH]).then_inc(uy_loaded, DMA)

            def load_rows(c):
                for j in range(TILES):
                    row = c * ROWS + j * P
                    if c > 0:
                        sp.wait_ge(turned.sem, turned.at(c - 1, j + 1))
                    sp.dma_start(ys[:, j, :], y_sb_dram[row:row + P, :]).then_inc(ys_loaded[j], DMA)
                    sp.wait_ge(stored[j].sem, stored[j].at(c - 1, DMA))
                    sp.dma_start(xt[:, j, :], x[row:row + P, :]).then_inc(x_loaded[j], DMA)

            load_uy(0)
            for src, dst in ((g_ssm, gain[:, 0:NF]), (g_sb, gain[:, NF:KC]), (d_skip, skip[:, :])):
                with nc.allow_non_contiguous_dma(reason="512 single values"):
                    sp.dma_start(dst, src.rearrange("(k p) -> p k", p=P)).then_inc(params_in, DMA)
            for n in range(W_PIECES):
                if n >= 2:
                    sp.wait_ge(w_split, n - 1)
                sp.dma_start(raw(n), w_piece(n)[0]).then_inc(w_loaded[n % 2], DMA)
                if n == W_GLU:
                    load_rows(0)
            for c in range(STEPS):
                if c + 1 < STEPS:
                    load_uy(c + 1)
                for j in range(TILES):
                    row = c * ROWS + j * P
                    sp.wait_ge(b_added.sem, b_added.at(c, j + 1))
                    sp.dma_start(x1_dram[row:row + P, :], xt[:, j, :]).then_inc(stored[j].sem, DMA)
                if c + 1 < STEPS:
                    load_rows(c + 1)
            for tally in stored:
                sp.wait_ge(tally.sem, tally.at(STEPS - 1, DMA))

        @block.gpsimd
        def _(pool):
            g_low.start(pool)
            fill_identity(pool, ident[:, :], consts)
            pool.memset(ones[:, :], 1.0).then_inc(consts, 1)

            with pool.Fori(0, STEPS) as c:
                for f in range(NF):
                    pool.wait_ge(g_high.sem, g_high.at(c, f + 1))
                    pool.wait_ge(glued.sem, glued.at(c - 1, NF))
                    pool.tensor_tensor(g_lo[:, f, :], g[:, f, :], g_hi[:, f, :].bitcast(F32), ALU.subtract
                                       ).then_inc(g_low.sem, 1)

        @block.scalar
        def _(act):
            for tally in ACT_TALLIES:
                tally.start(act)

            def gelus(c):
                for f in range(NF):
                    act.wait_ge(skipped.sem, skipped.at(c, f + 1))
                    act.wait_ge(y2_ready.sem, y2_ready.at(c - 1, NF))
                    act.wait_ge(g_low.sem, g_low.at(c - 1, NF))
                    act.activation(g[:, f, :], y[:, f, :], ACT.Gelu_apprx_tanh).then_inc(gelued.sem, 1)
                for f in range(NF):
                    act.wait_ge(gelued.sem, gelued.at(c, f + 1))
                    act.wait_ge(glued.sem, glued.at(c - 1, NF))
                    act.activation(g_hi[:, f, :], g[:, f, :], ACT.Copy).then_inc(g_high.sem, 1)

            def gates(c):
                for f in range(NF + 1):
                    if f < NF:
                        act.wait_ge(glued.sem, glued.at(c, f + 1))
                        act.wait_ge(y2_ready.sem, y2_ready.at(c, f - 1))
                        act.activation(gate[:, f % 2, :], glu_ps[f % 2][:, :], ACT.Sigmoid).then_inc(gated.sem, 1)
                    if f >= 1:
                        e = f - 1
                        act.wait_ge(y2_ready.sem, y2_ready.at(c, e + 1))
                        act.wait_ge(a_made.sem, a_made.at(c - 1, TILES))
                        act.activation(y2_hi[:, e, :], y2[:, e, :], ACT.Copy).then_inc(y2_high.sem, 1)
                        act.wait_ge(summed.sem, summed.at(c - 1, 1))
                        act.activation(y2_sq[:, e, :], y2[:, e, :], ACT.Square).then_inc(y2_squared.sem, 1)

            def squares_ys(c, count):
                for j in range(TILES):
                    act.wait_ge(ys_loaded[j], count)
                    act.wait_ge(normed.sem, normed.at(c - 1, 1))
                    act.wait_ge(ys_squared.sem, ys_squared.at(c, j))
                    act.activation(junk[:, :], ys[:, j, :], ACT.Square,
                                   accum_out=stat[:, 0, 1, j:j + 1]).then_inc(ys_squared.sem, 1)

            gelus(0)
            act.wait_ge(params_in, 3 * DMA)
            for n in range(W_PIECES):
                act.wait_ge(w_loaded[n % 2], (n // 2 + 1) * DMA)
                src, hi, lo, k = w_piece(n)
                if k is None:
                    act.activation(hi, raw(n), ACT.Copy).then_inc(w_hi_ready, 1)
                else:
                    act.activation(hi, raw(n), ACT.Copy, scale=gain[:, k:k + 1]).then_inc(w_hi_ready, 1)
            gates(0)
            squares_ys(0, DMA)

            def high_ys(c, j):
                act.wait_ge(turned.sem, turned.at(c, j + 1))
                act.wait_ge(b_made.sem, b_made.at(c, j))
                act.activation(ys_hi[:, :, :], turn_ps[:, :, :], ACT.Copy).then_inc(ys_high.sem, 1)

            def body(c, more):
                for j in range(TILES):
                    high_ys(c, j)
                if more:
                    gelus(c + 1)
                    squares_ys(c + 1, c * DMA + 2 * DMA)
                    gates(c + 1)

            with act.Fori(0, STEPS - 1) as c:
                body(c, True)
            body(STEPS - 1, False)

        @block.vector
        def _(dve):
            for tally in DVE_TALLIES:
                tally.start(dve)
            link = Chain(dve, dve_link)

            def skips(c, count):
                dve.wait_ge(uy_loaded, count)
                for f in range(NF):
                    dve.scalar_tensor_tensor(y[:, f, :], u[:, f, :], skip[:, f:f + 1], y[:, f, :], ALU.mult, ALU.add
                                             ).then_inc(skipped.sem, 1)

            def glus(c):
                for f in range(NF):
                    dve.wait_ge(gated.sem, gated.at(c, f + 1))
                    dve.wait_ge(y2_squared.sem, y2_squared.at(c - 1, NF))
                    dve.wait_ge(y2_low.sem, y2_low.at(c - 1, NF))
                    dve.tensor_tensor(y2[:, f, :].rearrange("p (n l) -> p l n", l=SUB),
                                      g[:, f, :].rearrange("p (l n) -> p l n", l=SUB),
                                      gate[:, f % 2, :].rearrange("p (l n) -> p l n", l=SUB), ALU.mult
                                      ).then_inc(y2_ready.sem, 1)
                    dve.wait_ge(y2_high.sem, y2_high.at(c, f + 1))
                    dve.wait_ge(a_made.sem, a_made.at(c - 1, TILES))
                    dve.tensor_tensor(y2_lo[:, f, :], y2[:, f, :], y2_hi[:, f, :].bitcast(F32), ALU.subtract
                                      ).then_inc(y2_low.sem, 1)

            def norms(c):
                dve.wait_ge(summed.sem, summed.at(c, 1))
                dve.wait_ge(ys_squared.sem, ys_squared.at(c, TILES))
                dve.wait_ge(b_added.sem, b_added.at(c - 1, TILES))
                link(dve.tensor_copy(stat[:, 0, 0, :], sum_ps[:, 0:TILES]))
                rsqrt_mean(dve, link, stat[:, 0, :, :], SSM_WIDTH, stat[:, 1, :, :], stat[:, 2, :, :], stat[:, 3, :, :])
                dve.tensor_copy(norm[:, :, :], stat[:, 2, :, :]).then_inc(normed.sem, 1)

            LINKS = 1 + RSQRT_LINKS

            dve.wait_ge(params_in, 3 * DMA)
            skips(0, 8 * DMA)
            for n in range(W_PIECES):
                dve.wait_ge(w_hi_ready, n + 1)
                src, hi, lo, k = w_piece(n)
                if k is None:
                    dve.tensor_tensor(lo, raw(n), hi.bitcast(F32), ALU.subtract).then_inc(w_split, 1)
                else:
                    dve.scalar_tensor_tensor(lo, raw(n), gain[:, k:k + 1], hi.bitcast(F32), ALU.mult, ALU.subtract
                                             ).then_inc(w_split, 1)
            glus(0)
            norms(0)

            def low_ys(c, j):
                dve.wait_ge(ys_high.sem, ys_high.at(c, j + 1))
                dve.wait_ge(b_made.sem, b_made.at(c, j))
                dve.tensor_tensor(ys_lo[:, :, :], turn_ps[:, :, :], ys_hi[:, :, :].bitcast(F32), ALU.subtract
                                  ).then_inc(ys_low.sem, 1)

            def add_a(c, j, count):
                if j == 0:
                    dve.wait_ge(normed.sem, normed.at(c, 1))
                dve.wait_ge(x_loaded[j], count)
                dve.wait_ge(a_made.sem, a_made.at(c, j + 1))
                dve.scalar_tensor_tensor(xt[:, j, :], a_ps[:, :], norm[:, 0, j:j + 1], xt[:, j, :],
                                         ALU.mult, ALU.add).then_inc(a_added.sem, 1)

            def add_b(c, j):
                dve.wait_ge(b_made.sem, b_made.at(c, j + 1))
                dve.wait_ge(a_added.sem, a_added.at(c, j + 1))
                dve.scalar_tensor_tensor(xt[:, j, :], b_ps[:, :], norm[:, 1, j:j + 1], xt[:, j, :],
                                         ALU.mult, ALU.add).then_inc(b_added.sem, 1)

            def body(c, more):
                low_ys(c, 0)
                for j in range(TILES):
                    add_a(c, j, c * DMA + DMA)
                    if j + 1 < TILES:
                        add_b(c, j)
                        low_ys(c, j + 1)
                if more:
                    skips(c + 1, c * (8 * DMA) + 16 * DMA)
                add_b(c, TILES - 1)
                if more:
                    glus(c + 1)
                    link.begin(c * LINKS + LINKS)
                    norms(c + 1)

            with dve.Fori(0, STEPS - 1) as c:
                body(c, True)
            body(STEPS - 1, False)

        @block.tensor
        def _(pe):
            for tally in PE_TALLIES:
                tally.start(pe)
            pe.wait_ge(consts, 3)

            def three_passes(out, hi_a, lo_a, hi_b, lo_b, start, stop):
                pe.matmul(out, hi_a, hi_b, start=start, stop=False)
                pe.matmul(out, hi_a, lo_b, start=False, stop=False)
                return pe.matmul(out, lo_a, hi_b, start=False, stop=stop)

            def glu(c):
                for f in range(NF):
                    pe.wait_ge(g_low.sem, g_low.at(c, NF))
                    pe.wait_ge(gated.sem, gated.at(c, f - 1) if f >= 2 else gated.at(c - 1, f + 3))
                    cols = slice(f * P, (f + 1) * P)
                    for k in range(NF):
                        mm = three_passes(glu_ps[f % 2][:, :], glu_hi[:, k, cols], glu_lo[:, k, cols],
                                          g_hi[:, k, :], g_lo[:, k, :], k == 0, k == NF - 1)
                    mm.then_inc(glued.sem, 1)

            def sums(c):
                pe.wait_ge(y2_squared.sem, y2_squared.at(c, NF))
                pe.wait_ge(normed.sem, normed.at(c - 1, 1))
                for j in range(TILES):
                    for k in range(NF):
                        mm = pe.matmul(sum_ps[:, j:j + 1], y2_sq[:, k, j * P:(j + 1) * P], ones[:, :],
                                       start=(k == 0), stop=(k == NF - 1))
                mm.then_inc(summed.sem, 1)

            def turn(c, j, count):
                pe.wait_ge(ys_loaded[j], count)
                pe.wait_ge(ys_low.sem, ys_low.at(c, j))
                for k in range(4):
                    mm = pe.transpose(turn_ps[:, k, :], ys[:, j, k * P:(k + 1) * P], ident[:, :])
                mm.then_inc(turned.sem, 1)

            def product(c, j, out, hi, lo, rows, base, done):
                for o in range(2):
                    cols = slice(o * BANK, (o + 1) * BANK)
                    for k in range(4):
                        mm = three_passes(out[:, cols], hi[:, k, rows], lo[:, k, rows], out_hi[:, base + k, cols],
                                          out_lo[:, base + k, cols], k == 0, k == 3)
                mm.then_inc(done.sem, 1)

            def body(c, more):
                turn(c, 0, c * DMA + DMA)
                pe.wait_ge(y2_low.sem, y2_low.at(c, NF))
                for j in range(TILES):
                    pe.wait_ge(a_added.sem, a_added.at(c, j))
                    product(c, j, a_ps, y2_hi, y2_lo, slice(j * P, (j + 1) * P), 0, a_made)
                    pe.wait_ge(ys_low.sem, ys_low.at(c, j + 1))
                    pe.wait_ge(b_added.sem, b_added.at(c, j))
                    product(c, j, b_ps, ys_hi, ys_lo, slice(0, P), NF, b_made)
                    if j + 1 < TILES:
                        turn(c, j + 1, c * DMA + DMA)
                if more:
                    glu(c + 1)
                    sums(c + 1)

            pe.wait_ge(w_split, W_GLU)
            glu(0)
            sums(0)
            pe.wait_ge(w_split, W_PIECES)
            with pe.Fori(0, STEPS - 1) as c:
                body(c, True)
            body(STEPS - 1, False)


def cross_attention(nc, x1_dram, mem, g_xa, g_mem, w_q, w_kv, g_q, g_k, w_o, x2_dram):
    TILES = 4
    STEPS = SEQ // (P * TILES)
    H = XA_HEADS
    SCALE = XA_HEAD ** -0.5
    MT = MEM // P
    TRAIL = 3
    with ExitStack() as ctx:
        def sb(name, shape, dt=F32):
            return ctx.enter_context(nc.sbuf_tensor("x_" + name, shape, dt))

        def ps(name, shape):
            return ctx.enter_context(nc.psum_tensor("x_ps_" + name, shape, F32))

        sem = ctx.enter_context(semaphores(nc, "x_"))

        w_raw = sb("w_raw", [P, 2, 1024])
        kv_hi = sb("kv_hi", [P, KC, XA_WIDTH], F32R)
        kv_lo = sb("kv_lo", [P, KC, XA_WIDTH], F32R)
        wq_hi = sb("wq_hi", [P, KC, XA_WIDTH], F32R)
        wq_lo = sb("wq_lo", [P, KC, XA_WIDTH], F32R)
        wo_hi = sb("wo_hi", [P, H, D_MODEL], F32R)
        wo_lo = sb("wo_lo", [P, H, D_MODEL], F32R)
        ident = sb("ident", [P, P])
        g_row = sb("g_row", [P, D_MODEL])
        gm_row = sb("gm_row", [P, D_MODEL])
        gains = sb("gains", [P, 2])
        mt = sb("mt", [P, MT, D_MODEL])
        memt_hi = sb("memt_hi", [P, KC, MEM], F32R)
        memt_lo = sb("memt_lo", [P, KC, MEM], F32R)
        kt = sb("kt", [P, H, MEM])
        v = sb("v", [P, MT, XA_WIDTH])
        xt = sb("xt", [P, 2, D_MODEL])
        xr = sb("xr", [P, 2, D_MODEL])
        junk = sb("junk", [P, D_MODEL])
        ht_hi = sb("ht_hi", [P, KC, P], F32R)
        ht_lo = sb("ht_lo", [P, KC, P], F32R)
        sq = sb("sq", [P, XA_WIDTH])
        qn = sb("qn", [P, XA_WIDTH])
        qt = sb("qt", [P, H, P])
        p = sb("p", [P, H, MEM])
        pt = sb("pt", [P, H * MT, P])
        ot_hi = sb("ot_hi", [P, H, P], F32R)
        ot_lo = sb("ot_lo", [P, H, P], F32R)
        xstat = sb("xstat", [P, 4, 1])
        mstat = sb("mstat", [P, 4, MT])
        qstat = sb("qstat", [P, 4, H])
        soft = sb("soft", [P, 4, H])

        th_ps = ps("th", [P, KC, P])
        to_ps = ps("to", [P, H, P])
        q_ps = ps("q", [P, BANK])
        s_ps = ps("s", [P, H, MEM])
        x_ps = ps("x", [P, D_MODEL])

        consts = sem("consts")
        params_in = sem("params_in")
        mem_in = sem("mem_in")
        w_loaded = [sem(f"w_loaded{i}") for i in range(2)]
        w_hi_ready = sem("w_hi_ready")
        w_split = sem("w_split")
        dve_link = sem("dve_link")
        mem_squared = sem("mem_squared")
        mem_normed = sem("mem_normed")
        mem_turned = sem("mem_turned")
        mem_high = sem("mem_high")
        mem_low = sem("mem_low")
        kv_made = sem("kv_made")
        kv_read = sem("kv_read")
        k_squared = sem("k_squared")
        k_normed = sem("k_normed")
        k_turned = sem("k_turned")
        kt_ready = sem("kt_ready")

        def tally(name):
            return Tally(sem(name), TILES)

        x_loaded = [sem(f"x_loaded{i}") for i in range(2)]
        xr_loaded = [sem(f"xr_loaded{i}") for i in range(2)]
        stored = [Tally(sem(f"stored{i}"), TILES // 2 * DMA) for i in range(2)]
        x_squared, h_high, q_squared, o_high, exped, pt_ready = [
            tally(n) for n in ("x_squared", "h_high", "q_squared", "o_high", "exped", "pt_ready")]
        x_normed, h_low, qt_ready, q_normed, o_low, maxed, p_scaled, added = [
            tally(n) for n in ("x_normed", "h_low", "qt_ready", "q_normed", "o_low", "maxed", "p_scaled", "added")]
        h_turned, q_made, q_turned, scored, p_turned, o_made, x_made = [
            tally(n) for n in ("h_turned", "q_made", "q_turned", "scored", "p_turned", "o_made", "x_made")]

        block = ctx.enter_context(nc.Block())
        PIECES = ([("kv", half, k) for half in range(2) for k in range(0, KC, 2)] + [("q", 0, k) for k in range(0, KC, 2)]
                  + [("o", 0, k) for k in range(H)])
        KV_PIECES = KC // 2

        def w_piece(n):
            what, half, k = PIECES[n]
            if what == "kv":
                src = w_kv[k * P:(k + 2) * P, half * XA_WIDTH:(half + 1) * XA_WIDTH].rearrange("(o p) f -> p o f", p=P)
                return src, kv_hi[:, k:k + 2, :], kv_lo[:, k:k + 2, :]
            if what == "q":
                src = w_q[k * P:(k + 2) * P, :].rearrange("(o p) f -> p o f", p=P)
                return src, wq_hi[:, k:k + 2, :], wq_lo[:, k:k + 2, :]
            two = "p (o f) -> p o f"
            return (w_o[k * P:(k + 1) * P, :].rearrange(two, o=2), wo_hi[:, k, :].rearrange(two, o=2),
                    wo_lo[:, k, :].rearrange(two, o=2))

        def raw(n):
            return w_raw[:, n % 2, :].rearrange("p (o f) -> p o f", o=2)

        def pipeline(eng, stage, lags, link=None):
            lead, trail = lags
            for j in range(-lead, TILES):
                stage(0, j, True)
            n0 = link.n if link else 0
            with eng.Fori(1, STEPS - 1) as c:
                if link:
                    link.begin((c - 1) * LINKS + n0)
                for j in range(TILES):
                    stage(c, j, None)
                assert not link or link.n == LINKS
            if link:
                link.begin((STEPS - 2) * LINKS + n0)
            for j in range(TILES + trail):
                stage(STEPS - 1, j, False)

        LINKS = TILES * (RSQRT_LINKS + 1 + RSQRT_LINKS + 1 + 1)

        def here(c, j, lag, edge):
            k = j - lag
            if edge is True:
                return k >= 0
            if edge is False:
                return k < TILES
            return True

        def slot(j, lag):
            return (j - lag) % 2

        @block.sync
        def _(sp):
            for t in stored:
                t.start(sp)
            for j in range(MT):
                sp.dma_start(mt[:, j, :], mem[j * P:(j + 1) * P, :]).then_inc(mem_in, DMA)
            sp.dma_start(gm_row[:, :], g_mem.partition_broadcast(P)).then_inc(params_in, DMA)
            sp.dma_start(g_row[:, :], g_xa.partition_broadcast(P)).then_inc(params_in, DMA)
            for n, src in enumerate((g_q, g_k)):
                sp.dma_start(gains[:, n:n + 1], src.rearrange("(p a) -> p a", a=1)).then_inc(params_in, DMA)

            def load_x(t):
                if t >= 2:
                    sp.wait_ge(h_turned.sem, h_turned.at(0, t - 1))
                sp.dma_start(xt[:, t % 2, :], x1_dram[t * P:(t + 1) * P, :]).then_inc(x_loaded[t % 2], DMA)

            def load_xr(t):
                if t >= 2:
                    sp.wait_ge(stored[t % 2].sem, stored[t % 2].at(0, (t // 2) * DMA))
                sp.dma_start(xr[:, t % 2, :], x1_dram[t * P:(t + 1) * P, :]).then_inc(xr_loaded[t % 2], DMA)

            for n in range(len(PIECES)):
                if n >= 2:
                    sp.wait_ge(w_split, n - 1)
                sp.dma_start(raw(n), w_piece(n)[0]).then_inc(w_loaded[n % 2], DMA)
                if n == 8:
                    load_x(0)
                    load_x(1)
                    load_xr(0)
                    load_xr(1)
            T = STEPS * TILES
            for t in range(T + TRAIL):
                if t + 2 < T:
                    load_x(t + 2)
                k = t - TRAIL
                if k >= 0:
                    sp.wait_ge(added.sem, added.at(0, k + 1))
                    sp.dma_start(x2_dram[k * P:(k + 1) * P, :], xr[:, k % 2, :]).then_inc(stored[k % 2].sem, DMA)
                    if k + 2 < T:
                        load_xr(k + 2)
            for i in range(2):
                sp.wait_ge(stored[i].sem, stored[i].at(STEPS - 1, TILES // 2 * DMA))

        @block.gpsimd
        def _(pool):
            fill_identity(pool, ident[:, :], consts)

        @block.scalar
        def _(act):
            for t in (x_squared, h_high, q_squared, o_high, exped, pt_ready):
                t.start(act)
            act.wait_ge(mem_in, MT * DMA)
            for j in range(MT):
                if j:
                    act.wait_ge(mem_squared, j)
                act.activation(junk[:, :], mt[:, j, :], ACT.Square, accum_out=mstat[:, 0, j:j + 1]).then_inc(mem_squared, 1)
            for n in range(len(PIECES)):
                act.wait_ge(w_loaded[n % 2], (n // 2 + 1) * DMA)
                if n == 4:
                    act.wait_ge(kv_made, MT)
                src, hi, lo = w_piece(n)
                act.activation(hi, raw(n), ACT.Copy).then_inc(w_hi_ready, 1)
                if n == 1:
                    for j in range(MT):
                        act.wait_ge(mem_turned, j + 1)
                        act.activation(memt_hi[:, :, j * P:(j + 1) * P], th_ps[:, :, :], ACT.Copy).then_inc(mem_high, 1)
                if n == 5:
                    for j in range(MT):
                        act.wait_ge(kv_made, j + 1)
                        if j:
                            act.wait_ge(k_normed, 1)
                        act.activation(sq[:, :], x_ps[:, j * BANK:(j + 1) * BANK], ACT.Square).then_inc(k_squared, 1)
                if n == 9:
                    for j in range(MT):
                        act.wait_ge(kv_made, MT + j + 1)
                        act.activation(v[:, j, :], x_ps[:, j * BANK:(j + 1) * BANK], ACT.Copy).then_inc(kv_read, 1)

            def square_x(c, j, lag, count):
                act.wait_ge(x_loaded[slot(j, lag)], count)
                act.wait_ge(x_normed.sem, x_normed.at(c, j - lag))
                act.wait_ge(x_squared.sem, x_squared.at(c, j - lag))
                act.activation(junk[:, :], xt[:, slot(j, lag), :], ACT.Square, accum_out=xstat[:, 0, 0:1]
                               ).then_inc(x_squared.sem, 1)

            def stage(c, j, edge):
                if here(c, j, -1, edge):
                    k = j + 1
                    act.wait_ge(h_turned.sem, h_turned.at(c, k + 1))
                    act.wait_ge(q_made.sem, q_made.at(c, k))
                    act.activation(ht_hi[:, :, :], th_ps[:, :, :], ACT.Copy).then_inc(h_high.sem, 1)
                if here(c, j, -2, edge):
                    square_x(c, j, -2, c * (2 * DMA) + ((j + 2) // 2 + 1) * DMA)
                if here(c, j, 0, edge):
                    act.wait_ge(q_made.sem, q_made.at(c, j + 1))
                    act.wait_ge(q_normed.sem, q_normed.at(c, j))
                    act.activation(sq[:, :], q_ps[:, :], ACT.Square).then_inc(q_squared.sem, 1)
                if here(c, j, 2, edge):
                    k = j - 2
                    act.wait_ge(o_made.sem, o_made.at(c, k + 1))
                    act.wait_ge(x_made.sem, x_made.at(c, k))
                    act.activation(ot_hi[:, :, :], to_ps[:, :, :], ACT.Copy).then_inc(o_high.sem, 1)
                if here(c, j, 1, edge):
                    k = j - 1
                    act.wait_ge(maxed.sem, maxed.at(c, k + 1))
                    act.wait_ge(p_turned.sem, p_turned.at(c, k))
                    for h in range(H):
                        ins = act.activation(p[:, h, :], s_ps[:, h, :], ACT.Exp, bias=soft[:, 1, h:h + 1], scale=SCALE,
                                             accum_out=soft[:, 2, h:h + 1])
                    ins.then_inc(exped.sem, 1)
                    act.wait_ge(p_turned.sem, p_turned.at(c, k + 1))
                    act.wait_ge(o_made.sem, o_made.at(c, k))
                    act.activation(pt[:, :, :], s_ps[:, :, :].rearrange("p h m -> p (h m)").rearrange("p (a q) -> p a q", q=P),
                                   ACT.Copy).then_inc(pt_ready.sem, 1)

            pipeline(act, stage, (2, 2))

        @block.vector
        def _(dve):
            for t in (x_normed, h_low, qt_ready, q_normed, o_low, maxed, p_scaled, added):
                t.start(dve)
            link = Chain(dve, dve_link)
            dve.wait_ge(params_in, 4 * DMA)
            dve.wait_ge(mem_squared, MT)
            rsqrt_mean(dve, link, mstat[:, 0, :], D_MODEL, mstat[:, 1, :], mstat[:, 2, :], mstat[:, 3, :])
            for j in range(MT):
                dve.scalar_tensor_tensor(mt[:, j, :], mt[:, j, :], mstat[:, 2, j:j + 1], gm_row[:, :],
                                         ALU.mult, ALU.mult).then_inc(mem_normed, 1)
            for n in range(len(PIECES)):
                dve.wait_ge(w_hi_ready, n + 1)
                src, hi, lo = w_piece(n)
                dve.tensor_tensor(lo, raw(n), hi.bitcast(F32), ALU.subtract).then_inc(w_split, 1)
                if n == 1:
                    for j in range(MT):
                        dve.wait_ge(mem_high, j + 1)
                        rows = slice(j * P, (j + 1) * P)
                        dve.tensor_tensor(memt_lo[:, :, rows], th_ps[:, :, :], memt_hi[:, :, rows].bitcast(F32), ALU.subtract
                                          ).then_inc(mem_low, 1)
                if n == 5:
                    for j in range(MT):
                        dve.wait_ge(k_squared, j + 1)
                        link(dve.tensor_reduce(qstat[:, 0, :], sq[:, :].rearrange("p (h d) -> p h d", h=H), AX_X, ALU.add))
                        rsqrt_mean(dve, link, qstat[:, 0, :], XA_HEAD, qstat[:, 1, :], qstat[:, 2, :], qstat[:, 3, :])
                        if j:
                            dve.wait_ge(k_turned, 1)
                        dve.tensor_tensor(qn[:, :].rearrange("p (h d) -> p h d", h=H),
                                          x_ps[:, j * BANK:(j + 1) * BANK].rearrange("p (h d) -> p h d", h=H),
                                          qstat[:, 2, :, None].to_broadcast([P, H, XA_HEAD]), ALU.mult).then_inc(k_normed, 1)
                        dve.wait_ge(k_turned, j + 1)
                        dve.tensor_scalar(kt[:, :, j * P:(j + 1) * P], to_ps[:, :, :], gains[:, 0:1], gains[:, 1:2],
                                          ALU.mult, ALU.mult).then_inc(kt_ready, 1)

            def stage(c, j, edge):
                if here(c, j, 3, edge):
                    add(c, j - 3)
                if here(c, j, 1, edge):
                    k = j - 1
                    dve.wait_ge(q_turned.sem, q_turned.at(c, k + 1))
                    dve.wait_ge(scored.sem, scored.at(c, k))
                    dve.tensor_copy(qt[:, :, :], to_ps[:, :, :]).then_inc(qt_ready.sem, 1)
                if here(c, j, -1, edge):
                    k = j + 1
                    dve.wait_ge(h_high.sem, h_high.at(c, k + 1))
                    dve.tensor_tensor(ht_lo[:, :, :], th_ps[:, :, :], ht_hi[:, :, :].bitcast(F32), ALU.subtract
                                      ).then_inc(h_low.sem, 1)
                if here(c, j, -2, edge):
                    k = j + 2
                    dve.wait_ge(x_squared.sem, x_squared.at(c, k + 1))
                    rsqrt_mean(dve, link, xstat[:, 0, :], D_MODEL, xstat[:, 1, :], xstat[:, 2, :], xstat[:, 3, :])
                    dve.scalar_tensor_tensor(xt[:, k % 2, :], xt[:, k % 2, :], xstat[:, 2, 0:1], g_row[:, :],
                                             ALU.mult, ALU.mult).then_inc(x_normed.sem, 1)
                if here(c, j, 2, edge):
                    k = j - 2
                    dve.wait_ge(o_high.sem, o_high.at(c, k + 1))
                    dve.tensor_tensor(ot_lo[:, :, :], to_ps[:, :, :], ot_hi[:, :, :].bitcast(F32), ALU.subtract
                                      ).then_inc(o_low.sem, 1)
                if here(c, j, 1, edge):
                    k = j - 1
                    dve.wait_ge(scored.sem, scored.at(c, k + 1))
                    dve.wait_ge(exped.sem, exped.at(c, k))
                    link(dve.tensor_reduce(soft[:, 0, :], s_ps[:, :, :], AX_X, ALU.max))
                    dve.tensor_scalar(soft[:, 1, :], soft[:, 0, :], -SCALE, None, ALU.mult).then_inc(maxed.sem, 1)
                if here(c, j, 0, edge):
                    dve.wait_ge(q_squared.sem, q_squared.at(c, j + 1))
                    link(dve.tensor_reduce(qstat[:, 0, :], sq[:, :].rearrange("p (h d) -> p h d", h=H), AX_X, ALU.add))
                    rsqrt_mean(dve, link, qstat[:, 0, :], XA_HEAD, qstat[:, 1, :], qstat[:, 2, :], qstat[:, 3, :])
                    dve.wait_ge(q_turned.sem, q_turned.at(c, j))
                    dve.tensor_tensor(qn[:, :].rearrange("p (h d) -> p h d", h=H), q_ps[:, :].rearrange("p (h d) -> p h d", h=H),
                                      qstat[:, 2, :, None].to_broadcast([P, H, XA_HEAD]), ALU.mult).then_inc(q_normed.sem, 1)
                if here(c, j, 1, edge):
                    k = j - 1
                    dve.wait_ge(exped.sem, exped.at(c, k + 1))
                    link(dve.reciprocal(soft[:, 3, :], soft[:, 2, :]))
                    dve.tensor_tensor(p[:, :, :], p[:, :, :], soft[:, 3, :, None].to_broadcast([P, H, MEM]), ALU.mult
                                      ).then_inc(p_scaled.sem, 1)

            def add(c, k):
                dve.wait_ge(x_made.sem, x_made.at(c, k + 1))
                dve.wait_ge(xr_loaded[k % 2], c * (2 * DMA) + (k // 2 + 1) * DMA)
                dve.tensor_tensor(xr[:, k % 2, :], x_ps[:, :], xr[:, k % 2, :], ALU.add).then_inc(added.sem, 1)

            pipeline(dve, stage, (2, 3), link)

        @block.tensor
        def _(pe):
            for t in (h_turned, q_made, q_turned, scored, p_turned, o_made, x_made):
                t.start(pe)

            def three_passes(out, hi_a, lo_a, hi_b, lo_b, start, stop):
                pe.matmul(out, hi_a, hi_b, start=start, stop=False)
                pe.matmul(out, hi_a, lo_b, start=False, stop=False)
                return pe.matmul(out, lo_a, hi_b, start=False, stop=stop)

            pe.wait_ge(consts, 2)
            for j in range(MT):
                pe.wait_ge(mem_normed, j + 1)
                if j:
                    pe.wait_ge(mem_low, j)
                for k in range(KC):
                    mm = pe.transpose(th_ps[:, k, :], mt[:, j, k * P:(k + 1) * P], ident[:, :])
                mm.then_inc(mem_turned, 1)
            pe.wait_ge(mem_low, MT)
            for half in range(2):
                pe.wait_ge(w_split, (half + 1) * KV_PIECES)
                for j in range(MT):
                    if half:
                        pe.wait_ge(k_normed, j + 1)
                    rows = slice(j * P, (j + 1) * P)
                    for k in range(KC):
                        mm = three_passes(x_ps[:, j * BANK:(j + 1) * BANK], memt_hi[:, k, rows], memt_lo[:, k, rows],
                                          kv_hi[:, k, :], kv_lo[:, k, :], k == 0, k == KC - 1)
                    mm.then_inc(kv_made, 1)
                if half == 0:
                    for j in range(MT):
                        pe.wait_ge(k_normed, j + 1)
                        if j:
                            pe.wait_ge(kt_ready, j)
                        for h in range(H):
                            mm = pe.transpose(to_ps[:, h, :], qn[:, h * P:(h + 1) * P], ident[:, :])
                        mm.then_inc(k_turned, 1)
            pe.wait_ge(kt_ready, MT)
            pe.wait_ge(kv_read, MT)
            pe.wait_ge(w_split, len(PIECES))

            def stage(c, j, edge):
                if here(c, j, -1, edge):
                    k = j + 1
                    pe.wait_ge(x_normed.sem, x_normed.at(c, k + 1))
                    pe.wait_ge(h_low.sem, h_low.at(c, k))
                    for i in range(KC):
                        mm = pe.transpose(th_ps[:, i, :], xt[:, k % 2, i * P:(i + 1) * P], ident[:, :])
                    mm.then_inc(h_turned.sem, 1)
                if here(c, j, 1, edge):
                    k = j - 1
                    pe.wait_ge(q_normed.sem, q_normed.at(c, k + 1))
                    pe.wait_ge(o_low.sem, o_low.at(c, k - 1))
                    for h in range(H):
                        mm = pe.transpose(to_ps[:, h, :], qn[:, h * P:(h + 1) * P], ident[:, :])
                    mm.then_inc(q_turned.sem, 1)
                if here(c, j, 0, edge):
                    pe.wait_ge(h_low.sem, h_low.at(c, j + 1))
                    pe.wait_ge(q_normed.sem, q_normed.at(c, j))
                    for k in range(KC):
                        mm = three_passes(q_ps[:, :], ht_hi[:, k, :], ht_lo[:, k, :], wq_hi[:, k, :], wq_lo[:, k, :],
                                          k == 0, k == KC - 1)
                    mm.then_inc(q_made.sem, 1)
                if here(c, j, 2, edge):
                    k = j - 2
                    pe.wait_ge(pt_ready.sem, pt_ready.at(c, k + 1))
                    pe.wait_ge(qt_ready.sem, qt_ready.at(c, k + 2 if here(c, j, 1, edge) else k + 1))
                    for h in range(H):
                        for m in range(MT):
                            mm = pe.matmul(to_ps[:, h, :], v[:, m, h * P:(h + 1) * P], pt[:, h * MT + m, :],
                                           start=(m == 0), stop=(m == MT - 1))
                    mm.then_inc(o_made.sem, 1)
                if here(c, j, 1, edge):
                    k = j - 1
                    pe.wait_ge(qt_ready.sem, qt_ready.at(c, k + 1))
                    pe.wait_ge(pt_ready.sem, pt_ready.at(c, k))
                    for h in range(H):
                        mm = pe.matmul(s_ps[:, h, :], qt[:, h, :], kt[:, h, :], start=True, stop=True)
                    mm.then_inc(scored.sem, 1)
                if here(c, j, 2, edge):
                    k = j - 2
                    pe.wait_ge(o_low.sem, o_low.at(c, k + 1))
                    pe.wait_ge(added.sem, added.at(c, k))
                    for o in range(2):
                        cols = slice(o * BANK, (o + 1) * BANK)
                        for h in range(H):
                            mm = three_passes(x_ps[:, cols], ot_hi[:, h, :], ot_lo[:, h, :], wo_hi[:, h, cols], wo_lo[:, h, cols],
                                              h == 0, h == H - 1)
                    mm.then_inc(x_made.sem, 1)
                if here(c, j, 1, edge):
                    k = j - 1
                    pe.wait_ge(p_scaled.sem, p_scaled.at(c, k + 1))
                    for i in range(H * MT):
                        mm = pe.transpose(s_ps[:, i // MT, (i % MT) * P:(i % MT + 1) * P], p[:, i // MT, (i % MT) * P:(i % MT + 1) * P],
                                          ident[:, :])
                    mm.then_inc(p_turned.sem, 1)

            pipeline(pe, stage, (1, 2))


def mlp(nc, x2_dram, g_mlp, w_up, w_down, out):
    ROWS = 1024
    CHUNKS2 = SEQ // ROWS
    TILES = ROWS // P
    FB = 256
    S = FB // P
    BLOCKS = D_FF // FB
    HALVES = ROWS // BANK
    U = HALVES * S
    LAST = CHUNKS2 * BLOCKS - 1
    with ExitStack() as ctx:
        def sb(name, shape, dt=F32):
            return ctx.enter_context(nc.sbuf_tensor("f_" + name, shape, dt))

        def ps(name, shape):
            return ctx.enter_context(nc.psum_tensor("f_ps_" + name, shape, F32))

        sem = ctx.enter_context(semaphores(nc, "f_"))

        ht_hi = sb("ht_hi", [P, KC, ROWS], F32R)
        ht_lo = sb("ht_lo", [P, KC, ROWS], F32R)
        y = sb("y", [P, TILES, D_MODEL])
        up_raw = sb("up_raw", [P, KC, FB])
        down_raw = sb("down_raw", [P, S, D_MODEL])
        up_hi = sb("up_hi", [P, KC, FB], F32R)
        up_lo = sb("up_lo", [P, KC, FB], F32R)
        down_hi = sb("down_hi", [P, S, D_MODEL], F32R)
        down_lo = sb("down_lo", [P, S, D_MODEL], F32R)
        a_hi = [sb(f"a_hi{b}", [P, S, ROWS], F32R) for b in range(2)]
        a_lo = [sb(f"a_lo{b}", [P, S, ROWS], F32R) for b in range(2)]
        act_f = sb("act_f", [P, 2, BANK])
        xt = sb("xt", [P, 2, D_MODEL])
        junk = sb("junk", [P, D_MODEL])
        g_row = sb("g_row", [P, D_MODEL])
        ident = sb("ident", [P, P])
        stat = sb("stat", [P, 4, 1])

        up_ps = [ps(f"up{i}", [P, BANK]) for i in range(2)]
        down_ps = [ps(f"down{i}", [P, D_MODEL]) for i in range(2)]
        th_ps = ps("th", [P, KC, P])

        consts = sem("consts")
        g_in = sem("g_in")
        dve_link = sem("dve_link")
        x_loaded = [sem(f"x_loaded{i}") for i in range(2)]
        x_squared = sem("x_squared")
        x_normed = sem("x_normed")
        h_turned = sem("h_turned")
        h_high = sem("h_high")
        h_low = sem("h_low")
        y_loaded = [sem(f"y_loaded{t}") for t in range(TILES)]
        stored = [sem(f"stored{t}") for t in range(TILES)]
        up_loaded = sem("up_loaded")
        down_loaded = sem("down_loaded")
        up_high = Tally(sem("up_high"), S)
        down_high = Tally(sem("down_high"), S)
        up_split = Tally(sem("up_split"), S)
        down_split = Tally(sem("down_split"), S)
        up_made = Tally(sem("up_made"), U)
        relued = Tally(sem("relued"), U)
        a_squared = Tally(sem("a_squared"), U)
        a_high = Tally(sem("a_high"), U)
        a_low = Tally(sem("a_low"), U)
        down_made = Tally(sem("down_made"), TILES)
        added = Tally(sem("added"), TILES)

        block = ctx.enter_context(nc.Block())

        def program(eng, prologue, up, down, boundary):
            prologue()
            for chunk in range(CHUNKS2):
                b0 = chunk * BLOCKS
                up(b0, 0, True)
                with eng.Fori(b0, b0 + BLOCKS - 2, 2) as b:
                    for par in range(2):
                        up(b + (par + 1), 1 - par, False)
                        down(b + par, par, False)
                for par in range(BLOCKS - 2, BLOCKS - 1):
                    up(b0 + par + 1, (par + 1) % 2, False)
                    down(b0 + par, par % 2, False)
                boundary(chunk)

        @block.sync
        def _(sp):
            def load_x(n):
                if n >= 2:
                    sp.wait_ge(h_turned, n - 1)
                sp.dma_start(xt[:, n % 2, :], x2_dram[n * P:(n + 1) * P, :]).then_inc(x_loaded[n % 2], DMA)

            def load_up(b):
                if b:
                    sp.wait_ge(up_split.sem, up_split.at(b - 1, S))
                sp.dma_start(up_raw[:, :, :], w_up[:, b % BLOCKS * FB:(b % BLOCKS + 1) * FB].rearrange("(k p) f -> p k f", p=P)
                             ).then_inc(up_loaded, DMA)

            def load_down(b):
                if b:
                    sp.wait_ge(down_split.sem, down_split.at(b - 1, S))
                sp.dma_start(down_raw[:, :, :], w_down[b % BLOCKS * FB:(b % BLOCKS + 1) * FB, :].rearrange("(s p) f -> p s f", p=P)
                             ).then_inc(down_loaded, DMA)

            def load_y(chunk, t):
                row = chunk * ROWS + t * P
                sp.dma_start(y[:, t, :], x2_dram[row:row + P, :]).then_inc(y_loaded[t], DMA)

            def store_y(chunk, t):
                row = chunk * ROWS + t * P
                sp.wait_ge(added.sem, added.at((chunk + 1) * BLOCKS - 1, t + 1))
                sp.dma_start(out[row:row + P, :], y[:, t, :]).then_inc(stored[t], DMA)

            load_x(0)
            sp.dma_start(g_row[:, :], g_mlp.partition_broadcast(P)).then_inc(g_in, DMA)
            load_x(1)
            load_up(0)
            for n in range(2, TILES):
                load_x(n)
            load_down(0)
            load_up(1)
            for t in range(TILES):
                load_y(0, t)
            load_x(TILES)
            load_x(TILES + 1)
            for b in range(2, LAST + 1):
                load_up(b)
                load_down(b - 1)
                if b == BLOCKS + 1:
                    for n in range(TILES + 2, 2 * TILES):
                        load_x(n)
                    for t in range(TILES):
                        store_y(0, t)
                    for t in range(TILES):
                        sp.wait_ge(stored[t], DMA)
                        load_y(1, t)
            load_down(LAST)
            for t in range(TILES):
                store_y(1, t)
            for t in range(TILES):
                sp.wait_ge(stored[t], 2 * DMA)

        @block.gpsimd
        def _(pool):
            fill_identity(pool, ident[:, :], consts)

        def up_slice(buf, s):
            return buf[:, :, s * P:(s + 1) * P]

        @block.scalar
        def _(act):
            for t in (up_high, down_high, relued, a_high):
                t.start(act)

            def square_x(n):
                act.wait_ge(x_loaded[n % 2], (n // 2 + 1) * DMA)
                if n:
                    act.wait_ge(x_normed, n)
                    act.wait_ge(x_squared, n)
                act.activation(junk[:, :], xt[:, n % 2, :], ACT.Square, accum_out=stat[:, 0, 0:1]).then_inc(x_squared, 1)

            def high_h(n):
                act.wait_ge(h_turned, n + 1)
                if n >= TILES:
                    act.wait_ge(up_made.sem, up_made.at(BLOCKS - 1, ((n - TILES) * P // BANK + 1) * S))
                t = n % TILES
                act.activation(ht_hi[:, :, t * P:(t + 1) * P], th_ps[:, :, :], ACT.Copy).then_inc(h_high, 1)

            def split_up(b, s, old):
                act.wait_ge(up_loaded, b * DMA + DMA)
                if old:
                    act.wait_ge(up_made.sem, up_made.at(b - 1, U - S + s + 1))
                act.activation(up_slice(up_hi, s), up_slice(up_raw, s), ACT.Copy).then_inc(up_high.sem, 1)

            def split_down(b, s):
                act.wait_ge(down_loaded, b * DMA + DMA)
                act.wait_ge(down_made.sem, down_made.at(b - 1, TILES))
                act.activation(down_hi[:, s, :], down_raw[:, s, :], ACT.Copy).then_inc(down_high.sem, 1)

            def prologue():
                square_x(0)
                for s in range(S):
                    split_up(0, s, False)
                for n in range(TILES):
                    if n + 1 < TILES:
                        square_x(n + 1)
                    high_h(n)

            def up(b, par, first):
                for u in range(U):
                    act.wait_ge(up_made.sem, up_made.at(b, u + 1))
                    act.wait_ge(a_low.sem, a_low.at(b - 1, u + U - 1) if u < 2 else a_low.at(b, u - 1))
                    act.activation(act_f[:, u % 2, :], up_ps[u % 2][:, :], ACT.Relu).then_inc(relued.sem, 1)
                    if u < S and not first:
                        split_down(b - 1, u)
                    if u >= U - S and b is not LAST:
                        split_up(b + 1, u - (U - S), True)
                    act.wait_ge(a_squared.sem, a_squared.at(b, u + 1))
                    act.wait_ge(down_made.sem, down_made.at(b - 2, TILES))
                    cols = slice(u // S * BANK, (u // S + 1) * BANK)
                    act.activation(a_hi[par][:, u % S, cols], act_f[:, u % 2, :], ACT.Copy).then_inc(a_high.sem, 1)

            def down(b, par, last):
                pass

            def boundary(chunk):
                b = (chunk + 1) * BLOCKS - 1
                if chunk == 0:
                    square_x(TILES)
                for s in range(S):
                    split_down(b, s)
                if chunk == 0:
                    for n in range(TILES, 2 * TILES):
                        if n + 1 < 2 * TILES:
                            square_x(n + 1)
                        high_h(n)

            program(act, prologue, up, down, boundary)

        @block.vector
        def _(dve):
            for t in (up_split, down_split, a_squared, a_low, added):
                t.start(dve)
            link = Chain(dve, dve_link)
            dve.wait_ge(g_in, DMA)

            def norm_x(n):
                dve.wait_ge(x_squared, n + 1)
                rsqrt_mean(dve, link, stat[:, 0, :], D_MODEL, stat[:, 1, :], stat[:, 2, :], stat[:, 3, :])
                dve.scalar_tensor_tensor(xt[:, n % 2, :], xt[:, n % 2, :], stat[:, 2, 0:1], g_row[:, :],
                                         ALU.mult, ALU.mult).then_inc(x_normed, 1)

            def low_h(n):
                dve.wait_ge(h_high, n + 1)
                t = n % TILES
                cols = slice(t * P, (t + 1) * P)
                dve.tensor_tensor(ht_lo[:, :, cols], th_ps[:, :, :], ht_hi[:, :, cols].bitcast(F32), ALU.subtract
                                  ).then_inc(h_low, 1)

            def split_up(b, s):
                dve.wait_ge(up_high.sem, up_high.at(b, s + 1))
                dve.tensor_tensor(up_slice(up_lo, s), up_slice(up_raw, s), up_slice(up_hi, s).bitcast(F32), ALU.subtract
                                  ).then_inc(up_split.sem, 1)

            def split_down(b, s):
                dve.wait_ge(down_high.sem, down_high.at(b, s + 1))
                dve.tensor_tensor(down_lo[:, s, :], down_raw[:, s, :], down_hi[:, s, :].bitcast(F32), ALU.subtract
                                  ).then_inc(down_split.sem, 1)

            def add(b, t, first, chunk):
                dve.wait_ge(down_made.sem, down_made.at(b, t + 1))
                dve.wait_ge(added.sem, added.at(b - 1, t + 1))
                dve.wait_ge(y_loaded[t], (chunk + 1) * DMA)
                dve.tensor_tensor(y[:, t, :], down_ps[t % 2][:, :], y[:, t, :], ALU.add).then_inc(added.sem, 1)

            def prologue():
                norm_x(0)
                for s in range(S):
                    split_up(0, s)
                for n in range(TILES):
                    if n + 1 < TILES:
                        norm_x(n + 1)
                    low_h(n)

            chunk_now = 0

            def up(b, par, first):
                for u in range(U):
                    dve.wait_ge(relued.sem, relued.at(b, u + 1))
                    dve.scalar_tensor_tensor(act_f[:, u % 2, :], up_ps[u % 2][:, :], 0.0, act_f[:, u % 2, :],
                                             ALU.max, ALU.mult).then_inc(a_squared.sem, 1)
                    if u < S and not first:
                        split_down(b - 1, u)
                    if u >= U - S and b is not LAST:
                        split_up(b + 1, u - (U - S))
                    dve.wait_ge(a_high.sem, a_high.at(b, u + 1))
                    cols = slice(u // S * BANK, (u // S + 1) * BANK)
                    dve.tensor_tensor(a_lo[par][:, u % S, cols], act_f[:, u % 2, :], a_hi[par][:, u % S, cols].bitcast(F32),
                                      ALU.subtract).then_inc(a_low.sem, 1)

            def down(b, par, last):
                for t in range(TILES):
                    add(b, t, False, chunk_now)

            def boundary(chunk):
                nonlocal chunk_now
                b = (chunk + 1) * BLOCKS - 1
                if chunk == 0:
                    norm_x(TILES)
                for s in range(S):
                    split_down(b, s)
                for i in range(TILES):
                    if chunk == 0:
                        if i % 2 == 1:
                            n = TILES + i // 2
                            norm_x(n + 1)
                            low_h(n)
                    add(b, i, False, chunk)
                if chunk == 0:
                    for n in range(TILES + TILES // 2, 2 * TILES):
                        if n + 1 < 2 * TILES:
                            norm_x(n + 1)
                        low_h(n)
                    chunk_now = 1

            program(dve, prologue, up, down, boundary)

        @block.tensor
        def _(pe):
            for t in (up_made, down_made):
                t.start(pe)
            pe.wait_ge(consts, 2)

            def turn_h(n):
                pe.wait_ge(x_normed, n + 1)
                if n:
                    pe.wait_ge(h_low, n)
                for k in range(KC):
                    mm = pe.transpose(th_ps[:, k, :], xt[:, n % 2, k * P:(k + 1) * P], ident[:, :])
                mm.then_inc(h_turned, 1)

            def prologue():
                for n in range(TILES // 2):
                    turn_h(n)

            def up(b, par, first):
                for u in range(U):
                    half, s = u // S, u % S
                    if first:
                        base = b // BLOCKS * TILES
                        if s == 0:
                            pe.wait_ge(h_low, base + (half + 1) * TILES // 2)
                        if half == 0:
                            turn_h(base + TILES // 2 + s)
                    if half == 0:
                        pe.wait_ge(up_split.sem, up_split.at(b, s + 1))
                    pe.wait_ge(a_squared.sem, a_squared.at(b - 1, U + u - 1) if u < 2 else a_squared.at(b, u - 1))
                    rows, cols = slice(half * BANK, (half + 1) * BANK), slice(s * P, (s + 1) * P)
                    o = up_ps[u % 2][:, :]
                    for k in range(KC):
                        pe.matmul(o, up_hi[:, k, cols], ht_hi[:, k, rows], start=(k == 0), stop=False)
                        pe.matmul(o, up_hi[:, k, cols], ht_lo[:, k, rows], start=False, stop=False)
                        mm = pe.matmul(o, up_lo[:, k, cols], ht_hi[:, k, rows], start=False, stop=(k == KC - 1))
                    mm.then_inc(up_made.sem, 1)
                    if first and u == S - 1:
                        for n in range(TILES // 2 + S, TILES):
                            turn_h(base + n)

            def down_tile(b, par, t):
                pe.wait_ge(added.sem, added.at(b - 1, TILES + t - 1) if t < 2 else added.at(b, t - 1))
                rows = slice(t * P, (t + 1) * P)
                for half in range(2):
                    cols = slice(half * BANK, (half + 1) * BANK)
                    o = down_ps[t % 2][:, cols]
                    for s in range(S):
                        pe.matmul(o, a_hi[par][:, s, rows], down_hi[:, s, cols], start=(s == 0), stop=False)
                        pe.matmul(o, a_hi[par][:, s, rows], down_lo[:, s, cols], start=False, stop=False)
                        mm = pe.matmul(o, a_lo[par][:, s, rows], down_hi[:, s, cols], start=False, stop=(s == S - 1))
                mm.then_inc(down_made.sem, 1)

            def down(b, par, last):
                pe.wait_ge(a_low.sem, a_low.at(b, U))
                pe.wait_ge(down_split.sem, down_split.at(b, S))
                for t in range(TILES):
                    down_tile(b, par, t)

            def boundary(chunk):
                b = (chunk + 1) * BLOCKS - 1
                if chunk == 0:
                    turn_h(TILES)
                pe.wait_ge(a_low.sem, a_low.at(b, U))
                pe.wait_ge(down_split.sem, down_split.at(b, S))
                for t in range(TILES):
                    down_tile(b, 1, t)
                    if chunk == 0 and t % 2 == 1 and t // 2 + 1 < TILES // 2:
                        turn_h(TILES + t // 2 + 1)

            program(pe, prologue, up, down, boundary)


def decoder_block(nc, t, out):
    def scratch(name, *shape):
        return nc.dram_tensor(name, shape, F32).ap()

    u = scratch("u", SSM_WIDTH, SUB, CHUNKS)
    q = scratch("q", HEADS, P, SEQ)
    k = scratch("k", HEADS, P, SEQ)
    v = scratch("v", SEQ, SB_WIDTH)
    y_ssm = scratch("y_ssm", SSM_WIDTH, SUB, CHUNKS)
    y_sb = scratch("y_sb", SEQ, SB_WIDTH)
    x1 = scratch("x1", SEQ, D_MODEL)
    x2 = scratch("x2", SEQ, D_MODEL)
    input_projection(nc, t["x"], t["g_mix"], t["w_in"], t["sb_g_q"], t["sb_g_k"], u, q, k, v)
    ssm_scan(nc, t["ssm_a_re"], t["ssm_a_im"], t["ssm_log_dt"], t["ssm_b_re"], t["ssm_b_im"],
             t["ssm_c_re"], t["ssm_c_im"], u, y_ssm)
    stick_breaking(nc, q, k, v, y_sb)
    mix_heads(nc, t["x"], u, y_ssm, y_sb, t["ssm_d"], t["ssm_w_glu"], t["g_out_ssm"], t["g_out_sb"], t["w_out"], x1)
    cross_attention(nc, x1, t["mem"], t["g_xa"], t["g_mem"], t["xa_w_q"], t["xa_w_kv"], t["xa_g_q"], t["xa_g_k"],
                    t["xa_w_o"], x2)
    mlp(nc, x2, t["g_mlp"], t["w_up"], t["w_down"], out)


INPUTS = ("x", "mem", "g_mix", "w_in", "ssm_a_re", "ssm_a_im", "ssm_log_dt", "ssm_b_re", "ssm_b_im", "ssm_c_re",
          "ssm_c_im", "ssm_d", "ssm_w_glu", "sb_g_q", "sb_g_k", "g_out_ssm", "g_out_sb", "w_out", "g_xa", "g_mem",
          "xa_w_q", "xa_w_kv", "xa_g_q", "xa_g_k", "xa_w_o", "g_mlp", "w_up", "w_down")


def kernel(**inputs):
    import numpy as np
    import concourse.bacc as bacc
    from concourse.bass_utils import run_bass_kernel_spmd

    nc = bacc.Bacc("TRN2", target_bir_lowering=False, num_devices=1)
    arrays, tensors = {}, {}
    for name in INPUTS:
        a = np.ascontiguousarray(inputs[name])
        arrays[f"in_{name}"] = a
        tensors[name] = nc.dram_tensor(f"in_{name}", a.shape, mybir.dt.from_np(a.dtype), kind="ExternalInput").ap()[0]
    out = nc.dram_tensor("out", (1, SEQ, D_MODEL), F32, kind="ExternalOutput").ap()
    decoder_block(nc, tensors, out[0])
    result = run_bass_kernel_spmd(nc, [arrays], core_ids=[0])
    return result.results[0]["out"]
```

```python
import math
from contextlib import ExitStack, contextmanager

from concourse import mybir
F32 = mybir.dt.float32
F32R = mybir.dt.float32r
BF16 = mybir.dt.bfloat16
I32 = mybir.dt.int32
ALU = mybir.AluOpType
ACT = mybir.ActivationFunctionType
AX_X = mybir.AxisListType.X

P = 128
BANK = 512
D_MODEL = 1024
SEQ = 2048
SSM_WIDTH = 512
SSM_GROUP = 16
SSM_GROUPS = 32
SSM_STATE = 64
HEADS = 8
HEAD = 64
SB_WIDTH = HEADS * HEAD
MEM = 256
XA_HEADS = 4
XA_HEAD = 128
XA_WIDTH = XA_HEADS * XA_HEAD
D_FF = 4096
EPS = 1e-6
KC = D_MODEL // P
SUB = P // SSM_GROUP
CHUNKS = SEQ // SUB
DMA = 16


class Tally:

    def __init__(self, sem, per, lead=2):
        self.sem, self.per, self.lead = sem, per, lead

    def start(self, eng):
        eng.sem_inc(self.sem, self.per * self.lead)

    def at(self, step, k):
        return step * self.per + (self.lead * self.per + k)


@contextmanager
def semaphores(nc, prefix):
    used = []

    def sem(name):
        used.append(nc.alloc_semaphore(name=prefix + name))
        return used[-1]

    yield sem
    nc.clear_and_free_semaphores(used)
    nc.all_engine_barrier()


class Chain:

    def __init__(self, eng, sem):
        self.eng, self.sem, self.base, self.n = eng, sem, 0, 0

    def begin(self, base):
        self.base, self.n = base, 0

    def __call__(self, ins):
        self.n += 1
        ins.then_inc(self.sem, 1)
        self.eng.wait_ge(self.sem, self.base + self.n)


def rsqrt_mean(dve, link, total, count, mean, y, t):
    link(dve.tensor_scalar(mean, total, 1.0 / count, EPS, ALU.mult, ALU.add))
    rsqrt(dve, link, mean, y, t)


def rsqrt(dve, link, mean, y, t):
    link(dve.tensor_scalar(t.bitcast(I32), mean.bitcast(I32), 1, None, ALU.arith_shift_right))
    link(dve.tensor_scalar(y.bitcast(I32), t.bitcast(I32), -1.0, float(0x5F3759DF), ALU.mult, ALU.add))
    for _ in range(3):
        link(dve.tensor_tensor(t, y, y, ALU.mult))
        link(dve.scalar_tensor_tensor(t, t, -0.5, mean, ALU.mult, ALU.mult))
        link(dve.scalar_tensor_tensor(y, t, 1.5, y, ALU.add, ALU.mult))


RSQRT_LINKS = 12


def fill_identity(pool, ident, sem):
    pool.memset(ident, 0.0).then_inc(sem, 1)
    pool.wait_ge(sem, 1)
    pool.affine_select(out=ident, in_=ident, compare_op=ALU.not_equal, fill=1.0, base=0,
                       pattern=[[-1, P]], channel_multiplier=1).then_inc(sem, 1)


def input_projection(nc, x, g_mix, w_in, g_q, g_k, u_dram, q_dram, k_dram, v_dram):
    ROWS = 256
    STEPS = SEQ // ROWS
    with ExitStack() as ctx:
        def sb(name, shape, dt=F32):
            return ctx.enter_context(nc.sbuf_tensor("p_" + name, shape, dt))

        def ps(name, shape):
            return ctx.enter_context(nc.psum_tensor("p_" + name, shape, F32))

        sem = ctx.enter_context(semaphores(nc, "p_"))

        w_hi = sb("w_hi", [P, KC, 2048], F32R)
        w_lo = sb("w_lo", [P, KC, 2048], F32R)
        ident = sb("ident", [P, P])
        g_row = sb("g_row", [P, D_MODEL])
        gq_row = sb("gq_row", [P, 2, HEAD])
        xt = sb("xt", [P, 2, D_MODEL])
        xstat = sb("xstat", [P, 4, 2])
        ht_hi = [sb(f"ht_hi{b}", [P, KC, ROWS], F32R) for b in range(2)]
        ht_lo = [sb(f"ht_lo{b}", [P, KC, ROWS], F32R) for b in range(2)]
        sq = sb("sq", [P, 2, SB_WIDTH])
        qstat = sb("qstat", [P, 4, 2 * HEADS])
        qn = sb("qn", [P, 2, SB_WIDTH])
        qs = sb("qs", [P, 2, HEADS, 2, HEAD])
        qt = sb("qt", [P, 2, HEADS, P])
        w_raw = [qs[:, i, :, :, :].rearrange("p h s d -> p (h s d)") for i in range(2)]
        w_raw += [qt[:, i, :, :].rearrange("p h t -> p (h t)") for i in range(2)]
        RAW = len(w_raw)
        v_out = sb("v_out", [P, 2, SB_WIDTH])
        u_out = sb("u_out", [P, 2, ROWS])

        acc = [ps(f"acc{i}", [P, BANK]) for i in range(4)]
        th_ps = ps("th_ps", [P, KC, P])
        tq_ps = ps("tq_ps", [P, HEADS, P])

        ident_ready = sem("ident_ready")
        rows_in = sem("rows_in")
        w_loaded = [sem(f"w_loaded{i}") for i in range(RAW)]
        w_split = sem("w_split")
        x_loaded = [sem(f"x_loaded{j}") for j in range(2)]
        dve_chain = sem("dve_chain")
        w_hi_ready = sem("w_hi_ready")
        squared = Tally(sem("squared"), 2)
        normed = Tally(sem("normed"), 2)
        h_turned = Tally(sem("h_turned"), 2)
        h_hi = Tally(sem("h_hi"), 2)
        h_lo = Tally(sem("h_lo"), 2)
        product = Tally(sem("product"), 10)
        qk_squared = Tally(sem("qk_squared"), 4)
        qk_normed = Tally(sem("qk_normed"), 4)
        qk_gained = Tally(sem("qk_gained"), 4)
        qk_hi = Tally(sem("qk_hi"), 4)
        qk_lo = Tally(sem("qk_lo"), 4)
        qk_turned = Tally(sem("qk_turned"), 4)
        qk_out = Tally(sem("qk_out"), 4)
        copied = Tally(sem("copied"), 6)
        qk_stored = [Tally(sem(f"qk_stored{i}"), 2 * DMA) for i in range(2)]
        v_stored = [Tally(sem(f"v_stored{i}"), DMA) for i in range(2)]
        u_stored = [Tally(sem(f"u_stored{i}"), 2 * DMA) for i in range(2)]
        ACT_TALLIES = [squared, h_hi, qk_squared, qk_hi, copied, qk_out]
        DVE_TALLIES = [normed, h_lo, qk_normed]
        POOL_TALLIES = [qk_gained, qk_lo]
        PE_TALLIES = [h_turned, product, qk_turned]
        SYNC_TALLIES = qk_stored + v_stored + u_stored

        block = ctx.enter_context(nc.Block())

        W_PIECES = 16

        def steps(eng, body):
            with eng.Fori(0, STEPS - 2, 2) as c:
                body(c, 0, True)
                body(c + 1, 1, True)
            body(STEPS - 2, 0, True)
            body(STEPS - 1, 1, False)

        @block.sync
        def _(sp):
            for tally in SYNC_TALLIES:
                tally.start(sp)

            def load_x(c):
                for j in range(2):
                    sp.wait_ge(h_turned.sem, h_turned.at(c - 1, j + 1))
                    sp.dma_start(xt[:, j, :], x[c * ROWS + j * P:c * ROWS + (j + 1) * P, :]).then_inc(x_loaded[j], DMA)

            load_x(0)
            sp.dma_start(g_row[:, :], g_mix.partition_broadcast(P)).then_inc(rows_in, DMA)
            sp.dma_start(gq_row[:, 0, :], g_q.partition_broadcast(P)).then_inc(rows_in, DMA)
            sp.dma_start(gq_row[:, 1, :], g_k.partition_broadcast(P)).then_inc(rows_in, DMA)
            for n in range(W_PIECES):
                k, cols = W_PIECE(n)
                if n >= RAW:
                    sp.wait_ge(w_split, n - RAW + 1)
                sp.dma_start(w_raw[n % RAW].rearrange("p (k f) -> p k f", k=2),
                             w_in[k * P:(k + 2) * P, cols].rearrange("(k p) f -> p k f", p=P)
                             ).then_inc(w_loaded[n % RAW], DMA)

            def body(c, b, more):
                if more:
                    load_x(c + 1)
                for j in range(2):
                    row = c * ROWS + j * P
                    for n, dst in ((2 * j, q_dram), (2 * j + 1, k_dram)):
                        sp.wait_ge(qk_out.sem, qk_out.at(c, n + 1))
                        sp.dma_start(dst[:, :, row:row + P].rearrange("h d t -> d h t"),
                                     qt[:, n % 2, :, :]).then_inc(qk_stored[n % 2].sem, DMA)
                    sp.wait_ge(copied.sem, copied.at(c, j + 1))
                    sp.dma_start(v_dram[row:row + P, :], v_out[:, j, :]).then_inc(v_stored[j].sem, DMA)
                for f in range(4):
                    sp.wait_ge(copied.sem, copied.at(c, 3 + f))
                    n_here = ROWS // SUB
                    sp.dma_start(u_dram[f * P:(f + 1) * P, :, c * n_here:(c + 1) * n_here],
                                 u_out[:, f % 2, :].rearrange("p (l n) -> p l n", l=SUB)
                                 ).then_inc(u_stored[f % 2].sem, DMA)

            for c in range(STEPS):
                body(c, c % 2, c < STEPS - 1)
            for tally in SYNC_TALLIES:
                sp.wait_ge(tally.sem, tally.at(STEPS - 1, tally.per))

        @block.gpsimd
        def _(pool):
            for tally in POOL_TALLIES:
                tally.start(pool)
            fill_identity(pool, ident[:, :], ident_ready)
            pool.wait_ge(rows_in, 3 * DMA)

            def body(c, b, more):
                for j in range(2):
                    for n in (2 * j, 2 * j + 1):
                        pool.wait_ge(qk_normed.sem, qk_normed.at(c, n + 1))
                        view = qn[:, n % 2, :].rearrange("p (h d) -> p h d", h=HEADS)
                        gain = gq_row[:, n % 2, None, :].to_broadcast([P, HEADS, HEAD])
                        pool.tensor_tensor(view, view, gain, ALU.mult).then_inc(qk_gained.sem, 1)
                    for n in (2 * j, 2 * j + 1):
                        pool.wait_ge(qk_hi.sem, qk_hi.at(c, n + 1))
                        pool.tensor_tensor(qs[:, n % 2, :, 1, :], qn[:, n % 2, :].rearrange("p (h d) -> p h d", h=HEADS),
                                           qs[:, n % 2, :, 0, :], ALU.subtract).then_inc(qk_lo.sem, 1)

            steps(pool, body)

        @block.scalar
        def _(act):
            for tally in ACT_TALLIES:
                tally.start(act)

            def square_x(c, j, count):
                act.wait_ge(x_loaded[j], count)
                act.wait_ge(normed.sem, normed.at(c - 1, 2))
                act.wait_ge(squared.sem, squared.at(c, j))
                act.wait_ge(qk_normed.sem, qk_normed.at(c - 2, 4))
                act.activation(sq[:, :, :].rearrange("p a n -> p (a n)"), xt[:, j, :], ACT.Square,
                               accum_out=xstat[:, 0, j:j + 1]).then_inc(squared.sem, 1)

            def high_of_h(c, j, b):
                act.wait_ge(h_turned.sem, h_turned.at(c, j + 1))
                act.wait_ge(product.sem, product.at(c - 2, 10))
                act.activation(ht_hi[b][:, :, j * P:(j + 1) * P], th_ps[:, :, :], ACT.Copy).then_inc(h_hi.sem, 1)

            square_x(0, 0, DMA)
            square_x(0, 1, DMA)
            for n in range(W_PIECES):
                act.wait_ge(w_loaded[n % RAW], DMA * (n // RAW + 1))
                k, cols = W_PIECE(n)
                act.activation(w_hi[:, k:k + 2, cols], w_raw[n % RAW].rearrange("p (k f) -> p k f", k=2),
                               ACT.Copy).then_inc(w_hi_ready, 1)
                if n == 3:
                    high_of_h(0, 0, 0)
                if n == 5:
                    high_of_h(0, 1, 0)

            def square_qk(c, n):
                act.wait_ge(product.sem, product.at(c, (1, 2, 4, 5)[n]))
                if more_steps:
                    act.wait_ge(squared.sem, squared.at(c + 1, 2))
                act.wait_ge(qk_normed.sem, qk_normed.at(c - 1, 4) if n < 2 else qk_normed.at(c, 2))
                act.activation(sq[:, n % 2, :], acc[ACC(c_par, (0, 1, 3, 4)[n])][:, :], ACT.Square
                               ).then_inc(qk_squared.sem, 1)

            def high_qk(c, n):
                act.wait_ge(qk_gained.sem, qk_gained.at(c, n + 1))
                act.wait_ge(qk_turned.sem, qk_turned.at(c - 1, n + 3) if n < 2 else qk_turned.at(c, n - 1))
                act.activation(qs[:, n % 2, :, 0, :].bitcast(F32R), qn[:, n % 2, :].rearrange("p (h d) -> p h d", h=HEADS),
                               ACT.Copy).then_inc(qk_hi.sem, 1)

            def copy_v(c, j):
                act.wait_ge(product.sem, product.at(c, 3 * j + 3))
                act.wait_ge(v_stored[j].sem, v_stored[j].at(c - 1, DMA))
                act.activation(v_out[:, j, :], acc[ACC(c_par, 3 * j + 2)][:, :], ACT.Copy).then_inc(copied.sem, 1)

            def copy_u(c, f):
                act.wait_ge(product.sem, product.at(c, 7 + f))
                act.wait_ge(u_stored[f % 2].sem, u_stored[f % 2].at(c - 1 + f // 2, DMA * (2 - f // 2)))
                act.activation(u_out[:, f % 2, :].rearrange("p (l n) -> p n l", l=SUB),
                               acc[ACC(c_par, 6 + f)][:, 0:ROWS].rearrange("p (n l) -> p n l", l=SUB),
                               ACT.Copy).then_inc(copied.sem, 1)

            def out_qk(c, n):
                act.wait_ge(qk_turned.sem, qk_turned.at(c, n + 1))
                act.wait_ge(qk_stored[n % 2].sem, qk_stored[n % 2].at(c - 1 + n // 2, DMA * (2 - n // 2)))
                act.activation(qt[:, n % 2, :, :], tq_ps[:, :, :], ACT.Copy).then_inc(qk_out.sem, 1)

            def body(c, b, more):
                nonlocal c_par, more_steps
                c_par, more_steps = b, more
                if more:
                    square_x(c + 1, 0, c * DMA + 2 * DMA)
                    square_x(c + 1, 1, c * DMA + 2 * DMA)
                square_qk(c, 0)
                square_qk(c, 1)
                copy_v(c, 0)
                if more:
                    high_of_h(c + 1, 0, 1 - b)
                high_qk(c, 0)
                high_qk(c, 1)
                square_qk(c, 2)
                out_qk(c, 0)
                out_qk(c, 1)
                square_qk(c, 3)
                copy_v(c, 1)
                if more:
                    high_of_h(c + 1, 1, 1 - b)
                copy_u(c, 0)
                high_qk(c, 2)
                high_qk(c, 3)
                copy_u(c, 1)
                out_qk(c, 2)
                out_qk(c, 3)
                copy_u(c, 2)
                copy_u(c, 3)

            c_par, more_steps = 0, True
            steps(act, body)

        @block.vector
        def _(dve):
            for tally in DVE_TALLIES:
                tally.start(dve)
            link = Chain(dve, dve_chain)

            def stats_x(c):
                dve.wait_ge(squared.sem, squared.at(c, 2))
                rsqrt_mean(dve, link, xstat[:, 0, :], D_MODEL, xstat[:, 1, :], xstat[:, 2, :], xstat[:, 3, :])

            def norm_x(c, j):
                dve.scalar_tensor_tensor(xt[:, j, :], xt[:, j, :], xstat[:, 2, j:j + 1], g_row[:, :],
                                         ALU.mult, ALU.mult).then_inc(normed.sem, 1)

            def low_of_h(c, j, b):
                dve.wait_ge(h_hi.sem, h_hi.at(c, j + 1))
                dve.tensor_tensor(ht_lo[b][:, :, j * P:(j + 1) * P], th_ps[:, :, :],
                                  ht_hi[b][:, :, j * P:(j + 1) * P].bitcast(F32), ALU.subtract).then_inc(h_lo.sem, 1)

            dve.wait_ge(rows_in, 3 * DMA)
            stats_x(0)
            norm_x(0, 0)
            for n in range(W_PIECES):
                dve.wait_ge(w_hi_ready, n + 1)
                k, cols = W_PIECE(n)
                dve.tensor_tensor(w_lo[:, k:k + 2, cols], w_raw[n % RAW].rearrange("p (k f) -> p k f", k=2),
                                  w_hi[:, k:k + 2, cols].bitcast(F32),
                                  ALU.subtract).then_inc(w_split, 1)
                if n == 3:
                    low_of_h(0, 0, 0)
                    norm_x(0, 1)
                if n == 5:
                    low_of_h(0, 1, 0)

            def norm_qk(c, j):
                for n in (2 * j, 2 * j + 1):
                    dve.wait_ge(qk_squared.sem, qk_squared.at(c, n + 1))
                    link(dve.tensor_reduce(qstat[:, 0, (n % 2) * HEADS:(n % 2 + 1) * HEADS],
                                           sq[:, n % 2, :].rearrange("p (h d) -> p h d", h=HEADS), AX_X, ALU.add))
                rsqrt_mean(dve, link, qstat[:, 0, :], HEAD, qstat[:, 1, :], qstat[:, 2, :], qstat[:, 3, :])
                for n in (2 * j, 2 * j + 1):
                    dve.wait_ge(qk_lo.sem, qk_lo.at(c - 1, n + 3) if n < 2 else qk_lo.at(c, n - 1))
                    scale = qstat[:, 2, (n % 2) * HEADS:(n % 2 + 1) * HEADS]
                    dve.tensor_tensor(qn[:, n % 2, :].rearrange("p (h d) -> p h d", h=HEADS),
                                      acc[ACC(c_par, (0, 1, 3, 4)[n])][:, :].rearrange("p (h d) -> p h d", h=HEADS),
                                      scale[:, :, None].to_broadcast([P, HEADS, HEAD]), ALU.mult
                                      ).then_inc(qk_normed.sem, 1)

            LINKS = RSQRT_LINKS + 2 * (2 + RSQRT_LINKS)

            def body(c, b, more):
                nonlocal c_par
                c_par = b
                link.begin(c * LINKS + RSQRT_LINKS)
                if more:
                    stats_x(c + 1)
                    norm_x(c + 1, 0)
                norm_qk(c, 0)
                if more:
                    low_of_h(c + 1, 0, 1 - b)
                    norm_x(c + 1, 1)
                norm_qk(c, 1)
                if more:
                    low_of_h(c + 1, 1, 1 - b)
                assert link.n == LINKS or not more

            c_par = 0
            steps(dve, body)

        @block.tensor
        def _(pe):
            for tally in PE_TALLIES:
                tally.start(pe)
            pe.wait_ge(ident_ready, 2)

            def turn_h(c, j):
                pe.wait_ge(normed.sem, normed.at(c, j + 1))
                pe.wait_ge(h_lo.sem, h_lo.at(c - 1, 2) if j == 0 else h_lo.at(c, 1))
                for k in range(KC):
                    mm = pe.transpose(th_ps[:, k, :], xt[:, j, k * P:(k + 1) * P], ident[:, :])
                mm.then_inc(h_turned.sem, 1)

            def turn_qk(c, n):
                pe.wait_ge(qk_lo.sem, qk_lo.at(c, n + 1))
                pe.wait_ge(qk_out.sem, qk_out.at(c - 1, 4) if n == 0 else qk_out.at(c, n))
                for h in range(HEADS):
                    mm = pe.transpose(tq_ps[:, h, :], qs[:, n % 2, h, :, :].rearrange("p s d -> p (s d)"), ident[:, :])
                mm.then_inc(qk_turned.sem, 1)

            def await_bank(c, n):
                prev, cc = n - 4, c
                if prev < 0:
                    prev, cc = prev + 10, c - 1
                if prev in (0, 1, 3, 4):
                    pe.wait_ge(qk_normed.sem, qk_normed.at(cc, (0, 1, 3, 4).index(prev) + 1))
                else:
                    pe.wait_ge(copied.sem, copied.at(cc, (2, 5, 6, 7, 8, 9).index(prev) + 1))

            def rows_product(c, b, n):
                j, kind = n // 3, n % 3
                await_bank(c, n)
                pe.wait_ge(w_split, 4 * (kind + 1))
                cols = slice(SSM_WIDTH * (kind + 1), SSM_WIDTH * (kind + 2))
                rows = slice(j * P, (j + 1) * P)
                out = acc[ACC(b, n)][:, :]
                for k in range(KC):
                    pe.matmul(out, ht_hi[b][:, k, rows], w_hi[:, k, cols], start=(k == 0), stop=False)
                    pe.matmul(out, ht_hi[b][:, k, rows], w_lo[:, k, cols], start=False, stop=False)
                    mm = pe.matmul(out, ht_lo[b][:, k, rows], w_hi[:, k, cols], start=False, stop=(k == KC - 1))
                mm.then_inc(product.sem, 1)

            def feature_product(c, b, f):
                await_bank(c, 6 + f)
                pe.wait_ge(w_split, W_PIECES)
                cols = slice(f * P, (f + 1) * P)
                out = acc[ACC(b, 6 + f)][:, 0:ROWS]
                for k in range(KC):
                    pe.matmul(out, w_hi[:, k, cols], ht_hi[b][:, k, :], start=(k == 0), stop=False)
                    pe.matmul(out, w_hi[:, k, cols], ht_lo[b][:, k, :], start=False, stop=False)
                    mm = pe.matmul(out, w_lo[:, k, cols], ht_hi[b][:, k, :], start=False, stop=(k == KC - 1))
                mm.then_inc(product.sem, 1)

            turn_h(0, 0)
            turn_h(0, 1)

            def body(c, b, more):
                pe.wait_ge(h_hi.sem, h_hi.at(c, 2))
                pe.wait_ge(h_lo.sem, h_lo.at(c, 2))
                rows_product(c, b, 0)
                rows_product(c, b, 1)
                rows_product(c, b, 2)
                if more:
                    turn_h(c + 1, 0)
                rows_product(c, b, 3)
                turn_qk(c, 0)
                turn_qk(c, 1)
                rows_product(c, b, 4)
                rows_product(c, b, 5)
                if more:
                    turn_h(c + 1, 1)
                feature_product(c, b, 0)
                feature_product(c, b, 1)
                turn_qk(c, 2)
                turn_qk(c, 3)
                feature_product(c, b, 2)
                feature_product(c, b, 3)

            steps(pe, body)


def W_PIECE(n):
    part = (n // 4 + 1) % 4
    return 2 * (n % 4), slice(part * 512, (part + 1) * 512)


def ACC(parity, n):
    return (10 * parity + n) % 4


def attention_units():
    units = []
    for i in range(SEQ // P):
        tiles = i + 1
        if tiles <= 8:
            units.append((i, 0, tiles * P, True, True))
        else:
            cut = tiles // 2
            units.append((i, cut * P, tiles * P, True, False))
            units.append((i, 0, cut * P, False, True))
    return units


def stick_breaking(nc, q_dram, k_dram, v_dram, y_dram):
    UNITS = attention_units()
    NU = len(UNITS)
    SLOTS = [(a, *u) for a in range(2) for u in UNITS]
    N = len(SLOTS)
    STEPS = HEADS // 2
    BLOCKS = SEQ // P
    SCALE = HEAD ** -0.5
    WIDE = 1024
    with ExitStack() as ctx:
        def sb(name, shape, dt=F32):
            return ctx.enter_context(nc.sbuf_tensor("a_" + name, shape, dt))

        sem = ctx.enter_context(semaphores(nc, "a_"))

        q2 = [sb(f"q2_{a}", [P, SEQ], F32R) for a in range(2)]
        k2_hi = [sb(f"k2_hi{a}", [P, SEQ], F32R) for a in range(2)]
        k2_lo = [sb(f"k2_lo{a}", [P, SEQ], F32R) for a in range(2)]
        v = [sb(f"v{a}", [P, BLOCKS, HEAD]) for a in range(2)]
        y = [sb(f"y{a}", [P, BLOCKS, HEAD]) for a in range(2)]
        off = [sb(f"off{b}", [P, WIDE]) for b in range(3)]
        on = [sb(f"on{b}", [P, WIDE]) for b in range(3)]
        left = [sb(f"left{b}", [P, SEQ + 1]) for b in range(2)]
        w = [sb(f"w{b}", [P, WIDE]) for b in range(3)]
        wt = [sb(f"wt{b}", [P, WIDE // P, P]) for b in range(3)]
        ident = sb("ident", [P, P])
        ident16 = sb("ident16", [P, P], BF16)
        never16 = sb("never16", [P, P], BF16)
        z_ps = [ctx.enter_context(nc.psum_tensor(f"a_ps_z{b}", [P, WIDE], F32)) for b in range(2)]
        wt_ps = [ctx.enter_context(nc.psum_tensor(f"a_ps_wt{b}", [P, BANK], F32)) for b in range(2)]
        y_ps = [ctx.enter_context(nc.psum_tensor(f"a_ps_y{b}", [P, BANK], F32)) for b in range(2)]

        constants = sem("constants")
        ones_ready = sem("ones_ready")
        head_loaded = [Tally(sem(f"head_loaded{a}"), 6 * DMA, 0) for a in range(2)]
        head_stored = [Tally(sem(f"head_stored{a}"), DMA, 1) for a in range(2)]
        scored = Tally(sem("scored"), N, 1)
        sig_off = Tally(sem("sig_off"), N, 1)
        sig_on = Tally(sem("sig_on"), N, 1)
        scanned = Tally(sem("scanned"), N, 1)
        by_pool = [m % 3 == 2 for m in range(N)]
        n_pool = sum(by_pool)
        weighed = Tally(sem("weighed"), N - n_pool, 1)
        weighed_p = Tally(sem("weighed_p"), n_pool, 1)
        groups = [(m, t0, min(4, (s[3] - s[2]) // P - t0)) for m, s in enumerate(SLOTS)
                  for t0 in range(0, (s[3] - s[2]) // P, 4)]
        first_group = [next(i for i, g in enumerate(groups) if g[0] == m) for m in range(N)] + [len(groups)]
        by_act = [g[1] > 0 or g[0] % 3 == 0 for g in groups]
        turned = Tally(sem("turned"), len(groups), 1)
        copied_a = Tally(sem("copied_a"), sum(by_act), 1)
        copied_d = Tally(sem("copied_d"), len(groups) - sum(by_act), 1)
        gathered = Tally(sem("gathered"), N, 1)
        y_copied = Tally(sem("y_copied"), 2 * BLOCKS, 1)
        blocks_before = [sum(1 for s in SLOTS[:m] if s[5]) for m in range(N + 1)]

        blocks_of = [a * BLOCKS + i for a, i, *_ in SLOTS]

        block = ctx.enter_context(nc.Block())

        def wait_weighed(eng, s, m):
            p = sum(by_pool[:m + 1]) if m >= -1 else -sum(by_pool[m + 1:])
            eng.wait_ge(weighed_p.sem, weighed_p.at(s, p))
            eng.wait_ge(weighed.sem, weighed.at(s, m + 1 - p))

        def wait_copied(eng, s, g):
            p = sum(by_act[:g + 1]) if g >= -1 else -sum(by_act[g + 1:])
            eng.wait_ge(copied_a.sem, copied_a.at(s, p))
            eng.wait_ge(copied_d.sem, copied_d.at(s, g + 1 - p))

        def weigh(eng, s, m, tally):
            a, i, k0, k1, first, last = SLOTS[m]
            at = SEQ - (i + 1) * P
            eng.wait_ge(scanned.sem, scanned.at(s, m + 1))
            eng.wait_ge(sig_on.sem, sig_on.at(s, m + 1))
            eng.wait_ge(turned.sem, turned.at(s, first_group[m - 2] if m >= 2 else first_group[N + m - 2] - len(groups)))
            eng.tensor_tensor(w[m % 3][:, 0:k1 - k0], on[m % 3][:, 0:k1 - k0],
                              left[i % 2][:, at + k0 + 1:at + k1 + 1], ALU.mult).then_inc(tally.sem, 1)

        @block.sync
        def _(sp):
            for tally in head_stored:
                tally.start(sp)

            def load(s, a):
                h = 2 * s + a
                if s > 0:
                    sp.wait_ge(gathered.sem, gathered.at(s - 1, NU * (a + 1)))
                for dst, src in ((q2[a][:, :], q_dram[h]),
                                 (v[a][:, :, :], v_dram[:, h * HEAD:(h + 1) * HEAD].rearrange("(i p) d -> p i d", p=P))):
                    sp.dma_start(dst.bitcast(F32), src).then_inc(head_loaded[a].sem, DMA)
                for dst, part in ((k2_hi[a], 0), (k2_lo[a], 1)):
                    for copy in range(2):
                        sp.dma_start(dst[copy * HEAD:(copy + 1) * HEAD, :].bitcast(F32),
                                     k_dram[h, part * HEAD:(part + 1) * HEAD, :]).then_inc(head_loaded[a].sem, DMA)

            load(0, 0)
            load(0, 1)
            for s in range(STEPS):
                for a in range(2):
                    if s + 1 < STEPS:
                        load(s + 1, a)
                    sp.wait_ge(y_copied.sem, y_copied.at(s, BLOCKS * (a + 1)))
                    h = 2 * s + a
                    sp.dma_start(y_dram[:, h * HEAD:(h + 1) * HEAD].rearrange("(i p) d -> p i d", p=P),
                                 y[a][:, :, :]).then_inc(head_stored[a].sem, DMA)
            for tally in head_stored:
                sp.wait_ge(tally.sem, tally.at(STEPS - 1, DMA))

        @block.gpsimd
        def _(pool):
            weighed_p.start(pool)
            fill_identity(pool, ident[:, :], constants)
            pool.wait_ge(constants, 2)
            pool.tensor_copy(ident16[:, :], ident[:, :]).then_inc(constants, 1)
            pool.memset(never16[:, :], 0.0).then_inc(constants, 1)
            pool.wait_ge(constants, 4)
            pool.affine_select(out=never16[:, :], in_=never16[:, :], compare_op=ALU.is_gt, fill=-1e30, base=0,
                               pattern=[[-1, P]], channel_multiplier=1).then_inc(constants, 1)

            with pool.Fori(0, STEPS) as s:
                for m, (a, i, k0, k1, first, last) in enumerate(SLOTS):
                    if by_pool[m]:
                        weigh(pool, s, m, weighed_p)

        @block.scalar
        def _(act):
            sig_off.start(act)
            sig_on.start(act)
            copied_a.start(act)

            def sigmoids(s, m):
                a, i, k0, k1, first, last = SLOTS[m]
                act.wait_ge(scored.sem, scored.at(s, m + 1))
                act.wait_ge(scanned.sem, scanned.at(s, m - 2))
                act.activation(off[m % 3][:, 0:k1 - k0], z_ps[m % 2][:, 0:k1 - k0], ACT.Sigmoid,
                               scale=-SCALE).then_inc(sig_off.sem, 1)
                wait_weighed(act, s, m - 3)
                act.activation(on[m % 3][:, 0:k1 - k0], z_ps[m % 2][:, 0:k1 - k0], ACT.Sigmoid,
                               scale=SCALE).then_inc(sig_on.sem, 1)

            def copies(s, m):
                for g in range(first_group[m], first_group[m + 1]):
                    if by_act[g]:
                        _, t0, n = groups[g]
                        act.wait_ge(turned.sem, turned.at(s, g + 1))
                        act.wait_ge(gathered.sem, gathered.at(s, m - 2))
                        act.activation(wt[m % 3][:, t0:t0 + n, :], wt_ps[g % 2][:, 0:n * P].rearrange("p (t q) -> p t q", q=P),
                                       ACT.Copy).then_inc(copied_a.sem, 1)

            with act.Fori(0, STEPS) as s:
                for m in range(N + 2):
                    if m < N:
                        sigmoids(s, m)
                    if m >= 2:
                        copies(s, m - 2)

        @block.vector
        def _(dve):
            scanned.start(dve)
            weighed.start(dve)
            copied_d.start(dve)
            y_copied.start(dve)
            for b in range(2):
                dve.memset(left[b][:, SEQ:SEQ + 1], 1.0).then_inc(ones_ready, 1)
            dve.wait_ge(ones_ready, 2)

            def scan(s, m):
                a, i, k0, k1, first, last = SLOTS[m]
                at = SEQ - (i + 1) * P
                dve.wait_ge(sig_off.sem, sig_off.at(s, m + 1))
                readers = [n for n in range(m) if blocks_of[n] == blocks_of[m] - 2]
                wait_weighed(dve, s, readers[-1] if readers else -1)
                dve.wait_ge(scanned.sem, scanned.at(s, m))
                old = off[m % 3][:, 0:k1 - k0]
                dve.tensor_tensor_scan(left[i % 2][:, at + k0:at + k1][:, ::-1], old[:, ::-1], old[:, ::-1],
                                       1.0 if first else left[i % 2][:, at + k1:at + k1 + 1],
                                       ALU.mult, ALU.bypass).then_inc(scanned.sem, 1)

            def copies(s, m):
                for g in range(first_group[m], first_group[m + 1]):
                    if not by_act[g]:
                        _, t0, n = groups[g]
                        dve.wait_ge(turned.sem, turned.at(s, g + 1))
                        dve.wait_ge(gathered.sem, gathered.at(s, m - 2))
                        dve.tensor_copy(wt[m % 3][:, t0:t0 + n, :],
                                        wt_ps[g % 2][:, 0:n * P].rearrange("p (t q) -> p t q", q=P)
                                        ).then_inc(copied_d.sem, 1)

            def copy_y(s, m):
                a, i, k0, k1, first, last = SLOTS[m]
                if last:
                    dve.wait_ge(gathered.sem, gathered.at(s, m + 1))
                    if i == 0:
                        dve.wait_ge(head_stored[a].sem, head_stored[a].at(s - 1, DMA))
                    dve.tensor_copy(y[a][:, i, :], y_ps[i % 2][:, 0:HEAD]).then_inc(y_copied.sem, 1)

            with dve.Fori(0, STEPS) as s:
                for m in range(N + 4):
                    if m < N:
                        scan(s, m)
                    if 1 <= m <= N and not by_pool[m - 1]:
                        weigh(dve, s, m - 1, weighed)
                    if 2 <= m < N + 2:
                        copies(s, m - 2)
                    if m >= 4:
                        copy_y(s, m - 4)

        @block.tensor
        def _(pe):
            for tally in (scored, turned, gathered):
                tally.start(pe)
            pe.wait_ge(constants, 5)

            def score(s, m):
                a, i, k0, k1, first, last = SLOTS[m]
                if i == 0:
                    pe.wait_ge(head_loaded[a].sem, head_loaded[a].at(s, 6 * DMA))
                pe.wait_ge(sig_on.sem, sig_on.at(s, m - 1))
                for c0 in range(k0, k1, BANK):
                    c1 = min(c0 + BANK, k1)
                    out = z_ps[m % 2][:, c0 - k0:c1 - k0]
                    diagonal = first and c1 == k1
                    pe.matmul(out, q2[a][:, i * P:(i + 1) * P], k2_hi[a][:, c0:c1], start=True, stop=False)
                    mm = pe.matmul(out, q2[a][:, i * P:(i + 1) * P], k2_lo[a][:, c0:c1], start=False, stop=not diagonal)
                    if diagonal:
                        mm = pe.matmul(z_ps[m % 2][:, k1 - P - k0:k1 - k0], ident16[:, :], never16[:, :],
                                       start=False, stop=True)
                mm.then_inc(scored.sem, 1)

            def turn(s, m):
                wait_weighed(pe, s, m)
                for g in range(first_group[m], first_group[m + 1]):
                    _, t0, n = groups[g]
                    wait_copied(pe, s, g - 2)
                    for t in range(n):
                        mm = pe.transpose(wt_ps[g % 2][:, t * P:(t + 1) * P], w[m % 3][:, (t0 + t) * P:(t0 + t + 1) * P],
                                          ident[:, :])
                    mm.then_inc(turned.sem, 1)

            def gather(s, m):
                a, i, k0, k1, first, last = SLOTS[m]
                wait_copied(pe, s, first_group[m + 1] - 1)
                pe.wait_ge(y_copied.sem, y_copied.at(s, blocks_before[m] - 1))
                for t in range((k1 - k0) // P):
                    mm = pe.matmul(y_ps[i % 2][:, 0:HEAD], wt[m % 3][:, t, :], v[a][:, k0 // P + t, :],
                                   start=(first and t == 0), stop=(last and t == (k1 - k0) // P - 1))
                mm.then_inc(gathered.sem, 1)

            with pe.Fori(0, STEPS) as s:
                score(s, 0)
                score(s, 1)
                for m in range(N + 3):
                    if m + 2 < N:
                        score(s, m + 2)
                    if m >= 3:
                        gather(s, m - 3)
                    if 1 <= m <= N:
                        turn(s, m - 1)


def ssm_scan(nc, a_re, a_im, log_dt, b_re, b_im, c_re, c_im, u_dram, y_dram):
    PC = SSM_STATE
    G = SSM_GROUPS
    C = SSM_GROUP
    LEVELS = int(math.log2(CHUNKS))
    with ExitStack() as ctx:
        def sb(name, shape, dt=F32):
            return ctx.enter_context(nc.sbuf_tensor("s_" + name, shape, dt))

        def ps(name, shape):
            return ctx.enter_context(nc.psum_tensor("s_ps_" + name, shape, F32))

        sem = ctx.enter_context(semaphores(nc, "s_"))

        ident = sb("ident", [P, P])
        swap = sb("swap", [P, P])
        a_rows = sb("a_rows", [G, 2, 2, PC])
        lam = sb("lam", [P, 2, G])
        dt = sb("dt", [P, G])
        num = sb("num", [P, 16, G])
        sgn = sb("sgn", [P, 1])
        abar = sb("abar", [P, 2, G])
        coef = sb("coef", [P, 2, G])
        pw = sb("pw", [P, SUB + 1, 2, G])
        dbl = sb("dbl", [P, LEVELS, 2, G])
        b_in = sb("b_in", [P, 2, G, C])
        bb = sb("bb", [P, 2, G, C])
        c_rows = sb("c_rows", [P, 4, 3, PC])
        cc = sb("cc", [P, 2, G * C])
        t_in = sb("t_in", [P, G, SUB, C])
        mat_out = sb("mat_out", [P, G, SUB + 1, C])
        mat_in = sb("mat_in", [P, G, P])
        kern = sb("kern", [C, G, P])
        mat_within = sb("mat_within", [P, G, P])
        scratch = sb("scratch", [P, G, C])
        pool_scratch = [sb(f"pool_scratch{i}", [P, G, C]) for i in range(2)]
        cross = scratch[:, :, :].rearrange("p g c -> p (g c)").rearrange("p (n a g) -> p n a g", a=2, g=G)
        scratch2 = sb("scratch2", [P, G, C])

        u = sb("u", [P, G, CHUNKS])
        a_mat = [sb(f"a_mat{b}", [P, 2, LEVELS, P]) for b in range(4)]
        turned_part = sb("turned_part", [P, LEVELS, P])
        plain_part = [sb(f"plain_part{b}", [P, LEVELS, P]) for b in range(2)]
        s = [sb(f"s{b}", [P, 2, CHUNKS]) for b in range(4)]
        y = [sb(f"y{b}", [P, 2, CHUNKS]) for b in range(2)]
        bank = [ps(f"bank{i}", [P, BANK]) for i in range(8)]

        consts = sem("consts")
        params_in = sem("params_in")
        u_in = sem("u_in")
        dve_link = sem("dve_link")
        params_turned = sem("params_turned")
        params_read = sem("params_read")
        angles = sem("angles")
        sines = sem("sines")
        powers = sem("powers")
        in_rows = sem("in_rows")
        out_rows = sem("out_rows")
        out_rows_p = sem("out_rows_p")
        in_turned = sem("in_turned")
        in_copied = sem("in_copied")
        kern_made = sem("kern_made")
        kern_copied = sem("kern_copied")
        cleared = sem("cleared")
        within_in = sem("within_in")
        PAIRS = G // 2
        plain_ready = sem("plain_ready")
        turned_ready = sem("turned_ready")
        a_ready = sem("a_ready")
        v_made = sem("v_made")
        term_made = [sem(f"term_made{i}") for i in range(2)]
        s_ready = [sem(f"s_ready{i}") for i in range(2)]
        y_made = sem("y_made")
        y_copied = sem("y_copied")
        y_stored = [sem(f"y_stored{i}") for i in range(2)]
        STEP = LEVELS + 1
        POOL_POWERS = range(SUB // 2 + 1, SUB + 1)

        block = ctx.enter_context(nc.Block())

        @block.sync
        def _(sp):
            for part, src in ((0, a_re), (1, a_im)):
                for copy in range(2):
                    sp.dma_start(a_rows[:, part, copy, :], src).then_inc(params_in, DMA)
            sp.dma_start(dt[:, :], log_dt.partition_broadcast(P)).then_inc(params_in, DMA)
            for h, parts in ((0, (b_re, b_im)), (1, (b_im, b_re))):
                for x in range(2):
                    sp.dma_start(b_in[h * PC:(h + 1) * PC, x, :, :], parts[x].rearrange("g p c -> p g c")
                                 ).then_inc(params_in, DMA)
            for part, src in enumerate((c_re, c_im, c_re)):
                sp.dma_start(c_rows[:, :, part, :], src.rearrange("(s g) c p -> (g c) s p", s=4)).then_inc(params_in, DMA)
            for slab in range(4):
                for l in range(SUB):
                    sp.dma_start(u[l * C:(l + 1) * C, slab * 8:(slab + 1) * 8, :],
                                 u_dram[slab * P:(slab + 1) * P, l, :].rearrange("(g c) n -> c g n", c=C)
                                 ).then_inc(u_in, DMA)
            sp.wait_ge(kern_copied, G // 4)
            sp.wait_ge(cleared, 1)
            for l in range(SUB):
                sp.dma_start(mat_within[l * C:(l + 1) * C, :, l * C:], kern[:, :, 0:P - l * C]).then_inc(within_in, DMA)
            for p in range(PAIRS):
                sp.wait_ge(y_copied, p + 1)
                for i in range(2):
                    g = 2 * p + i
                    sp.dma_start(y_dram[g * C:(g + 1) * C, :, :].rearrange("c l n -> l c n"), y[p % 2][:, i, :]
                                 ).then_inc(y_stored[p % 2], DMA)
            for b in range(2):
                sp.wait_ge(y_stored[b], PAIRS * DMA)

        @block.gpsimd
        def _(pool):
            fill_identity(pool, ident[:, :], consts)
            pool.wait_ge(consts, 2)
            pool.tensor_copy(swap[:, 0:PC], ident[:, PC:P]).then_inc(consts, 1)
            pool.tensor_copy(swap[:, PC:P], ident[:, 0:PC]).then_inc(consts, 1)
            pool.memset(sgn[:, :], 1.0).then_inc(consts, 1)
            pool.wait_ge(consts, 5)
            pool.memset(sgn[0:PC, :], -1.0).then_inc(consts, 1)
            pool.memset(mat_within[:, :, :], 0.0).then_inc(cleared, 1)
            pool.wait_ge(powers, 1)
            pool.wait_ge(consts, 6)

            def make_out_rows():
                c_of = [cc[:, x, :].rearrange("p (g c) -> p g c", c=C) for x in range(2)]
                for n, m in enumerate(POOL_POWERS):
                    if n:
                        pool.wait_ge(out_rows_p, 3 * n)
                    for x in range(2):
                        pool.tensor_tensor(pool_scratch[x][:, :, :], c_of[x], pw[:, m, x, :, None].to_broadcast([P, G, C]),
                                           ALU.mult).then_inc(out_rows_p, 1)
                    pool.wait_ge(out_rows_p, 3 * n + 2)
                    pool.tensor_tensor(mat_out[:, :, m, :], pool_scratch[0][:, :, :], pool_scratch[1][:, :, :], ALU.add
                                       ).then_inc(out_rows_p, 1)

            make_out_rows()
            for g in range(G):
                if g >= 1:
                    pool.wait_ge(a_ready, g)
                pool.tensor_tensor(turned_part[:, :, :], swap[:, None, :].to_broadcast([P, LEVELS, P]),
                                   dbl[:, :, 1, g:g + 1].to_broadcast([P, LEVELS, P]), ALU.mult
                                   ).then_inc(turned_ready, 1)
                pool.wait_ge(turned_ready, g + 1)
                pool.wait_ge(plain_ready, g + 1)
                if g >= 8:
                    pool.wait_ge(y_made, g // 2 - 3)
                pool.tensor_tensor(a_mat[g // 2 % 4][:, g % 2, :, :], plain_part[g % 2][:, :, :], turned_part[:, :, :],
                                   ALU.add).then_inc(a_ready, 1)

        @block.scalar
        def _(act):
            act.wait_ge(angles, 1)
            act.activation(num[:, 6, :], num[:, 5, :], ACT.Sin).then_inc(sines, 1)
            act.activation(num[:, 7, :], num[:, 5, :], ACT.Sin, scale=0.5).then_inc(sines, 1)
            act.wait_ge(powers, 1)
            act.wait_ge(consts, 2)

            def plain(g):
                if g >= 2:
                    act.wait_ge(a_ready, g - 1)
                for k in range(LEVELS):
                    ins = act.activation(plain_part[g % 2][:, k, :], ident[:, :], ACT.Copy, scale=dbl[:, k, 0, g:g + 1])
                ins.then_inc(plain_ready, 1)

            plain(0)
            plain(1)
            for n in range(G // 4):
                act.wait_ge(in_turned, n + 1)
                act.activation(mat_in[:, 4 * n:4 * n + 4, :], bank[4 + n % 2][:, :].rearrange("p (g s) -> p g s", g=4),
                               ACT.Copy).then_inc(in_copied, 1)
            plain(2)
            plain(3)
            plain(4)
            plain(5)
            for p in range(PAIRS):
                if 2 * p + 7 < G:
                    plain(2 * p + 6)
                    plain(2 * p + 7)
                act.wait_ge(y_made, p + 1)
                if p >= 2:
                    act.wait_ge(y_stored[p % 2], p // 2 * 2 * DMA)
                act.activation(y[p % 2][:, :, :], bank[2 + p % 2][:, :].rearrange("p (g n) -> p g n", g=2),
                               ACT.Copy).then_inc(y_copied, 1)

        @block.vector
        def _(dve):
            link = Chain(dve, dve_link)

            def tt(out, a, b, op):
                link(dve.tensor_tensor(out, a, b, op))

            def ts(out, a, x, op0, y_=None, op1=ALU.bypass):
                link(dve.tensor_scalar(out, a, x, y_, op0, op1))

            def stt(out, a, x, op0, b, op1):
                link(dve.scalar_tensor_tensor(out, a, x, b, op0, op1))

            ROUND = 12582912.0

            def exp_of(out, x, k, r):
                ts(x, x, -87.0, ALU.max, 88.0, ALU.min)
                ts(k, x, 1.4426950408889634, ALU.mult, ROUND, ALU.add)
                ts(k, k, ROUND, ALU.subtract)
                stt(r, k, -0.693359375, ALU.mult, x, ALU.add)
                stt(r, k, 2.12194440e-4, ALU.mult, r, ALU.add)
                ts(out, r, 1.0 / 5040, ALU.mult)
                for term in (1 / 720, 1 / 120, 1 / 24, 1 / 6, 1 / 2, 1.0):
                    stt(out, out, term, ALU.add, r, ALU.mult)
                ts(out, out, 1.0, ALU.add)
                ts(k.bitcast(I32), k, 127.0, ALU.add, 8388608.0, ALU.mult)
                tt(out, out, k, ALU.mult)

            dve.wait_ge(params_in, 12 * DMA)
            dve.wait_ge(consts, 6)
            dve.wait_ge(params_turned, 2)
            link(dve.tensor_copy(lam[:, :, :], bank[0][:, 0:2 * G].rearrange("p (a g) -> p a g", a=2)))
            dve.wait_ge(params_turned, 10)
            for x in range(2):
                ts(cc[:, x, :], bank[1 + x][:, :], sgn[:, 0:1], ALU.mult, -1.0, ALU.mult)
            step, x_, k_, r_, e_ = dt[:, :], num[:, 0, :], num[:, 1, :], num[:, 2, :], num[:, 3, :]
            exp_of(num[:, 8, :], step, k_, r_)
            step = num[:, 8, :]
            tt(num[:, 4, :], lam[:, 1, :], step, ALU.mult)
            ts(k_, num[:, 4, :], 1.0 / (2 * math.pi), ALU.mult, ROUND, ALU.add)
            ts(k_, k_, ROUND, ALU.subtract)
            stt(r_, k_, -6.28125, ALU.mult, num[:, 4, :], ALU.add)
            stt(r_, k_, -TWO_PI_MID, ALU.mult, r_, ALU.add)
            stt(r_, k_, -TWO_PI_LOW, ALU.mult, r_, ALU.add)
            dve.tensor_scalar(num[:, 5, :], r_, -3.1415925, 3.1415925, ALU.max, ALU.min).then_inc(angles, 1)
            tt(x_, lam[:, 0, :], step, ALU.mult)
            exp_of(e_, x_, k_, r_)
            dve.wait_ge(sines, 2)
            tt(num[:, 9, :], num[:, 7, :], num[:, 7, :], ALU.mult)
            ts(num[:, 9, :], num[:, 9, :], -2.0, ALU.mult, 1.0, ALU.add)
            tt(abar[:, 0, :], e_, num[:, 9, :], ALU.mult)
            stt(abar[:, 1, :], num[:, 6, :], sgn[:, 0:1], ALU.mult, e_, ALU.mult)
            ts(num[:, 10, :], abar[:, 0, :], -1.0, ALU.add)
            ts(num[:, 11, :], lam[:, 1, :], sgn[:, 0:1], ALU.mult)
            tt(num[:, 12, :], lam[:, 0, :], lam[:, 0, :], ALU.mult)
            tt(num[:, 13, :], lam[:, 1, :], lam[:, 1, :], ALU.mult)
            tt(num[:, 12, :], num[:, 12, :], num[:, 13, :], ALU.add)
            link(dve.reciprocal(num[:, 12, :], num[:, 12, :]))
            tt(num[:, 13, :], num[:, 10, :], lam[:, 0, :], ALU.mult)
            tt(num[:, 14, :], abar[:, 1, :], num[:, 11, :], ALU.mult)
            tt(num[:, 13, :], num[:, 13, :], num[:, 14, :], ALU.add)
            tt(coef[:, 0, :], num[:, 13, :], num[:, 12, :], ALU.mult)
            tt(num[:, 13, :], abar[:, 1, :], lam[:, 0, :], ALU.mult)
            tt(num[:, 14, :], num[:, 10, :], num[:, 11, :], ALU.mult)
            tt(num[:, 13, :], num[:, 13, :], num[:, 14, :], ALU.subtract)
            tt(coef[:, 1, :], num[:, 13, :], num[:, 12, :], ALU.mult)
            link(dve.memset(pw[:, 0, 0, :], 1.0))
            link(dve.memset(pw[:, 0, 1, :], 0.0))
            link(dve.tensor_copy(pw[:, 1, :, :], abar[:, :, :]))

            def both(*instructions):
                for ins in instructions[:-1]:
                    ins.then_inc(dve_link, 1)
                    link.n += 1
                link(instructions[-1])

            def complex_product(out, a, b, n):
                straight = cross[:, 0:n, :, :]
                crossed = cross[:, n:2 * n, :, :]
                over = b[:, None, :, :].to_broadcast([P, n, 2, G])
                exchanged = b[:, ::-1, :][:, None, :, :].to_broadcast([P, n, 2, G])
                both(dve.tensor_tensor(straight, a, over, ALU.mult), dve.tensor_tensor(crossed, a, exchanged, ALU.mult))
                both(dve.tensor_tensor(out[:, :, 0, :], straight[:, :, 0, :], straight[:, :, 1, :], ALU.subtract),
                     dve.tensor_tensor(out[:, :, 1, :], crossed[:, :, 0, :], crossed[:, :, 1, :], ALU.add))

            m = 1
            while m < SUB:
                complex_product(pw[:, m + 1:2 * m + 1, :, :], pw[:, 1:m + 1, :, :], pw[:, m, :, :], m)
                m *= 2
            link(dve.tensor_copy(dbl[:, 0, 0, :], pw[:, SUB, 0, :]))
            ts(dbl[:, 0, 1, :], pw[:, SUB, 1, :], -1.0, ALU.mult)
            for k in range(1, LEVELS):
                complex_product(dbl[:, k:k + 1, :, :], dbl[:, k - 1:k, :, :], dbl[:, k - 1, :, :], 1)
            dve.engine_nop().then_inc(powers, 1)

            def by_group(x):
                return x[:, :, None].to_broadcast([P, G, C])

            tt(scratch[:, :, :], b_in[:, 0, :, :], by_group(coef[:, 0, :]), ALU.mult)
            tt(scratch2[:, :, :], b_in[:, 1, :, :], by_group(coef[:, 1, :]), ALU.mult)
            tt(bb[:, 0, :, :], scratch[:, :, :], scratch2[:, :, :], ALU.add)
            tt(scratch[:, :, :], b_in[:, 1, :, :], by_group(coef[:, 0, :]), ALU.mult)
            tt(scratch2[:, :, :], b_in[:, 0, :, :], by_group(coef[:, 1, :]), ALU.mult)
            tt(bb[:, 1, :, :], scratch[:, :, :], scratch2[:, :, :], ALU.subtract)
            for l in range(SUB):
                tt(scratch[:, :, :], bb[:, 0, :, :], by_group(pw[:, SUB - 1 - l, 0, :]), ALU.mult)
                tt(scratch2[:, :, :], bb[:, 1, :, :], by_group(pw[:, SUB - 1 - l, 1, :]), ALU.mult)
                tt(t_in[:, :, l, :], scratch[:, :, :], scratch2[:, :, :], ALU.add)
            dve.engine_nop().then_inc(in_rows, 1)
            c_of = [cc[:, x, :].rearrange("p (g c) -> p g c", c=C) for x in range(2)]
            for m in range(POOL_POWERS[0]):
                tt(scratch[:, :, :], c_of[0], by_group(pw[:, m, 0, :]), ALU.mult)
                tt(scratch2[:, :, :], c_of[1], by_group(pw[:, m, 1, :]), ALU.mult)
                tt(mat_out[:, :, m, :], scratch[:, :, :], scratch2[:, :, :], ALU.add)
            dve.engine_nop().then_inc(out_rows, 1)
            for n in range(G // 4):
                dve.wait_ge(kern_made, n + 1)
                dve.tensor_copy(kern[:, 4 * n:4 * n + 4, :], bank[6 + n % 2][0:C, :].rearrange("p (g s) -> p g s", g=4)
                                ).then_inc(kern_copied, 1)
            for b in range(4):
                link(dve.memset(s[b][:, :, 0:1], 0.0))

            def take_v(p):
                dve.wait_ge(v_made, p + 1)
                if p >= 4:
                    dve.wait_ge(y_made, p - 3)
                dve.tensor_copy(s[p % 4][:, :, 1:CHUNKS],
                                bank[p % 2][:, :].rearrange("p (g n) -> p g n", g=2)[:, :, 0:CHUNKS - 1]
                                ).then_inc(s_ready[p % 2], 1)

            def add_term(p, k):
                d = 1 << k
                dve.wait_ge(term_made[p % 2], p // 2 * LEVELS + k + 1)
                dve.wait_ge(s_ready[p % 2], p // 2 * STEP + k + 1)
                dve.tensor_tensor(s[p % 4][:, :, d:], s[p % 4][:, :, d:],
                                  bank[p % 2][:, :].rearrange("p (g n) -> p g n", g=2)[:, :, 0:CHUNKS - d],
                                  ALU.add).then_inc(s_ready[p % 2], 1)

            for q in range(PAIRS // 2):
                take_v(2 * q)
                take_v(2 * q + 1)
                for k in range(LEVELS):
                    add_term(2 * q, k)
                    add_term(2 * q + 1, k)

        @block.tensor
        def _(pe):
            pe.wait_ge(consts, 2)
            pe.wait_ge(params_in, 12 * DMA)
            for part in range(2):
                pe.transpose(bank[0][:, part * G:(part + 1) * G], a_rows[:, part, :, :].rearrange("g a p -> g (a p)"),
                             ident[0:G, 0:G]).then_inc(params_turned, 1)
            for x in range(2):
                for slab in range(4):
                    pe.transpose(bank[1 + x][:, slab * P:(slab + 1) * P],
                                 c_rows[:, slab, x:x + 2, :].rearrange("q a p -> q (a p)"), ident[:, :]
                                 ).then_inc(params_turned, 1)
            pe.wait_ge(in_rows, 1)
            for n in range(G // 4):
                if n >= 2:
                    pe.wait_ge(in_copied, n - 1)
                for i in range(4):
                    mm = pe.transpose(bank[4 + n % 2][:, i * P:(i + 1) * P],
                                      t_in[:, 4 * n + i, :, :].rearrange("p l c -> p (l c)"), ident[:, :])
                mm.then_inc(in_turned, 1)
            pe.wait_ge(out_rows, 1)
            pe.wait_ge(out_rows_p, 3 * len(POOL_POWERS))
            for n in range(G // 4):
                if n >= 2:
                    pe.wait_ge(kern_copied, n - 1)
                for i in range(4):
                    mm = pe.matmul(bank[6 + n % 2][0:C, i * P:(i + 1) * P], bb[:, 0, 4 * n + i, :],
                                   mat_out[:, 4 * n + i, 0:SUB, :].rearrange("p l c -> p (l c)"), start=True, stop=True)
                mm.then_inc(kern_made, 1)
            pe.wait_ge(in_copied, G // 4)
            pe.wait_ge(u_in, 4 * SUB * DMA)

            def make_v(p):
                if p >= 2:
                    pe.wait_ge(s_ready[p % 2], p // 2 * STEP)
                for i in range(2):
                    g = 2 * p + i
                    mm = pe.matmul(bank[p % 2][:, i * CHUNKS:(i + 1) * CHUNKS], mat_in[:, g, :], u[:, g, :],
                                   start=True, stop=True)
                mm.then_inc(v_made, 1)

            def make_term(p, k):
                d = 1 << k
                pe.wait_ge(s_ready[p % 2], p // 2 * STEP + k + 1)
                pe.wait_ge(a_ready, 2 * p + 2)
                for i in range(2):
                    mm = pe.matmul(bank[p % 2][:, i * CHUNKS:(i + 1) * CHUNKS - d], a_mat[p % 4][:, i, k, :],
                                   s[p % 4][:, i, 0:CHUNKS - d], start=True, stop=True)
                mm.then_inc(term_made[p % 2], 1)

            def make_y(p):
                pe.wait_ge(s_ready[p % 2], (p // 2 + 1) * STEP)
                if p >= 2:
                    pe.wait_ge(y_copied, p - 1)
                pe.wait_ge(within_in, SUB * DMA)
                for i in range(2):
                    g = 2 * p + i
                    out = bank[2 + p % 2][:, i * CHUNKS:(i + 1) * CHUNKS]
                    pe.matmul(out, mat_within[:, g, :], u[:, g, :], start=True, stop=False)
                    mm = pe.matmul(out, mat_out[:, g, 1:SUB + 1, :].rearrange("p l c -> p (l c)"), s[p % 4][:, i, :],
                                   start=False, stop=True)
                mm.then_inc(y_made, 1)

            for q in range(PAIRS // 2):
                make_v(2 * q)
                make_v(2 * q + 1)
                if q >= 1:
                    make_y(2 * q - 2)
                    make_y(2 * q - 1)
                for k in range(LEVELS):
                    make_term(2 * q, k)
                    make_term(2 * q + 1, k)
            make_y(PAIRS - 2)
            make_y(PAIRS - 1)


TWO_PI_MID = 0.0019350051879882812
TWO_PI_LOW = 2 * math.pi - 6.28125 - TWO_PI_MID


def mix_heads(nc, x, u_dram, y_ssm_dram, y_sb_dram, d_skip, w_glu, g_ssm, g_sb, w_out, x1_dram):
    ROWS = 512
    STEPS = SEQ // ROWS
    TILES = ROWS // P
    NF = SSM_WIDTH // P
    NCH = ROWS // SUB
    RAW = 4
    PRODUCTS = 2 * TILES
    with ExitStack() as ctx:
        def sb(name, shape, dt=F32):
            return ctx.enter_context(nc.sbuf_tensor("m_" + name, shape, dt))

        def ps(name, shape):
            return ctx.enter_context(nc.psum_tensor("m_ps_" + name, shape, F32))

        sem = ctx.enter_context(semaphores(nc, "m_"))

        w_raw = sb("w_raw", [P, RAW, 1024])
        glu_hi = sb("glu_hi", [P, NF, SSM_WIDTH], F32R)
        glu_lo = sb("glu_lo", [P, NF, SSM_WIDTH], F32R)
        out_hi = sb("out_hi", [P, KC, D_MODEL], F32R)
        out_lo = sb("out_lo", [P, KC, D_MODEL], F32R)
        gain = sb("gain", [P, KC])
        skip = sb("skip", [P, NF])
        ident = sb("ident", [P, P])
        ones = sb("ones", [P, 1])
        u = sb("u", [P, NF, ROWS])
        y = sb("y", [P, NF, ROWS])
        g = sb("g", [P, NF, ROWS])
        g_hi = sb("g_hi", [P, NF, ROWS], F32R)
        g_lo = sb("g_lo", [P, NF, ROWS], F32R)
        gate = sb("gate", [P, 2, ROWS])
        y2 = sb("y2", [P, NF, ROWS])
        y2_sq = sb("y2_sq", [P, NF, ROWS])
        y2_hi = sb("y2_hi", [P, NF, ROWS], F32R)
        y2_lo = sb("y2_lo", [P, NF, ROWS], F32R)
        xt = sb("xt", [P, TILES, D_MODEL])
        ys = sb("ys", [P, TILES, SB_WIDTH])
        junk = sb("junk", [P, SB_WIDTH])
        ys_hi = sb("ys_hi", [P, 4, P], F32R)
        ys_lo = sb("ys_lo", [P, 4, P], F32R)
        norm = sb("norm", [P, 2, TILES])
        stat = sb("stat", [P, 4, 2, TILES])

        mix_ps = [ps(f"mix{i}", [P, D_MODEL]) for i in range(2)]
        glu_ps = [ps(f"glu{i}", [P, BANK]) for i in range(2)]
        turn_ps = ps("turn", [P, 4, P])
        sum_ps = ps("sum", [P, BANK])

        consts = sem("consts")
        params_in = sem("params_in")
        w_loaded = [sem(f"w_loaded{i}") for i in range(RAW)]
        w_hi_ready = sem("w_hi_ready")
        w_split = sem("w_split")
        dve_link = sem("dve_link")
        uy_loaded = sem("uy_loaded")
        x_loaded = [sem(f"x_loaded{j}") for j in range(TILES)]
        ys_loaded = [sem(f"ys_loaded{j}") for j in range(TILES)]
        skipped = Tally(sem("skipped"), NF)
        gelued = Tally(sem("gelued"), NF)
        g_high = Tally(sem("g_high"), NF)
        g_low = Tally(sem("g_low"), NF)
        glued = Tally(sem("glued"), NF)
        gated = Tally(sem("gated"), NF)
        y2_ready = Tally(sem("y2_ready"), NF)
        y2_squared = Tally(sem("y2_squared"), NF)
        y2_high = Tally(sem("y2_high"), NF)
        y2_low = Tally(sem("y2_low"), NF)
        summed = Tally(sem("summed"), 1)
        ys_squared = Tally(sem("ys_squared"), TILES)
        normed = Tally(sem("normed"), 1)
        turned = Tally(sem("turned"), TILES)
        ys_high = Tally(sem("ys_high"), TILES)
        ys_low = Tally(sem("ys_low"), TILES)
        made = Tally(sem("made"), PRODUCTS)
        added = Tally(sem("added"), PRODUCTS)
        stored = [Tally(sem(f"stored{j}"), DMA) for j in range(TILES)]
        ACT_TALLIES = [gelued, g_high, gated, y2_squared, y2_high, ys_squared, ys_high]
        DVE_TALLIES = [skipped, y2_ready, y2_low, normed, ys_low, added]
        PE_TALLIES = [glued, summed, turned, made]

        block = ctx.enter_context(nc.Block())
        W_GLU = 2
        W_PIECES = W_GLU + KC

        def w_piece(n):
            if n < W_GLU:
                rows = slice(2 * n, 2 * n + 2)
                src = w_glu.rearrange("(k p) f -> p k f", p=P)[:, rows, :]
                return src, glu_hi[:, rows, :], glu_lo[:, rows, :], None
            k = n - W_GLU
            src = w_out[k * P:(k + 1) * P, :].rearrange("p (o f) -> p o f", o=2)
            return (src, out_hi[:, k, :].rearrange("p (o f) -> p o f", o=2),
                    out_lo[:, k, :].rearrange("p (o f) -> p o f", o=2), k)

        def raw(n):
            return w_raw[:, n % RAW, :].rearrange("p (o f) -> p o f", o=2)

        @block.sync
        def _(sp):
            for tally in stored:
                tally.start(sp)

            def load_uy(c):
                for src, dst in ((u_dram, u), (y_ssm_dram, y)):
                    if c > 0:
                        sp.wait_ge(gelued.sem, gelued.at(c - 1, NF))
                    for f in range(NF):
                        sp.dma_start(dst[:, f, :].rearrange("p (l n) -> p l n", l=SUB),
                                     src[f * P:(f + 1) * P, :, c * NCH:(c + 1) * NCH]).then_inc(uy_loaded, DMA)

            def load_ys(c, j):
                if c > 0:
                    sp.wait_ge(turned.sem, turned.at(c - 1, j + 1))
                sp.dma_start(ys[:, j, :], y_sb_dram[c * ROWS + j * P:c * ROWS + (j + 1) * P, :]).then_inc(ys_loaded[j], DMA)

            def load_x(c, j):
                sp.wait_ge(stored[j].sem, stored[j].at(c - 1, DMA))
                sp.dma_start(xt[:, j, :], x[c * ROWS + j * P:c * ROWS + (j + 1) * P, :]).then_inc(x_loaded[j], DMA)

            load_uy(0)
            for src, dst in ((g_ssm, gain[:, 0:NF]), (g_sb, gain[:, NF:KC]), (d_skip, skip[:, :])):
                with nc.allow_non_contiguous_dma(reason="512 single values"):
                    sp.dma_start(dst, src.rearrange("(k p) -> p k", p=P)).then_inc(params_in, DMA)
            for n in range(W_PIECES):
                if n >= RAW:
                    sp.wait_ge(w_split, n - RAW + 1)
                sp.dma_start(raw(n), w_piece(n)[0]).then_inc(w_loaded[n % RAW], DMA)
            for j in range(TILES):
                load_ys(0, j)
            for j in range(TILES):
                load_x(0, j)
            load_uy(1)
            for c in range(STEPS):
                more = c + 1 < STEPS
                for j in range(TILES):
                    if j == 1 and c + 2 < STEPS:
                        load_uy(c + 2)
                    row = c * ROWS + j * P
                    sp.wait_ge(added.sem, added.at(c, TILES + j + 1))
                    sp.dma_start(x1_dram[row:row + P, :], xt[:, j, :]).then_inc(stored[j].sem, DMA)
                    if more:
                        load_ys(c + 1, j)
                        if j:
                            load_x(c + 1, j - 1)
                if more:
                    load_x(c + 1, TILES - 1)
            for tally in stored:
                sp.wait_ge(tally.sem, tally.at(STEPS - 1, DMA))

        @block.gpsimd
        def _(pool):
            g_low.start(pool)
            fill_identity(pool, ident[:, :], consts)
            pool.memset(ones[:, :], 1.0).then_inc(consts, 1)

            with pool.Fori(0, STEPS) as c:
                for f in range(NF):
                    pool.wait_ge(g_high.sem, g_high.at(c, f + 1))
                    pool.wait_ge(glued.sem, glued.at(c - 1, NF))
                    pool.tensor_tensor(g_lo[:, f, :], g[:, f, :], g_hi[:, f, :].bitcast(F32), ALU.subtract
                                       ).then_inc(g_low.sem, 1)

        @block.scalar
        def _(act):
            for tally in ACT_TALLIES:
                tally.start(act)

            def gelus(c):
                for f in range(NF):
                    act.wait_ge(skipped.sem, skipped.at(c, f + 1))
                    act.wait_ge(y2_ready.sem, y2_ready.at(c - 1, NF))
                    act.wait_ge(g_low.sem, g_low.at(c - 1, NF))
                    act.activation(g[:, f, :], y[:, f, :], ACT.Gelu_apprx_tanh).then_inc(gelued.sem, 1)
                for f in range(NF):
                    act.wait_ge(gelued.sem, gelued.at(c, f + 1))
                    act.wait_ge(glued.sem, glued.at(c - 1, NF))
                    act.activation(g_hi[:, f, :], g[:, f, :], ACT.Copy).then_inc(g_high.sem, 1)

            def gated_high(c, f):
                act.wait_ge(glued.sem, glued.at(c, f + 1))
                act.wait_ge(y2_ready.sem, y2_ready.at(c, f - 1))
                act.activation(gate[:, f % 2, :], glu_ps[f % 2][:, :], ACT.Sigmoid).then_inc(gated.sem, 1)
                act.wait_ge(y2_ready.sem, y2_ready.at(c, f + 1))
                act.wait_ge(made.sem, made.at(c - 1, TILES))
                act.activation(y2_hi[:, f, :], y2[:, f, :], ACT.Copy).then_inc(y2_high.sem, 1)
                act.wait_ge(summed.sem, summed.at(c - 1, 1))
                act.activation(y2_sq[:, f, :], y2[:, f, :], ACT.Square).then_inc(y2_squared.sem, 1)

            def squares_ys(c, count):
                for j in range(TILES):
                    act.wait_ge(ys_loaded[j], count)
                    act.wait_ge(normed.sem, normed.at(c - 1, 1))
                    act.wait_ge(ys_squared.sem, ys_squared.at(c, j))
                    act.activation(junk[:, :], ys[:, j, :], ACT.Square,
                                   accum_out=stat[:, 0, 1, j:j + 1]).then_inc(ys_squared.sem, 1)

            gelus(0)
            act.wait_ge(params_in, 3 * DMA)

            def split(n):
                act.wait_ge(w_loaded[n % RAW], (n // RAW + 1) * DMA)
                src, hi, lo, k = w_piece(n)
                if k is None:
                    act.activation(hi, raw(n), ACT.Copy).then_inc(w_hi_ready, 1)
                else:
                    act.activation(hi, raw(n), ACT.Copy, scale=gain[:, k:k + 1]).then_inc(w_hi_ready, 1)

            for n in range(W_GLU):
                split(n)
            for f in range(NF):
                gated_high(0, f)
                for n in range(W_GLU + f * KC // NF, W_GLU + (f + 1) * KC // NF):
                    split(n)
            squares_ys(0, DMA)

            def high_ys(c, j):
                act.wait_ge(turned.sem, turned.at(c, j + 1))
                act.wait_ge(made.sem, made.at(c, TILES + j))
                act.activation(ys_hi[:, :, :], turn_ps[:, :, :], ACT.Copy).then_inc(ys_high.sem, 1)

            def body(c, more):
                if more:
                    gelus(c + 1)
                for j in range(TILES):
                    high_ys(c, j)
                    if more:
                        gated_high(c + 1, j)
                if more:
                    squares_ys(c + 1, c * DMA + 2 * DMA)

            with act.Fori(0, STEPS - 1) as c:
                body(c, True)
            body(STEPS - 1, False)

        @block.vector
        def _(dve):
            for tally in DVE_TALLIES:
                tally.start(dve)
            link = Chain(dve, dve_link)

            def skips(c, count):
                dve.wait_ge(uy_loaded, count)
                for f in range(NF):
                    dve.scalar_tensor_tensor(y[:, f, :], u[:, f, :], skip[:, f:f + 1], y[:, f, :], ALU.mult, ALU.add
                                             ).then_inc(skipped.sem, 1)

            def glu_low(c, f):
                dve.wait_ge(gated.sem, gated.at(c, f + 1))
                dve.wait_ge(y2_squared.sem, y2_squared.at(c - 1, NF))
                dve.wait_ge(y2_low.sem, y2_low.at(c - 1, NF))
                dve.tensor_tensor(y2[:, f, :].rearrange("p (n l) -> p l n", l=SUB),
                                  g[:, f, :].rearrange("p (l n) -> p l n", l=SUB),
                                  gate[:, f % 2, :].rearrange("p (l n) -> p l n", l=SUB), ALU.mult
                                  ).then_inc(y2_ready.sem, 1)
                dve.wait_ge(y2_high.sem, y2_high.at(c, f + 1))
                dve.wait_ge(made.sem, made.at(c - 1, TILES))
                dve.tensor_tensor(y2_lo[:, f, :], y2[:, f, :], y2_hi[:, f, :].bitcast(F32), ALU.subtract
                                  ).then_inc(y2_low.sem, 1)

            def norms(c):
                dve.wait_ge(summed.sem, summed.at(c, 1))
                dve.wait_ge(ys_squared.sem, ys_squared.at(c, TILES))
                dve.wait_ge(added.sem, added.at(c - 1, PRODUCTS))
                link(dve.tensor_copy(stat[:, 0, 0, :], sum_ps[:, 0:TILES]))
                rsqrt_mean(dve, link, stat[:, 0, :, :], SSM_WIDTH, stat[:, 1, :, :], stat[:, 2, :, :], stat[:, 3, :, :])
                dve.tensor_copy(norm[:, :, :], stat[:, 2, :, :]).then_inc(normed.sem, 1)

            LINKS = 1 + RSQRT_LINKS

            dve.wait_ge(params_in, 3 * DMA)
            skips(0, 8 * DMA)

            def split(n):
                dve.wait_ge(w_hi_ready, n + 1)
                src, hi, lo, k = w_piece(n)
                if k is None:
                    dve.tensor_tensor(lo, raw(n), hi.bitcast(F32), ALU.subtract).then_inc(w_split, 1)
                else:
                    dve.scalar_tensor_tensor(lo, raw(n), gain[:, k:k + 1], hi.bitcast(F32), ALU.mult, ALU.subtract
                                             ).then_inc(w_split, 1)

            for n in range(W_GLU):
                split(n)
            for f in range(NF):
                glu_low(0, f)
                for n in range(W_GLU + f * KC // NF, W_GLU + (f + 1) * KC // NF):
                    split(n)
            norms(0)

            def low_ys(c, j):
                dve.wait_ge(ys_high.sem, ys_high.at(c, j + 1))
                dve.wait_ge(made.sem, made.at(c, TILES + j))
                dve.tensor_tensor(ys_lo[:, :, :], turn_ps[:, :, :], ys_hi[:, :, :].bitcast(F32), ALU.subtract
                                  ).then_inc(ys_low.sem, 1)

            def add(c, i, count=None):
                half, j = i // TILES, i % TILES
                if i == 0:
                    dve.wait_ge(normed.sem, normed.at(c, 1))
                if half == 0:
                    dve.wait_ge(x_loaded[j], count)
                else:
                    dve.wait_ge(added.sem, added.at(c, j + 1))
                dve.wait_ge(made.sem, made.at(c, i + 1))
                dve.scalar_tensor_tensor(xt[:, j, :], mix_ps[i % 2][:, :], norm[:, half, j:j + 1], xt[:, j, :],
                                         ALU.mult, ALU.add).then_inc(added.sem, 1)

            def body(c, more):
                if more:
                    skips(c + 1, c * (8 * DMA) + 16 * DMA)
                for j in range(TILES):
                    add(c, j, c * DMA + DMA)
                low_ys(c, 0)
                for j in range(TILES):
                    if more:
                        glu_low(c + 1, j)
                    add(c, TILES + j)
                    if j + 1 < TILES:
                        low_ys(c, j + 1)
                if more:
                    link.begin(c * LINKS + LINKS)
                    norms(c + 1)

            with dve.Fori(0, STEPS - 1) as c:
                body(c, True)
            body(STEPS - 1, False)

        @block.tensor
        def _(pe):
            for tally in PE_TALLIES:
                tally.start(pe)
            pe.wait_ge(consts, 3)

            def three_passes(out, hi_a, lo_a, hi_b, lo_b, start, stop):
                pe.matmul(out, hi_a, hi_b, start=start, stop=False)
                pe.matmul(out, hi_a, lo_b, start=False, stop=False)
                return pe.matmul(out, lo_a, hi_b, start=False, stop=stop)

            def glu(c, f):
                pe.wait_ge(g_low.sem, g_low.at(c, NF))
                pe.wait_ge(gated.sem, gated.at(c, f - 1) if f >= 2 else gated.at(c - 1, f + 3))
                cols = slice(f * P, (f + 1) * P)
                for k in range(NF):
                    mm = three_passes(glu_ps[f % 2][:, :], glu_hi[:, k, cols], glu_lo[:, k, cols],
                                      g_hi[:, k, :], g_lo[:, k, :], k == 0, k == NF - 1)
                mm.then_inc(glued.sem, 1)

            def sums(c):
                pe.wait_ge(y2_squared.sem, y2_squared.at(c, NF))
                pe.wait_ge(normed.sem, normed.at(c - 1, 1))
                for j in range(TILES):
                    for k in range(NF):
                        mm = pe.matmul(sum_ps[:, j:j + 1], y2_sq[:, k, j * P:(j + 1) * P], ones[:, :],
                                       start=(k == 0), stop=(k == NF - 1))
                mm.then_inc(summed.sem, 1)

            def turn(c, j, count):
                pe.wait_ge(ys_loaded[j], count)
                pe.wait_ge(ys_low.sem, ys_low.at(c, j))
                for k in range(4):
                    mm = pe.transpose(turn_ps[:, k, :], ys[:, j, k * P:(k + 1) * P], ident[:, :])
                mm.then_inc(turned.sem, 1)

            def product(c, i, hi, lo, rows):
                pe.wait_ge(added.sem, added.at(c, i - 1) if i >= 2 else added.at(c - 1, PRODUCTS - 1 + i))
                base = i // TILES * NF
                for o in range(2):
                    cols = slice(o * BANK, (o + 1) * BANK)
                    for k in range(NF):
                        mm = three_passes(mix_ps[i % 2][:, cols], hi[:, k, rows], lo[:, k, rows], out_hi[:, base + k, cols],
                                          out_lo[:, base + k, cols], k == 0, k == NF - 1)
                mm.then_inc(made.sem, 1)

            def body(c, more):
                pe.wait_ge(y2_low.sem, y2_low.at(c, NF))
                for j in range(TILES):
                    product(c, j, y2_hi, y2_lo, slice(j * P, (j + 1) * P))
                    if j == 0:
                        turn(c, 0, c * DMA + DMA)
                for j in range(TILES):
                    if more:
                        glu(c + 1, j)
                    pe.wait_ge(ys_low.sem, ys_low.at(c, j + 1))
                    product(c, TILES + j, ys_hi, ys_lo, slice(0, P))
                    if j + 1 < TILES:
                        turn(c, j + 1, c * DMA + DMA)
                if more:
                    sums(c + 1)

            pe.wait_ge(w_split, W_GLU)
            for f in range(NF):
                glu(0, f)
            sums(0)
            pe.wait_ge(w_split, W_PIECES)
            with pe.Fori(0, STEPS - 1) as c:
                body(c, True)
            body(STEPS - 1, False)


def cross_attention(nc, x1_dram, mem, g_xa, g_mem, w_q, w_kv, g_q, g_k, w_o, x2_dram, x2_sums):
    TILES = 4
    STEPS = SEQ // (P * TILES)
    H = XA_HEADS
    SCALE = XA_HEAD ** -0.5
    MT = MEM // P
    RAW = 4
    TRAIL = 2
    with ExitStack() as ctx:
        def sb(name, shape, dt=F32):
            return ctx.enter_context(nc.sbuf_tensor("x_" + name, shape, dt))

        def ps(name, shape):
            return ctx.enter_context(nc.psum_tensor("x_ps_" + name, shape, F32))

        sem = ctx.enter_context(semaphores(nc, "x_"))

        w_raw = sb("w_raw", [P, RAW, 1024])
        kv_hi = sb("kv_hi", [P, KC, XA_WIDTH], F32R)
        kv_lo = sb("kv_lo", [P, KC, XA_WIDTH], F32R)
        wq_hi = sb("wq_hi", [P, KC, XA_WIDTH], F32R)
        wq_lo = sb("wq_lo", [P, KC, XA_WIDTH], F32R)
        wo_hi = sb("wo_hi", [P, H, D_MODEL], F32R)
        wo_lo = sb("wo_lo", [P, H, D_MODEL], F32R)
        ident = sb("ident", [P, P])
        g_row = sb("g_row", [P, D_MODEL])
        gm_row = sb("gm_row", [P, D_MODEL])
        gains = sb("gains", [P, 2])
        memt_hi = sb("memt_hi", [P, KC, MEM], F32R)
        memt_lo = sb("memt_lo", [P, KC, MEM], F32R)
        kt = sb("kt", [P, H, MEM])
        v = sb("v", [P, MT, XA_WIDTH])
        xt = sb("xt", [P, TILES, D_MODEL])
        mt = xt[:, 2:2 + MT, :]
        xr = sb("xr", [P, 2, D_MODEL])
        sums = sb("sums", [P, TILES])
        junk = sb("junk", [P, D_MODEL])
        ht_hi = sb("ht_hi", [P, KC, P], F32R)
        ht_lo = sb("ht_lo", [P, KC, P], F32R)
        sq = sb("sq", [P, XA_WIDTH])
        qn = sb("qn", [P, XA_WIDTH])
        qt = sb("qt", [P, H, P])
        p = sb("p", [P, H, MEM])
        pt = sb("pt", [P, H * MT, P])
        ot_hi = sb("ot_hi", [P, H, P], F32R)
        ot_lo = sb("ot_lo", [P, H, P], F32R)
        mstat = sb("mstat", [P, 4, MT])
        stat = sb("stat", [P, 4, 1 + H])
        soft = sb("soft", [P, 4, H])

        th_ps = ps("th", [P, KC, P])
        to_ps = ps("to", [P, H, P])
        q_ps = ps("q", [P, BANK])
        s_ps = ps("s", [P, H, MEM])
        x_ps = ps("x", [P, D_MODEL])

        consts = sem("consts")
        params_in = sem("params_in")
        mem_in = sem("mem_in")
        w_loaded = [sem(f"w_loaded{i}") for i in range(RAW)]
        w_hi_ready = sem("w_hi_ready")
        w_split = sem("w_split")
        dve_link = sem("dve_link")
        mem_squared = sem("mem_squared")
        mem_normed = sem("mem_normed")
        mem_turned = sem("mem_turned")
        mem_high = sem("mem_high")
        mem_low = sem("mem_low")
        kv_made = sem("kv_made")
        kv_read = sem("kv_read")
        k_squared = sem("k_squared")
        k_normed = sem("k_normed")
        k_turned = sem("k_turned")
        kt_ready = sem("kt_ready")

        def tally(name):
            return Tally(sem(name), TILES)

        x_loaded = [sem(f"x_loaded{i}") for i in range(TILES)]
        xr_loaded = [sem(f"xr_loaded{i}") for i in range(2)]
        stored = [Tally(sem(f"stored{i}"), TILES // 2 * DMA) for i in range(2)]
        sums_stored = Tally(sem("sums_stored"), DMA)
        x_squared, h_high, q_squared, o_high, exped, pt_ready, x2_squared = [
            tally(n) for n in ("x_squared", "h_high", "q_squared", "o_high", "exped", "pt_ready", "x2_squared")]
        x_normed, h_low, qt_ready, q_normed, o_low, maxed, p_scaled, added = [
            tally(n) for n in ("x_normed", "h_low", "qt_ready", "q_normed", "o_low", "maxed", "p_scaled", "added")]
        h_turned, q_made, q_turned, scored, p_turned, o_made, x_made = [
            tally(n) for n in ("h_turned", "q_made", "q_turned", "scored", "p_turned", "o_made", "x_made")]

        block = ctx.enter_context(nc.Block())
        TWOS = range(0, KC, 2)
        PIECES = ([("kv", 0, k) for k in TWOS] + [("q", 0, k) for k in TWOS] + [("kv", 1, k) for k in TWOS]
                  + [("o", 0, k) for k in range(H)])
        NP = KC // 2

        def w_piece(n):
            what, half, k = PIECES[n]
            if what == "kv":
                src = w_kv[k * P:(k + 2) * P, half * XA_WIDTH:(half + 1) * XA_WIDTH].rearrange("(o p) f -> p o f", p=P)
                return src, kv_hi[:, k:k + 2, :], kv_lo[:, k:k + 2, :]
            if what == "q":
                src = w_q[k * P:(k + 2) * P, :].rearrange("(o p) f -> p o f", p=P)
                return src, wq_hi[:, k:k + 2, :], wq_lo[:, k:k + 2, :]
            two = "p (o f) -> p o f"
            return (w_o[k * P:(k + 1) * P, :].rearrange(two, o=2), wo_hi[:, k, :].rearrange(two, o=2),
                    wo_lo[:, k, :].rearrange(two, o=2))

        def raw(n):
            return w_raw[:, n % RAW, :].rearrange("p (o f) -> p o f", o=2)

        def pipeline(eng, stage, lags, before, link=None):
            lead, trail = lags
            for j in range(-lead, TILES):
                if j in before:
                    before[j]()
                stage(0, j, True)
            n0 = link.n if link else 0
            with eng.Fori(1, STEPS - 1) as c:
                if link:
                    link.begin((c - 1) * LINKS + n0)
                for j in range(TILES):
                    stage(c, j, None)
                assert not link or link.n == LINKS
            if link:
                link.begin((STEPS - 2) * LINKS + n0)
            for j in range(TILES + trail):
                stage(STEPS - 1, j, False)

        LINKS = TILES * (1 + 2 + RSQRT_LINKS - 1 + 1 + 1)

        def here(c, j, lag, edge):
            k = j - lag
            if edge is True:
                return k >= 0
            if edge is False:
                return k < TILES
            return True

        @block.sync
        def _(sp):
            for t in stored + [sums_stored]:
                t.start(sp)
            for j in range(MT):
                sp.dma_start(mt[:, j, :], mem[j * P:(j + 1) * P, :]).then_inc(mem_in, DMA)
            sp.dma_start(gm_row[:, :], g_mem.partition_broadcast(P)).then_inc(params_in, DMA)
            sp.dma_start(g_row[:, :], g_xa.partition_broadcast(P)).then_inc(params_in, DMA)
            for n, src in enumerate((g_q, g_k)):
                sp.dma_start(gains[:, n:n + 1], src.rearrange("(p a) -> p a", a=1)).then_inc(params_in, DMA)

            def load_x(t):
                if t >= TILES:
                    sp.wait_ge(h_turned.sem, h_turned.at(0, t - TILES + 1))
                elif t >= 2:
                    sp.wait_ge(mem_turned, MT)
                sp.dma_start(xt[:, t % TILES, :], x1_dram[t * P:(t + 1) * P, :]).then_inc(x_loaded[t % TILES], DMA)

            def load_xr(t):
                if t >= 2:
                    sp.wait_ge(stored[t % 2].sem, stored[t % 2].at(0, (t // 2) * DMA))
                    sp.wait_ge(x2_squared.sem, x2_squared.at(0, t - 1))
                sp.dma_start(xr[:, t % 2, :], x1_dram[t * P:(t + 1) * P, :]).then_inc(xr_loaded[t % 2], DMA)

            def store_sums(c):
                sp.wait_ge(x2_squared.sem, x2_squared.at(c, TILES))
                sp.dma_start(x2_sums[:, c * TILES:(c + 1) * TILES], sums[:, :]).then_inc(sums_stored.sem, DMA)

            T = STEPS * TILES
            for n in range(len(PIECES)):
                if n == NP:
                    load_x(0)
                    load_x(1)
                    load_xr(0)
                    load_xr(1)
                if n == 3 * NP:
                    for t in range(2, 5):
                        load_x(t)
                if n >= RAW:
                    sp.wait_ge(w_split, n - RAW + 1)
                sp.dma_start(raw(n), w_piece(n)[0]).then_inc(w_loaded[n % RAW], DMA)
            for t in range(2, T + TRAIL):
                if t + 3 < T:
                    load_x(t + 3)
                k = t - TRAIL
                sp.wait_ge(added.sem, added.at(0, k + 1))
                sp.dma_start(x2_dram[k * P:(k + 1) * P, :], xr[:, k % 2, :]).then_inc(stored[k % 2].sem, DMA)
                if 1 <= k < T - 1:
                    load_xr(k + 1)
                if k >= TILES and k % TILES == 0:
                    store_sums(k // TILES - 1)
            store_sums(STEPS - 1)
            sp.wait_ge(sums_stored.sem, sums_stored.at(STEPS - 1, DMA))
            for i in range(2):
                sp.wait_ge(stored[i].sem, stored[i].at(STEPS - 1, TILES // 2 * DMA))

        @block.gpsimd
        def _(pool):
            fill_identity(pool, ident[:, :], consts)

        @block.scalar
        def _(act):
            for t in (x_squared, h_high, q_squared, o_high, exped, pt_ready, x2_squared):
                t.start(act)
            act.wait_ge(mem_in, MT * DMA)
            for j in range(MT):
                if j:
                    act.wait_ge(mem_squared, j)
                act.activation(junk[:, :], mt[:, j, :], ACT.Square, accum_out=mstat[:, 0, j:j + 1]).then_inc(mem_squared, 1)

            def split(n):
                act.wait_ge(w_loaded[n % RAW], (n // RAW + 1) * DMA)
                if n == 2 * NP:
                    act.wait_ge(kv_made, MT)
                src, hi, lo = w_piece(n)
                act.activation(hi, raw(n), ACT.Copy).then_inc(w_hi_ready, 1)

            for n in range(NP):
                split(n)
                if n == 1:
                    for j in range(MT):
                        act.wait_ge(mem_turned, j + 1)
                        act.activation(memt_hi[:, :, j * P:(j + 1) * P], th_ps[:, :, :], ACT.Copy).then_inc(mem_high, 1)

            def prepare_q_and_k():
                for n in range(NP, 2 * NP):
                    split(n)
                for j in range(MT):
                    act.wait_ge(kv_made, j + 1)
                    if j:
                        act.wait_ge(k_normed, 1)
                    act.activation(sq[:, :], x_ps[:, j * BANK:(j + 1) * BANK], ACT.Square).then_inc(k_squared, 1)

            def prepare_v_and_o():
                for n in range(2 * NP, 4 * NP):
                    split(n)
                    if n == 4 * NP - 2:
                        for j in range(MT):
                            act.wait_ge(kv_made, MT + j + 1)
                            act.activation(v[:, j, :], x_ps[:, j * BANK:(j + 1) * BANK], ACT.Copy).then_inc(kv_read, 1)

            def square_x(c, j, lag):
                k = j - lag
                act.wait_ge(x_loaded[k % TILES], c * DMA + (k // TILES + 1) * DMA)
                act.wait_ge(x_normed.sem, x_normed.at(c, j - lag))
                act.wait_ge(x_squared.sem, x_squared.at(c, j - lag))
                act.wait_ge(x2_squared.sem, x2_squared.at(c, j - 2))
                act.activation(junk[:, :], xt[:, k % TILES, :], ACT.Square, accum_out=stat[:, 0, 0:1]
                               ).then_inc(x_squared.sem, 1)

            def stage(c, j, edge):
                if here(c, j, 0, edge):
                    act.wait_ge(q_made.sem, q_made.at(c, j + 1))
                    if edge is True and j == 0:
                        act.wait_ge(k_normed, MT)
                    act.wait_ge(q_normed.sem, q_normed.at(c, j))
                    act.activation(sq[:, :], q_ps[:, :], ACT.Square).then_inc(q_squared.sem, 1)
                if here(c, j, 2, edge):
                    k = j - 2
                    act.wait_ge(o_made.sem, o_made.at(c, k + 1))
                    act.wait_ge(x_made.sem, x_made.at(c, k))
                    act.activation(ot_hi[:, :, :], to_ps[:, :, :], ACT.Copy).then_inc(o_high.sem, 1)
                if here(c, j, 3, edge):
                    k = j - 3
                    act.wait_ge(added.sem, added.at(c, k + 1))
                    act.wait_ge(sums_stored.sem, sums_stored.at(c + k // TILES - 1, DMA))
                    act.wait_ge(x_squared.sem, x_squared.at(c, min(j + 3, TILES) if edge is False else j + 3))
                    act.wait_ge(x2_squared.sem, x2_squared.at(c, k))
                    act.activation(junk[:, :], xr[:, k % 2, :], ACT.Square, accum_out=sums[:, k % TILES:k % TILES + 1]
                                   ).then_inc(x2_squared.sem, 1)
                if here(c, j, -1, edge):
                    k = j + 1
                    act.wait_ge(h_turned.sem, h_turned.at(c, k + 1))
                    act.wait_ge(q_made.sem, q_made.at(c, k))
                    act.activation(ht_hi[:, :, :], th_ps[:, :, :], ACT.Copy).then_inc(h_high.sem, 1)
                if here(c, j, 1, edge):
                    k = j - 1
                    act.wait_ge(maxed.sem, maxed.at(c, k + 1))
                    act.wait_ge(p_turned.sem, p_turned.at(c, k))
                    for h in range(H):
                        ins = act.activation(p[:, h, :], s_ps[:, h, :], ACT.Exp, bias=soft[:, 1, h:h + 1], scale=SCALE,
                                             accum_out=soft[:, 2, h:h + 1])
                    ins.then_inc(exped.sem, 1)
                    act.wait_ge(p_turned.sem, p_turned.at(c, k + 1))
                    act.wait_ge(o_made.sem, o_made.at(c, k))
                    act.activation(pt[:, :, :], s_ps[:, :, :].rearrange("p h m -> p (h m)").rearrange("p (a q) -> p a q", q=P),
                                   ACT.Copy).then_inc(pt_ready.sem, 1)
                if here(c, j, -3, edge):
                    square_x(c, j, -3)

            pipeline(act, stage, (3, 3), {-2: prepare_q_and_k, 1: prepare_v_and_o})

        @block.vector
        def _(dve):
            for t in (x_normed, h_low, qt_ready, q_normed, o_low, maxed, p_scaled, added):
                t.start(dve)
            link = Chain(dve, dve_link)
            dve.wait_ge(params_in, 4 * DMA)
            dve.wait_ge(mem_squared, MT)
            rsqrt_mean(dve, link, mstat[:, 0, :], D_MODEL, mstat[:, 1, :], mstat[:, 2, :], mstat[:, 3, :])
            for j in range(MT):
                dve.scalar_tensor_tensor(mt[:, j, :], mt[:, j, :], mstat[:, 2, j:j + 1], gm_row[:, :],
                                         ALU.mult, ALU.mult).then_inc(mem_normed, 1)

            def split(n):
                dve.wait_ge(w_hi_ready, n + 1)
                src, hi, lo = w_piece(n)
                dve.tensor_tensor(lo, raw(n), hi.bitcast(F32), ALU.subtract).then_inc(w_split, 1)

            def by_head(ap):
                return ap.rearrange("p (h d) -> p h d", h=H)

            for n in range(NP):
                split(n)
                if n == 1:
                    for j in range(MT):
                        dve.wait_ge(mem_high, j + 1)
                        rows = slice(j * P, (j + 1) * P)
                        dve.tensor_tensor(memt_lo[:, :, rows], th_ps[:, :, :], memt_hi[:, :, rows].bitcast(F32), ALU.subtract
                                          ).then_inc(mem_low, 1)

            def prepare_q_and_k():
                for n in range(NP, 2 * NP):
                    split(n)
                for j in range(MT):
                    dve.wait_ge(k_squared, j + 1)
                    link(dve.tensor_reduce(stat[:, 0, 1:], by_head(sq[:, :]), AX_X, ALU.add))
                    rsqrt_mean(dve, link, stat[:, 0, 1:], XA_HEAD, stat[:, 1, 1:], stat[:, 2, 1:], stat[:, 3, 1:])
                    if j:
                        dve.wait_ge(k_turned, 1)
                    dve.tensor_tensor(by_head(qn[:, :]), by_head(x_ps[:, j * BANK:(j + 1) * BANK]),
                                      stat[:, 2, 1:, None].to_broadcast([P, H, XA_HEAD]), ALU.mult).then_inc(k_normed, 1)
                    dve.wait_ge(k_turned, j + 1)
                    dve.tensor_scalar(kt[:, :, j * P:(j + 1) * P], to_ps[:, :, :], gains[:, 0:1], gains[:, 1:2],
                                      ALU.mult, ALU.mult).then_inc(kt_ready, 1)

            def prepare_v_and_o():
                for n in range(2 * NP, 4 * NP):
                    split(n)

            def norm_x(c, k):
                dve.scalar_tensor_tensor(xt[:, k % TILES, :], xt[:, k % TILES, :], stat[:, 2, 0:1], g_row[:, :],
                                         ALU.mult, ALU.mult).then_inc(x_normed.sem, 1)

            def stage(c, j, edge):
                has_q, has_x = here(c, j, 0, edge), here(c, j, -2, edge)
                if has_x:
                    dve.wait_ge(x_squared.sem, x_squared.at(c, j + 3))
                if has_q:
                    dve.wait_ge(q_squared.sem, q_squared.at(c, j + 1))
                    link(dve.tensor_reduce(stat[:, 0, 1:], by_head(sq[:, :]), AX_X, ALU.add))
                    link(dve.tensor_scalar(stat[:, 1, 0:1], stat[:, 0, 0:1], 1.0 / D_MODEL, EPS, ALU.mult, ALU.add))
                    link(dve.tensor_scalar(stat[:, 1, 1:], stat[:, 0, 1:], 1.0 / XA_HEAD, EPS, ALU.mult, ALU.add))
                    rsqrt(dve, link, stat[:, 1, :], stat[:, 2, :], stat[:, 3, :])
                elif has_x:
                    rsqrt_mean(dve, link, stat[:, 0, 0:1], D_MODEL, stat[:, 1, 0:1], stat[:, 2, 0:1], stat[:, 3, 0:1])
                if here(c, j, 2, edge):
                    k = j - 2
                    dve.wait_ge(o_high.sem, o_high.at(c, k + 1))
                    dve.tensor_tensor(ot_lo[:, :, :], to_ps[:, :, :], ot_hi[:, :, :].bitcast(F32), ALU.subtract
                                      ).then_inc(o_low.sem, 1)
                if has_q:
                    dve.wait_ge(q_turned.sem, q_turned.at(c, j))
                    if edge is True and j == 0:
                        dve.wait_ge(k_turned, MT)
                    dve.tensor_tensor(by_head(qn[:, :]), by_head(q_ps[:, :]),
                                      stat[:, 2, 1:, None].to_broadcast([P, H, XA_HEAD]), ALU.mult).then_inc(q_normed.sem, 1)
                if here(c, j, 1, edge):
                    k = j - 1
                    dve.wait_ge(scored.sem, scored.at(c, k + 1))
                    dve.wait_ge(exped.sem, exped.at(c, k))
                    link(dve.tensor_reduce(soft[:, 0, :], s_ps[:, :, :], AX_X, ALU.max))
                    dve.tensor_scalar(soft[:, 1, :], soft[:, 0, :], -SCALE, None, ALU.mult).then_inc(maxed.sem, 1)
                if has_x:
                    norm_x(c, j + 2)
                if here(c, j, 1, edge):
                    k = j - 1
                    dve.wait_ge(exped.sem, exped.at(c, k + 1))
                    link(dve.reciprocal(soft[:, 3, :], soft[:, 2, :]))
                    dve.tensor_tensor(p[:, :, :], p[:, :, :], soft[:, 3, :, None].to_broadcast([P, H, MEM]), ALU.mult
                                      ).then_inc(p_scaled.sem, 1)
                if here(c, j, -1, edge):
                    k = j + 1
                    dve.wait_ge(h_high.sem, h_high.at(c, k + 1))
                    dve.tensor_tensor(ht_lo[:, :, :], th_ps[:, :, :], ht_hi[:, :, :].bitcast(F32), ALU.subtract
                                      ).then_inc(h_low.sem, 1)
                if has_q:
                    dve.wait_ge(q_turned.sem, q_turned.at(c, j + 1))
                    dve.wait_ge(scored.sem, scored.at(c, j))
                    dve.tensor_copy(qt[:, :, :], to_ps[:, :, :]).then_inc(qt_ready.sem, 1)
                if here(c, j, 2, edge):
                    k = j - 2
                    dve.wait_ge(x_made.sem, x_made.at(c, k + 1))
                    dve.wait_ge(xr_loaded[k % 2], c * (2 * DMA) + (k // 2 + 1) * DMA)
                    dve.tensor_tensor(xr[:, k % 2, :], x_ps[:, :], xr[:, k % 2, :], ALU.add).then_inc(added.sem, 1)

            pipeline(dve, stage, (2, 2), {-1: prepare_q_and_k, 1: prepare_v_and_o}, link)

        @block.tensor
        def _(pe):
            for t in (h_turned, q_made, q_turned, scored, p_turned, o_made, x_made):
                t.start(pe)

            def three_passes(out, hi_a, lo_a, hi_b, lo_b, start, stop):
                pe.matmul(out, hi_a, hi_b, start=start, stop=False)
                pe.matmul(out, hi_a, lo_b, start=False, stop=False)
                return pe.matmul(out, lo_a, hi_b, start=False, stop=stop)

            pe.wait_ge(consts, 2)
            for j in range(MT):
                pe.wait_ge(mem_normed, j + 1)
                if j:
                    pe.wait_ge(mem_low, j)
                for k in range(KC):
                    mm = pe.transpose(th_ps[:, k, :], mt[:, j, k * P:(k + 1) * P], ident[:, :])
                mm.then_inc(mem_turned, 1)
            pe.wait_ge(mem_low, MT)

            def memory_products(half):
                for j in range(MT):
                    rows = slice(j * P, (j + 1) * P)
                    for k in range(KC):
                        mm = three_passes(x_ps[:, j * BANK:(j + 1) * BANK], memt_hi[:, k, rows], memt_lo[:, k, rows],
                                          kv_hi[:, k, :], kv_lo[:, k, :], k == 0, k == KC - 1)
                    mm.then_inc(kv_made, 1)

            pe.wait_ge(w_split, NP)
            memory_products(0)

            def turn_keys():
                for j in range(MT):
                    pe.wait_ge(k_normed, j + 1)
                    if j:
                        pe.wait_ge(kt_ready, j)
                    for h in range(H):
                        mm = pe.transpose(to_ps[:, h, :], qn[:, h * P:(h + 1) * P], ident[:, :])
                    mm.then_inc(k_turned, 1)
                pe.wait_ge(w_split, 2 * NP)
                pe.wait_ge(kt_ready, MT)

            def make_values():
                pe.wait_ge(k_normed, MT)
                pe.wait_ge(w_split, 3 * NP)
                memory_products(1)

            def await_values_and_w_o():
                pe.wait_ge(kv_read, MT)
                pe.wait_ge(w_split, 4 * NP)

            def stage(c, j, edge):
                if here(c, j, 0, edge):
                    pe.wait_ge(h_low.sem, h_low.at(c, j + 1))
                    pe.wait_ge(q_normed.sem, q_normed.at(c, j))
                    for k in range(KC):
                        mm = three_passes(q_ps[:, :], ht_hi[:, k, :], ht_lo[:, k, :], wq_hi[:, k, :], wq_lo[:, k, :],
                                          k == 0, k == KC - 1)
                    mm.then_inc(q_made.sem, 1)
                if here(c, j, 2, edge):
                    k = j - 2
                    pe.wait_ge(pt_ready.sem, pt_ready.at(c, k + 1))
                    pe.wait_ge(qt_ready.sem, qt_ready.at(c, k + 2 if here(c, j, 1, edge) else k + 1))
                    for h in range(H):
                        for m in range(MT):
                            mm = pe.matmul(to_ps[:, h, :], v[:, m, h * P:(h + 1) * P], pt[:, h * MT + m, :],
                                           start=(m == 0), stop=(m == MT - 1))
                    mm.then_inc(o_made.sem, 1)
                if here(c, j, 1, edge):
                    k = j - 1
                    pe.wait_ge(qt_ready.sem, qt_ready.at(c, k + 1))
                    pe.wait_ge(pt_ready.sem, pt_ready.at(c, k))
                    for h in range(H):
                        mm = pe.matmul(s_ps[:, h, :], qt[:, h, :], kt[:, h, :], start=True, stop=True)
                    mm.then_inc(scored.sem, 1)
                if here(c, j, -1, edge):
                    k = j + 1
                    pe.wait_ge(x_normed.sem, x_normed.at(c, k + 1))
                    pe.wait_ge(h_low.sem, h_low.at(c, k))
                    for i in range(KC):
                        mm = pe.transpose(th_ps[:, i, :], xt[:, k % TILES, i * P:(i + 1) * P], ident[:, :])
                    mm.then_inc(h_turned.sem, 1)
                if here(c, j, 2, edge):
                    k = j - 2
                    pe.wait_ge(o_low.sem, o_low.at(c, k + 1))
                    pe.wait_ge(added.sem, added.at(c, k))
                    for o in range(2):
                        cols = slice(o * BANK, (o + 1) * BANK)
                        for h in range(H):
                            mm = three_passes(x_ps[:, cols], ot_hi[:, h, :], ot_lo[:, h, :], wo_hi[:, h, cols], wo_lo[:, h, cols],
                                              h == 0, h == H - 1)
                    mm.then_inc(x_made.sem, 1)
                if here(c, j, 0, edge):
                    pe.wait_ge(q_normed.sem, q_normed.at(c, j + 1))
                    pe.wait_ge(o_low.sem, o_low.at(c, j - 1))
                    for h in range(H):
                        mm = pe.transpose(to_ps[:, h, :], qn[:, h * P:(h + 1) * P], ident[:, :])
                    mm.then_inc(q_turned.sem, 1)
                if here(c, j, 1, edge):
                    k = j - 1
                    pe.wait_ge(p_scaled.sem, p_scaled.at(c, k + 1))
                    for i in range(H * MT):
                        mm = pe.transpose(s_ps[:, i // MT, (i % MT) * P:(i % MT + 1) * P], p[:, i // MT, (i % MT) * P:(i % MT + 1) * P],
                                          ident[:, :])
                    mm.then_inc(p_turned.sem, 1)

            pipeline(pe, stage, (1, 2), {0: turn_keys, 1: make_values, 2: await_values_and_w_o})


def mlp(nc, x2_dram, x2_sums, g_mlp, w_up, w_down, out):
    ROWS = 1024
    CHUNKS2 = SEQ // ROWS
    TILES = ROWS // P
    FB = 256
    S = FB // P
    BLOCKS = D_FF // FB
    HALVES = ROWS // BANK
    U = HALVES * S
    XT = 4
    LAST = CHUNKS2 * BLOCKS - 1
    with ExitStack() as ctx:
        def sb(name, shape, dt=F32):
            return ctx.enter_context(nc.sbuf_tensor("f_" + name, shape, dt))

        def ps(name, shape):
            return ctx.enter_context(nc.psum_tensor("f_ps_" + name, shape, F32))

        sem = ctx.enter_context(semaphores(nc, "f_"))

        ht_hi = sb("ht_hi", [P, KC, ROWS], F32R)
        ht_lo = sb("ht_lo", [P, KC, ROWS], F32R)
        y = sb("y", [P, TILES, D_MODEL])
        up_raw = sb("up_raw", [P, KC, FB])
        down_raw = sb("down_raw", [P, S, D_MODEL])
        up_hi = sb("up_hi", [P, KC, FB], F32R)
        up_lo = sb("up_lo", [P, KC, FB], F32R)
        down_hi = sb("down_hi", [P, S, D_MODEL], F32R)
        down_lo = sb("down_lo", [P, S, D_MODEL], F32R)
        a_hi = [sb(f"a_hi{b}", [P, S, ROWS], F32R) for b in range(2)]
        a_lo = [sb(f"a_lo{b}", [P, S, ROWS], F32R) for b in range(2)]
        act_f = sb("act_f", [P, 2, BANK])
        xt = sb("xt", [P, XT, D_MODEL])
        g_row = sb("g_row", [P, D_MODEL])
        ident = sb("ident", [P, P])
        stat = sb("stat", [P, 4, SEQ // P])

        up_ps = [ps(f"up{i}", [P, BANK]) for i in range(2)]
        down_ps = [ps(f"down{i}", [P, D_MODEL]) for i in range(2)]
        th_ps = ps("th", [P, KC, P])

        consts = sem("consts")
        g_in = sem("g_in")
        dve_link = sem("dve_link")
        x_loaded = [sem(f"x_loaded{i}") for i in range(XT)]
        x_normed = sem("x_normed")
        h_turned = sem("h_turned")
        h_high = sem("h_high")
        h_low = sem("h_low")
        y_loaded = [sem(f"y_loaded{t}") for t in range(TILES)]
        stored = [sem(f"stored{t}") for t in range(TILES)]
        up_loaded = sem("up_loaded")
        down_loaded = sem("down_loaded")
        up_high = Tally(sem("up_high"), S)
        down_high = Tally(sem("down_high"), S)
        up_split = Tally(sem("up_split"), S)
        down_split = Tally(sem("down_split"), S)
        up_made = Tally(sem("up_made"), U)
        relued = Tally(sem("relued"), U)
        a_squared = Tally(sem("a_squared"), U)
        a_high = Tally(sem("a_high"), U)
        a_low = Tally(sem("a_low"), U)
        down_made = Tally(sem("down_made"), TILES)
        added = Tally(sem("added"), TILES)

        def turned_into(n):
            return down_ps[0][:, :].rearrange("p (k q) -> p k q", q=P) if n < TILES and n % 2 else th_ps[:, :, :]

        block = ctx.enter_context(nc.Block())

        def program(eng, prologue, up, down, boundary):
            prologue()
            for chunk in range(CHUNKS2):
                b0 = chunk * BLOCKS
                up(b0, 0, True)
                with eng.Fori(b0, b0 + BLOCKS - 2, 2) as b:
                    for par in range(2):
                        up(b + (par + 1), 1 - par, False)
                        down(b + par, par, False)
                for par in range(BLOCKS - 2, BLOCKS - 1):
                    up(b0 + par + 1, (par + 1) % 2, False)
                    down(b0 + par, par % 2, False)
                boundary(chunk)

        @block.sync
        def _(sp):
            def load_x(n):
                if n >= XT:
                    sp.wait_ge(h_turned, n - XT + 1)
                sp.dma_start(xt[:, n % XT, :], x2_dram[n * P:(n + 1) * P, :]).then_inc(x_loaded[n % XT], DMA)

            def load_up(b):
                if b:
                    sp.wait_ge(up_split.sem, up_split.at(b - 1, S))
                sp.dma_start(up_raw[:, :, :], w_up[:, b % BLOCKS * FB:(b % BLOCKS + 1) * FB].rearrange("(k p) f -> p k f", p=P)
                             ).then_inc(up_loaded, DMA)

            def load_down(b):
                if b:
                    sp.wait_ge(down_split.sem, down_split.at(b - 1, S))
                sp.dma_start(down_raw[:, :, :], w_down[b % BLOCKS * FB:(b % BLOCKS + 1) * FB, :].rearrange("(s p) f -> p s f", p=P)
                             ).then_inc(down_loaded, DMA)

            def load_y(chunk, t):
                row = chunk * ROWS + t * P
                sp.dma_start(y[:, t, :], x2_dram[row:row + P, :]).then_inc(y_loaded[t], DMA)

            def store_y(chunk, t):
                row = chunk * ROWS + t * P
                sp.wait_ge(added.sem, added.at((chunk + 1) * BLOCKS - 1, t + 1))
                sp.dma_start(out[row:row + P, :], y[:, t, :]).then_inc(stored[t], DMA)

            sp.dma_start(stat[:, 0, :], x2_sums[:, :]).then_inc(g_in, DMA)
            load_x(0)
            sp.dma_start(g_row[:, :], g_mlp.partition_broadcast(P)).then_inc(g_in, DMA)
            for n in range(1, XT):
                load_x(n)
            load_up(0)
            for n in range(XT, TILES):
                load_x(n)
            load_down(0)
            load_up(1)
            for n in range(TILES, TILES + XT):
                load_x(n)
            for t in range(TILES):
                load_y(0, t)
            for b in range(2, LAST + 1):
                load_up(b)
                load_down(b - 1)
                if b == BLOCKS + 1:
                    for n in range(TILES + XT, 2 * TILES):
                        load_x(n)
                    for t in range(TILES):
                        store_y(0, t)
                    for t in range(TILES):
                        sp.wait_ge(stored[t], DMA)
                        load_y(1, t)
            load_down(LAST)
            for t in range(TILES):
                store_y(1, t)
            for t in range(TILES):
                sp.wait_ge(stored[t], 2 * DMA)

        @block.gpsimd
        def _(pool):
            fill_identity(pool, ident[:, :], consts)

        def up_slice(buf, s):
            return buf[:, :, s * P:(s + 1) * P]

        @block.scalar
        def _(act):
            for t in (up_high, down_high, relued, a_high):
                t.start(act)

            def high_h(n):
                act.wait_ge(h_turned, n + 1)
                if n >= TILES:
                    act.wait_ge(up_made.sem, up_made.at(BLOCKS - 1, ((n - TILES) * P // BANK + 1) * S))
                t = n % TILES
                act.activation(ht_hi[:, :, t * P:(t + 1) * P], turned_into(n), ACT.Copy).then_inc(h_high, 1)

            def split_up(b, s, old):
                act.wait_ge(up_loaded, b * DMA + DMA)
                if old:
                    act.wait_ge(up_made.sem, up_made.at(b - 1, U - S + s + 1))
                act.activation(up_slice(up_hi, s), up_slice(up_raw, s), ACT.Copy).then_inc(up_high.sem, 1)

            def split_down(b, s):
                act.wait_ge(down_loaded, b * DMA + DMA)
                act.wait_ge(down_made.sem, down_made.at(b - 1, TILES))
                act.activation(down_hi[:, s, :], down_raw[:, s, :], ACT.Copy).then_inc(down_high.sem, 1)

            def prologue():
                for n in range(TILES):
                    high_h(n)
                    if n < S:
                        split_up(0, n, False)

            def up(b, par, first):
                for u in range(U):
                    act.wait_ge(up_made.sem, up_made.at(b, u + 1))
                    act.wait_ge(a_low.sem, a_low.at(b - 1, u + U - 1) if u < 2 else a_low.at(b, u - 1))
                    act.activation(act_f[:, u % 2, :], up_ps[u % 2][:, :], ACT.Relu).then_inc(relued.sem, 1)
                    if u < S and not first:
                        split_down(b - 1, u)
                    if u >= U - S and b is not LAST:
                        split_up(b + 1, u - (U - S), True)
                    act.wait_ge(a_squared.sem, a_squared.at(b, u + 1))
                    act.wait_ge(down_made.sem, down_made.at(b - 2, TILES))
                    cols = slice(u // S * BANK, (u // S + 1) * BANK)
                    act.activation(a_hi[par][:, u % S, cols], act_f[:, u % 2, :], ACT.Copy).then_inc(a_high.sem, 1)

            def down(b, par, last):
                pass

            def boundary(chunk):
                b = (chunk + 1) * BLOCKS - 1
                for s in range(S):
                    split_down(b, s)
                if chunk == 0:
                    for n in range(TILES, 2 * TILES):
                        high_h(n)

            program(act, prologue, up, down, boundary)

        @block.vector
        def _(dve):
            for t in (up_split, down_split, a_squared, a_low, added):
                t.start(dve)
            link = Chain(dve, dve_link)
            dve.wait_ge(g_in, 2 * DMA)
            rsqrt_mean(dve, link, stat[:, 0, :], D_MODEL, stat[:, 1, :], stat[:, 2, :], stat[:, 3, :])

            def norm_x(n):
                dve.wait_ge(x_loaded[n % XT], (n // XT + 1) * DMA)
                dve.scalar_tensor_tensor(xt[:, n % XT, :], xt[:, n % XT, :], stat[:, 2, n:n + 1], g_row[:, :],
                                         ALU.mult, ALU.mult).then_inc(x_normed, 1)

            def low_h(n):
                dve.wait_ge(h_high, n + 1)
                t = n % TILES
                cols = slice(t * P, (t + 1) * P)
                dve.tensor_tensor(ht_lo[:, :, cols], turned_into(n), ht_hi[:, :, cols].bitcast(F32), ALU.subtract
                                  ).then_inc(h_low, 1)

            def split_up(b, s):
                dve.wait_ge(up_high.sem, up_high.at(b, s + 1))
                dve.tensor_tensor(up_slice(up_lo, s), up_slice(up_raw, s), up_slice(up_hi, s).bitcast(F32), ALU.subtract
                                  ).then_inc(up_split.sem, 1)

            def split_down(b, s):
                dve.wait_ge(down_high.sem, down_high.at(b, s + 1))
                dve.tensor_tensor(down_lo[:, s, :], down_raw[:, s, :], down_hi[:, s, :].bitcast(F32), ALU.subtract
                                  ).then_inc(down_split.sem, 1)

            def add(b, t, first, chunk):
                dve.wait_ge(down_made.sem, down_made.at(b, t + 1))
                dve.wait_ge(added.sem, added.at(b - 1, t + 1))
                dve.wait_ge(y_loaded[t], (chunk + 1) * DMA)
                dve.tensor_tensor(y[:, t, :], down_ps[t % 2][:, :], y[:, t, :], ALU.add).then_inc(added.sem, 1)

            def prologue():
                norm_x(0)
                norm_x(1)
                for n in range(TILES):
                    low_h(n)
                    if n + 2 < TILES:
                        norm_x(n + 2)
                    if n < S:
                        split_up(0, n)

            chunk_now = 0

            def up(b, par, first):
                for u in range(U):
                    dve.wait_ge(relued.sem, relued.at(b, u + 1))
                    dve.scalar_tensor_tensor(act_f[:, u % 2, :], up_ps[u % 2][:, :], 0.0, act_f[:, u % 2, :],
                                             ALU.max, ALU.mult).then_inc(a_squared.sem, 1)
                    if u < S and not first:
                        split_down(b - 1, u)
                    if u >= U - S and b is not LAST:
                        split_up(b + 1, u - (U - S))
                    dve.wait_ge(a_high.sem, a_high.at(b, u + 1))
                    cols = slice(u // S * BANK, (u // S + 1) * BANK)
                    dve.tensor_tensor(a_lo[par][:, u % S, cols], act_f[:, u % 2, :], a_hi[par][:, u % S, cols].bitcast(F32),
                                      ALU.subtract).then_inc(a_low.sem, 1)

            def down(b, par, last):
                for t in range(TILES):
                    add(b, t, False, chunk_now)

            def boundary(chunk):
                nonlocal chunk_now
                b = (chunk + 1) * BLOCKS - 1
                if chunk == 0:
                    norm_x(TILES)
                    norm_x(TILES + 1)
                for s in range(S):
                    split_down(b, s)
                for i in range(TILES):
                    if chunk == 0:
                        if i % 2 == 1:
                            n = TILES + i // 2
                            low_h(n)
                            norm_x(n + 2)
                    add(b, i, False, chunk)
                if chunk == 0:
                    for n in range(TILES + TILES // 2, 2 * TILES):
                        low_h(n)
                        if n + 2 < 2 * TILES:
                            norm_x(n + 2)
                    chunk_now = 1

            program(dve, prologue, up, down, boundary)

        @block.tensor
        def _(pe):
            for t in (up_made, down_made):
                t.start(pe)
            pe.wait_ge(consts, 2)

            def turn_h(n):
                pe.wait_ge(x_normed, n + 1)
                read = n - 1 if n < TILES else n
                if read > 0:
                    pe.wait_ge(h_low, read)
                for k in range(KC):
                    mm = pe.transpose(turned_into(n)[:, k, :], xt[:, n % XT, k * P:(k + 1) * P], ident[:, :])
                mm.then_inc(h_turned, 1)

            def prologue():
                for n in range(TILES // 2):
                    turn_h(n)

            def up(b, par, first):
                for u in range(U):
                    half, s = u // S, u % S
                    if first:
                        base = b // BLOCKS * TILES
                        if s == 0:
                            pe.wait_ge(h_low, base + (half + 1) * TILES // 2)
                        if half == 0:
                            turn_h(base + TILES // 2 + s)
                    if half == 0:
                        pe.wait_ge(up_split.sem, up_split.at(b, s + 1))
                    pe.wait_ge(a_squared.sem, a_squared.at(b - 1, U + u - 1) if u < 2 else a_squared.at(b, u - 1))
                    rows, cols = slice(half * BANK, (half + 1) * BANK), slice(s * P, (s + 1) * P)
                    o = up_ps[u % 2][:, :]
                    for k in range(KC):
                        pe.matmul(o, up_hi[:, k, cols], ht_hi[:, k, rows], start=(k == 0), stop=False)
                        pe.matmul(o, up_hi[:, k, cols], ht_lo[:, k, rows], start=False, stop=False)
                        mm = pe.matmul(o, up_lo[:, k, cols], ht_hi[:, k, rows], start=False, stop=(k == KC - 1))
                    mm.then_inc(up_made.sem, 1)
                    if first and u == S - 1:
                        for n in range(TILES // 2 + S, TILES):
                            turn_h(base + n)

            def down_tile(b, par, t):
                pe.wait_ge(added.sem, added.at(b - 1, TILES + t - 1) if t < 2 else added.at(b, t - 1))
                rows = slice(t * P, (t + 1) * P)
                for half in range(2):
                    cols = slice(half * BANK, (half + 1) * BANK)
                    o = down_ps[t % 2][:, cols]
                    for s in range(S):
                        pe.matmul(o, a_hi[par][:, s, rows], down_hi[:, s, cols], start=(s == 0), stop=False)
                        pe.matmul(o, a_hi[par][:, s, rows], down_lo[:, s, cols], start=False, stop=False)
                        mm = pe.matmul(o, a_lo[par][:, s, rows], down_hi[:, s, cols], start=False, stop=(s == S - 1))
                mm.then_inc(down_made.sem, 1)

            def down(b, par, last):
                pe.wait_ge(a_low.sem, a_low.at(b, U))
                pe.wait_ge(down_split.sem, down_split.at(b, S))
                for t in range(TILES):
                    down_tile(b, par, t)

            def boundary(chunk):
                b = (chunk + 1) * BLOCKS - 1
                if chunk == 0:
                    turn_h(TILES)
                pe.wait_ge(a_low.sem, a_low.at(b, U))
                pe.wait_ge(down_split.sem, down_split.at(b, S))
                for t in range(TILES):
                    down_tile(b, 1, t)
                    if chunk == 0 and t % 2 == 1 and t // 2 + 1 < TILES // 2:
                        turn_h(TILES + t // 2 + 1)

            program(pe, prologue, up, down, boundary)


def decoder_block(nc, t, out):
    def scratch(name, *shape):
        return nc.dram_tensor(name, shape, F32).ap()

    u = scratch("u", SSM_WIDTH, SUB, CHUNKS)
    q = scratch("q", HEADS, P, SEQ)
    k = scratch("k", HEADS, P, SEQ)
    v = scratch("v", SEQ, SB_WIDTH)
    y_ssm = scratch("y_ssm", SSM_WIDTH, SUB, CHUNKS)
    y_sb = scratch("y_sb", SEQ, SB_WIDTH)
    x1 = scratch("x1", SEQ, D_MODEL)
    x2 = scratch("x2", SEQ, D_MODEL)
    x2_sums = scratch("x2_sums", P, SEQ // P)
    input_projection(nc, t["x"], t["g_mix"], t["w_in"], t["sb_g_q"], t["sb_g_k"], u, q, k, v)
    ssm_scan(nc, t["ssm_a_re"], t["ssm_a_im"], t["ssm_log_dt"], t["ssm_b_re"], t["ssm_b_im"],
             t["ssm_c_re"], t["ssm_c_im"], u, y_ssm)
    stick_breaking(nc, q, k, v, y_sb)
    mix_heads(nc, t["x"], u, y_ssm, y_sb, t["ssm_d"], t["ssm_w_glu"], t["g_out_ssm"], t["g_out_sb"], t["w_out"], x1)
    cross_attention(nc, x1, t["mem"], t["g_xa"], t["g_mem"], t["xa_w_q"], t["xa_w_kv"], t["xa_g_q"], t["xa_g_k"],
                    t["xa_w_o"], x2, x2_sums)
    mlp(nc, x2, x2_sums, t["g_mlp"], t["w_up"], t["w_down"], out)


INPUTS = ("x", "mem", "g_mix", "w_in", "ssm_a_re", "ssm_a_im", "ssm_log_dt", "ssm_b_re", "ssm_b_im", "ssm_c_re",
          "ssm_c_im", "ssm_d", "ssm_w_glu", "sb_g_q", "sb_g_k", "g_out_ssm", "g_out_sb", "w_out", "g_xa", "g_mem",
          "xa_w_q", "xa_w_kv", "xa_g_q", "xa_g_k", "xa_w_o", "g_mlp", "w_up", "w_down")


def kernel(**inputs):
    import numpy as np
    import concourse.bacc as bacc
    from concourse.bass_utils import run_bass_kernel_spmd

    nc = bacc.Bacc("TRN2", target_bir_lowering=False, num_devices=1)
    arrays, tensors = {}, {}
    for name in INPUTS:
        a = np.ascontiguousarray(inputs[name])
        arrays[f"in_{name}"] = a
        tensors[name] = nc.dram_tensor(f"in_{name}", a.shape, mybir.dt.from_np(a.dtype), kind="ExternalInput").ap()[0]
    out = nc.dram_tensor("out", (1, SEQ, D_MODEL), F32, kind="ExternalOutput").ap()
    decoder_block(nc, tensors, out[0])
    result = run_bass_kernel_spmd(nc, [arrays], core_ids=[0])
    return result.results[0]["out"]
```
